# Optimizing a Trainium2 kernel written in Bass

```python
import jax, jax.numpy as jnp
from jax import lax
import numpy as np

D_MODEL = 1024
BATCH = 1
SEQ = 2048
DEPTH = 1

MIX_WIDTH = D_MODEL
RET_WIDTH = MIX_WIDTH // 2
CONV_WIDTH = MIX_WIDTH - RET_WIDTH
RET_HEADS = 4
RET_HEAD_DIM = RET_WIDTH // RET_HEADS
CHUNK = 128
CONV_KERNEL = 31
MEM_LEN = 256
XATTN_HEADS = 4
XATTN_HEAD_DIM = D_MODEL // XATTN_HEADS
D_FF = 4 * D_MODEL
ROPE_THETA = 10000.0
EPS = 1e-6
IN_COLS = 4 * RET_WIDTH + 2 * CONV_WIDTH

kernel_name = "hybrid_retention_conformer_xattn_block"

def rmsnorm(x, w):
    xf = x.astype(jnp.float32)
    y = xf * lax.rsqrt(jnp.mean(xf * xf, axis=-1, keepdims=True) + EPS)
    return (y * w.astype(jnp.float32)).astype(x.dtype)

def layernorm(x, w, b):
    xf = x.astype(jnp.float32)
    mu = jnp.mean(xf, axis=-1, keepdims=True)
    var = jnp.mean(jnp.square(xf - mu), axis=-1, keepdims=True)
    y = (xf - mu) * lax.rsqrt(var + EPS)
    return y * w.astype(jnp.float32) + b.astype(jnp.float32)

def rotary(x, positions):
    dh = x.shape[-1]
    half = dh // 2
    inv_freq = ROPE_THETA ** (-jnp.arange(half, dtype=jnp.float32) / half)
    ang = positions.astype(jnp.float32)[..., None] * inv_freq
    cos = jnp.cos(ang)[:, :, None, :]
    sin = jnp.sin(ang)[:, :, None, :]
    xf = x.astype(jnp.float32)
    x1, x2 = xf[..., :half], xf[..., half:]
    return jnp.concatenate([x1 * cos - x2 * sin, x2 * cos + x1 * sin], axis=-1)

def to_chunks(t):
    b, s, h, d = t.shape
    return t.reshape(b, s // CHUNK, CHUNK, h, d).transpose(0, 3, 1, 2, 4)

def from_chunks(t):
    b, h, nc, c, d = t.shape
    return t.transpose(0, 2, 3, 1, 4).reshape(b, nc * c, h, d)

def retention_chunkwise(q, k, v, log_gamma, include_diag):
    c = q.shape[3]
    idx = jnp.arange(c, dtype=jnp.float32)
    diff = idx[:, None] - idx[None, :]
    mask = (diff >= 0) if include_diag else (diff > 0)
    decay_in = jnp.where(mask[None], jnp.exp(log_gamma[:, None, None] * jnp.maximum(diff, 0.0)[None]), 0.0)
    scores = jnp.einsum('bhnqd,bhnkd->bhnqk', q, k) * decay_in[None, :, None]
    inner = jnp.einsum('bhnqk,bhnkd->bhnqd', scores, v)
    zeta = jnp.exp(log_gamma[:, None] * (c - 1 - idx)[None])
    chunk_kv = jnp.einsum('bhnkd,bhnke->bhnde', k * zeta[None, :, None, :, None], v)
    chunk_decay = jnp.exp(log_gamma * c)[None, :, None, None]

    def step(state, kv_n):
        return chunk_decay * state + kv_n, state

    init = jnp.zeros(chunk_kv.shape[:2] + chunk_kv.shape[3:], jnp.float32)
    _, r_prev = lax.scan(step, init, jnp.moveaxis(chunk_kv, 2, 0))
    r_prev = jnp.moveaxis(r_prev, 0, 2)
    xi = jnp.exp(log_gamma[:, None] * (idx + 1.0)[None])
    cross = jnp.einsum('bhnqd,bhnde->bhnqe', q * xi[None, :, None, :, None], r_prev)
    return inner + cross

def retention_group(proj_q, proj_k, proj_v, proj_g, positions, decay_f, decay_b, gn_w, gn_b):
    b, s, _ = proj_q.shape
    q = rotary(proj_q.reshape(b, s, RET_HEADS, RET_HEAD_DIM), positions)
    k = rotary(proj_k.reshape(b, s, RET_HEADS, RET_HEAD_DIM), positions) * (RET_HEAD_DIM ** -0.5)
    v = proj_v.reshape(b, s, RET_HEADS, RET_HEAD_DIM).astype(jnp.float32)
    lg_f = jax.nn.log_sigmoid(decay_f.astype(jnp.float32))
    lg_b = jax.nn.log_sigmoid(decay_b.astype(jnp.float32))
    y_f = from_chunks(retention_chunkwise(to_chunks(q), to_chunks(k), to_chunks(v), lg_f, True))
    y_b = from_chunks(retention_chunkwise(to_chunks(q[:, ::-1]), to_chunks(k[:, ::-1]),
                                          to_chunks(v[:, ::-1]), lg_b, False))[:, ::-1]
    y = y_f + y_b
    mu = jnp.mean(y, axis=-1, keepdims=True)
    var = jnp.mean(jnp.square(y - mu), axis=-1, keepdims=True)
    y = ((y - mu) * lax.rsqrt(var + EPS)).reshape(b, s, RET_WIDTH)
    y = y * gn_w.astype(jnp.float32) + gn_b.astype(jnp.float32)
    return (jax.nn.silu(proj_g.astype(jnp.float32)) * y).astype(proj_q.dtype)

def conformer_conv_group(proj_a, proj_b, conv_w, conv_b, ln_w, ln_b):
    u = proj_a * jax.nn.sigmoid(proj_b)
    pad = CONV_KERNEL // 2
    y = lax.conv_general_dilated(u, conv_w, window_strides=(1,), padding=((pad, pad),),
                                 dimension_numbers=('NWC', 'WIO', 'NWC'),
                                 feature_group_count=CONV_WIDTH) + conv_b
    y = layernorm(y, ln_w, ln_b)
    return jax.nn.silu(y).astype(proj_a.dtype)

def memory_cross_attention(h, m, w_q, w_kv, w_o):
    b, s, _ = h.shape
    q = (h @ w_q).reshape(b, s, XATTN_HEADS, XATTN_HEAD_DIM)
    kv = m @ w_kv
    k = kv[..., :D_MODEL].reshape(b, m.shape[1], XATTN_HEADS, XATTN_HEAD_DIM)
    v = kv[..., D_MODEL:].reshape(b, m.shape[1], XATTN_HEADS, XATTN_HEAD_DIM)
    scores = jnp.einsum('bshd,bmhd->bhsm', q.astype(jnp.float32), k.astype(jnp.float32)) * (XATTN_HEAD_DIM ** -0.5)
    p = jax.nn.softmax(scores, axis=-1)
    o = jnp.einsum('bhsm,bmhd->bshd', p, v.astype(jnp.float32)).reshape(b, s, D_MODEL)
    return o.astype(h.dtype) @ w_o

def setup_inputs(seed: int = 0) -> dict:
    key = jax.random.key(seed)
    ks = jax.random.split(key, 24)
    f32 = jnp.float32

    def nrm(k, shape, scale):
        return jax.random.normal(k, shape, f32) * scale

    def gain(k, shape):
        return 1.0 + 0.05 * jax.random.normal(k, shape, f32)

    g0 = 1.0 - 2.0 ** (-5.0 - np.arange(RET_HEADS, dtype=np.float32))
    base_logit = jnp.asarray(np.log(g0) - np.log1p(-g0), f32)
    return {
        "x": jax.random.normal(ks[0], (BATCH, SEQ, D_MODEL), f32),
        "mem": jax.random.normal(ks[1], (BATCH, MEM_LEN, D_MODEL), f32),
        "positions": jnp.broadcast_to(jnp.arange(SEQ, dtype=jnp.int32), (BATCH, SEQ)),
        "mix_norm_w": gain(ks[2], (DEPTH, D_MODEL)),
        "w_in": nrm(ks[3], (DEPTH, D_MODEL, IN_COLS), D_MODEL ** -0.5),
        "ret_decay_f": base_logit[None] + 0.1 * jax.random.normal(ks[4], (DEPTH, RET_HEADS), f32),
        "ret_decay_b": base_logit[None] + 0.1 * jax.random.normal(ks[5], (DEPTH, RET_HEADS), f32),
        "ret_gn_w": gain(ks[6], (DEPTH, RET_WIDTH)),
        "ret_gn_b": nrm(ks[7], (DEPTH, RET_WIDTH), 0.02),
        "conv_w": nrm(ks[8], (DEPTH, CONV_KERNEL, 1, CONV_WIDTH), CONV_KERNEL ** -0.5),
        "conv_b": nrm(ks[9], (DEPTH, CONV_WIDTH), 0.02),
        "conv_ln_w": gain(ks[10], (DEPTH, CONV_WIDTH)),
        "conv_ln_b": nrm(ks[11], (DEPTH, CONV_WIDTH), 0.02),
        "w_out": nrm(ks[12], (DEPTH, MIX_WIDTH, D_MODEL), MIX_WIDTH ** -0.5),
        "xattn_norm_w": gain(ks[13], (DEPTH, D_MODEL)),
        "mem_norm_w": gain(ks[14], (DEPTH, D_MODEL)),
        "w_xq": nrm(ks[15], (DEPTH, D_MODEL, D_MODEL), D_MODEL ** -0.5),
        "w_xkv": nrm(ks[16], (DEPTH, D_MODEL, 2 * D_MODEL), D_MODEL ** -0.5),
        "w_xo": nrm(ks[17], (DEPTH, D_MODEL, D_MODEL), D_MODEL ** -0.5),
        "mlp_norm_w": gain(ks[18], (DEPTH, D_MODEL)),
        "w_ff1": nrm(ks[19], (DEPTH, D_MODEL, D_FF), D_MODEL ** -0.5),
        "w_ff2": nrm(ks[20], (DEPTH, D_FF, D_MODEL), D_FF ** -0.5),
        "final_norm_w": gain(ks[21], (D_MODEL,)),
    }

def reference(x, mem, positions, mix_norm_w, w_in, ret_decay_f, ret_decay_b, ret_gn_w, ret_gn_b,
              conv_w, conv_b, conv_ln_w, conv_ln_b, w_out, xattn_norm_w, mem_norm_w,
              w_xq, w_xkv, w_xo, mlp_norm_w, w_ff1, w_ff2, final_norm_w):
    R = RET_WIDTH
    for l in range(DEPTH):
        h = rmsnorm(x, mix_norm_w[l])
        proj = h @ w_in[l]
        p_q, p_k, p_v, p_g = proj[..., :R], proj[..., R:2 * R], proj[..., 2 * R:3 * R], proj[..., 3 * R:4 * R]
        p_a = proj[..., 4 * R:4 * R + CONV_WIDTH]
        p_b = proj[..., 4 * R + CONV_WIDTH:]
        y_ret = retention_group(p_q, p_k, p_v, p_g, positions, ret_decay_f[l], ret_decay_b[l],
                                ret_gn_w[l], ret_gn_b[l])
        y_conv = conformer_conv_group(p_a, p_b, conv_w[l], conv_b[l], conv_ln_w[l], conv_ln_b[l])
        x = x + jnp.concatenate([y_ret, y_conv], axis=-1) @ w_out[l]
        x = x + memory_cross_attention(rmsnorm(x, xattn_norm_w[l]), rmsnorm(mem, mem_norm_w[l]),
                                       w_xq[l], w_xkv[l], w_xo[l])
        hm = rmsnorm(x, mlp_norm_w[l])
        x = x + jnp.square(jax.nn.relu(hm @ w_ff1[l])) @ w_ff2[l]
    return rmsnorm(x, final_norm_w)


_drawn_inputs = setup_inputs


def setup_inputs(seed=0):
    import zlib

    import numpy as np

    out = dict(_drawn_inputs(seed))
    spreads = {}
    factors = {'ret_gn_w': 2.829,
     'ret_gn_b': 7.245,
     'conv_b': 3.812,
     'conv_ln_b': 6.903,
     'xattn_norm_w': 8.0,
     'mem_norm_w': 8.0,
     'mlp_norm_w': 6.601}
    for name, (base, spread) in spreads.items():
        noise = np.random.default_rng([zlib.crc32(name.encode()), seed]).standard_normal(out[name].shape)
        drawn = base * np.exp(spread * noise) if base else spread * noise
        out[name] = __import__('jax').numpy.asarray(drawn.astype(out[name].dtype))
    for name, factor in factors.items():
        out[name] = (out[name] * factor).astype(out[name].dtype)
    return out
```

```python
from contextlib import ExitStack

import numpy as np
import concourse.bass as bass
from concourse import mybir

F32 = mybir.dt.float32
F32R = mybir.dt.float32r
I32 = mybir.dt.int32
ALU = mybir.AluOpType
ACT = mybir.ActivationFunctionType
AX = mybir.AxisListType

P = 128
ROPE_THETA = 10000.0
EPS = 1e-6
MAGIC = 1.5 * 2.0 ** 23
TWO_PI_PARTS = (6.28125, 0.0019340515136718750, 1.2556440196931362e-06)


def build(nc, x, mem, positions, mix_norm_w, w_in, ret_decay_f, ret_decay_b, ret_gn_w, ret_gn_b,
          conv_w, conv_b, conv_ln_w, conv_ln_b, w_out, xattn_norm_w, mem_norm_w,
          w_xq, w_xkv, w_xo, mlp_norm_w, w_ff1, w_ff2, final_norm_w, rope_freq, out):
    S, D = x.shape[1], x.shape[2]
    M = mem.shape[1]
    KT = D // P
    NC = 512
    NS = S // NC
    HALF = S // 2
    NH = HALF // NC
    R = ret_gn_w.shape[1]
    CW = conv_b.shape[1]
    CT = CW // P
    TAPS = conv_w.shape[1]
    PAD = TAPS // 2
    HEADS = ret_decay_f.shape[1]
    HD = R // HEADS
    CH = S // P
    XH = 4
    XHD = D // XH
    FF = w_ff1.shape[2]
    FG = FF // D
    KSCALE = float(HD) ** -0.5
    XSCALE = float(XHD) ** -0.5
    assert HD == P and CT == HEADS == XH == NS == 4 and KT == 8 and NH == 2 and M == 2 * P and TAPS == 31

    G_MEM = NS * KT
    G_PROJ = G_MEM + KT
    PROJ = [("a", 16, 4), ("V", 0, 1), ("b", 20, 4), ("V", 1, 1), ("q", 0, 4), ("K", 0, 1),
            ("k", 4, 4), ("K", 1, 1), ("v", 8, 4), ("g", 12, 4)]
    GP = sum(b[2] for b in PROJ)
    BP = len(PROJ)
    CUM = [sum(b[2] for b in PROJ[:i]) for i in range(BP + 1)]
    G_HALF0 = G_PROJ + HEADS * GP
    G_XQ = NH * KT
    G_XO = G_XQ + XH * 8
    G_FF = G_XO + NH * KT
    G_PER_HALF = G_FF + FG * 2 * NH * KT
    J_HALF0 = HEADS * BP
    J_XQ, J_XO, J_FF = KT, 2 * KT, 3 * KT
    J_PER_HALF = J_FF + FG * 2 * KT
    N_PER_HALF = KT + FG * KT
    H_XQ, H_XO, H_FF = 16, 32, 48
    H_PER_HALF = H_FF + FG * 16
    Q_PER_HALF = 48

    xT_d = nc.dram_tensor("xT_d", [KT, P, NS, NC], F32).ap()
    proj_d = nc.dram_tensor("proj_d", [16, P, S], F32).ap()
    conv_d = nc.dram_tensor("conv_d", [CT, P, S], F32).ap()
    y_d = nc.dram_tensor("y_d", [KT, P, S], F32).ap()
    k_d = nc.dram_tensor("k_d", [KT, P, 2, M], F32).ap()
    v_d = nc.dram_tensor("v_d", [KT, P, 2, M], F32).ap()

    es = ExitStack()
    with es:
        def sem(name):
            return es.enter_context(nc.semaphore(name))

        def alloc(stack, name, shape, dt):
            return stack.enter_context(nc.sbuf_tensor(name, shape, dt))

        wraw = alloc(es, "wraw", [P, 2, KT, P], F32)
        whi = alloc(es, "whi", [P, 2, KT, P], F32R)
        wlo = alloc(es, "wlo", [P, 2, KT, P], F32R)
        ident = alloc(es, "ident", [P, P], F32)
        mean_mat = alloc(es, "mean_mat", [P, P], F32)
        vec = alloc(es, "vec", [P, 60], F32)
        taps = alloc(es, "taps", [P, TAPS * CT], F32)
        eps = alloc(es, "eps", [P, 1], F32)
        half_pi = alloc(es, "half_pi", [P, 1], F32)
        junk = alloc(es, "junk", [P, 8], F32)
        V_MIX, V_MEM, V_XN, V_MLP, V_FIN, V_CB, V_LNW, V_LNB, V_GNW, V_GNB = 0, 8, 16, 24, 32, 40, 44, 48, 52, 56
        ps = es.enter_context(nc.psum_tensor("ps", [P, 8, NC], F32))

        with ExitStack() as s1:
            xhi = alloc(s1, "xhi", [P, KT, NS, NC], F32R)
            xlo = alloc(s1, "xlo", [P, KT, NS, NC], F32R)
            mhi = alloc(s1, "mhi", [P, KT, M], F32R)
            mlo = alloc(s1, "mlo", [P, KT, M], F32R)
            rs = alloc(s1, "rs", [P, NS, NC], F32)
            rsm = alloc(s1, "rsm", [P, M], F32)
            with ExitStack() as s0:
                xt = alloc(s0, "xt", [P, 2, 4, D // 2], F32)
                memt = alloc(s0, "memt", [P, 2, D], F32)
                xf = alloc(s0, "xf", [P, 2, NC], F32)
                sq0 = alloc(s0, "sq0", [P, 2, NC], F32)
                ssq0 = alloc(s0, "ssq0", [P, NS, NC], F32)
                ssqm = alloc(s0, "ssqm", [P, M], F32)
                vrow, trow = xf[:, 0, 0:P], xf[:, 1, 0:P]
            upad = alloc(s1, "upad", [P, S + 2 * PAD], F32)
            acc = alloc(s1, "acc", [P, S], F32)
            st = alloc(s1, "st", [P, NS, NC], F32)
            kz = alloc(s1, "kz", [P, 4, M], F32)
            khl = alloc(s1, "khl", [P, 4, 2, M], F32R)

        with ExitStack() as s2:
            def b2(name, shape=(P, S), dt=F32):
                return alloc(s2, name, list(shape), dt)
            qb_, qsb, kb_, ksb, vb, gb = (b2(n) for n in ("q_in", "q_sw", "k_in", "k_sw", "v_in", "g_in"))
            q_rot_b, k_rot_b, q_f, q_b = (b2(n) for n in ("q_rot", "k_rot", "q_f", "q_b"))
            cos_t, sin_t = b2("cos_t"), b2("sin_t")
            k_tok, v_tok, v_f, v_b = (b2(n, (P, CH, P)) for n in ("k_tok", "v_tok", "v_f", "v_b"))
            st_f, st_b = b2("st_f", (P, CH, P)), b2("st_b", (P, CH, P))
            sT = b2("sT", (P, CH, P))
            y_b, w1, sg = (b2(n, (P, NS, NC)) for n in ("y_b", "w1", "sg"))
            dmask = b2("dmask", (P, HEADS, P))
            xi_f, xi_b = b2("xi_f", (P, HEADS, P)), b2("xi_b", (P, HEADS, P))
            io_t = b2("io_t", (P, 3, P))
            io_s = b2("io_s", (P, 2, P))
            io_c = b2("io_c", (P, 2))
            dec = b2("dec", (P, 2, HEADS))
            lg = b2("lg", (P, 6, 2, HEADS))
            zeta = b2("zeta", (P, 2, HEADS))
            gch = b2("gch", (P, 2, HEADS))
            freq = b2("freq", (P, 1))
            pos_i = b2("pos_i", (P, S), I32)

        with ExitStack() as s3:
            def b3(name, shape, dt=F32):
                return alloc(s3, name, list(shape), dt)
            ahi, alo, bhi, blo = (b3(n, (P, KT, NH, NC), F32R) for n in ("ahi", "alo", "bhi", "blo"))
            res = b3("res", (P, KT, NH, NC))
            kh = b3("kh", (P, 2, 2, M), F32R)
            vh = b3("vh", (P, 2, 2, 2, P), F32R)
            pth, ptl = b3("pth", (P, 2, NC), F32R), b3("ptl", (P, 2, NC), F32R)
            rstd = b3("rstd", (P, NH, NC))
            sq = b3("sq", (P, 2, NC))
            ssq = b3("ssq", (P, NH, NC))
            z = b3("z", (P, 2, NC))
            pr = b3("pr", (P, 2, M))
            mx, nb, sm, ri = (b3(n, (P, 8)) for n in ("mx", "nb", "sm", "ri"))

        phase = sem("phase")
        passed = sem("passed")
        consts = sem("consts")
        vec_in, vec_mm, vec_ok = sem("vec_in"), sem("vec_mm"), sem("vec_ok")
        w_full = [sem("w_full0"), sem("w_full1")]
        w_scaled = sem("w_scaled")
        w_hi = sem("w_hi")
        w_ready = sem("w_ready")
        mm_done = sem("mm_done")
        bank_free = sem("bank_free")
        x_in = [sem("x_in0"), sem("x_in1")]
        mem_in = sem("mem_in")
        hi0, sq0_done, ssq_done = sem("hi0"), sem("sq0_done"), sem("ssq_done")
        xf_done = sem("xf_done")
        xf_st = [sem("xf_st0"), sem("xf_st1")]
        stat_mm, stat_sq, stat_rc = sem("stat_mm"), sem("stat_sq"), sem("stat_rc")
        sig_done, u_done, pad_ok = sem("sig_done"), sem("u_done"), sem("pad_ok")
        conv_step, acc_st = sem("conv_step"), sem("acc_st")
        st_st = [sem(f"st_st{n}") for n in range(NS)]
        kv_hi, kv_lo, vt_mm0 = sem("kv_hi"), sem("kv_lo"), sem("vt_mm0")
        kv_st = [sem(f"kv_st{n}") for n in range(4)]

        G0 = 4

        def released(eng, g):
            eng.wait_ge(bank_free, g + 1 + G0)

        def wait_alone(eng, which, value):
            eng.wait_ge(which, value)
            eng.sem_inc(passed, 1)

        def leave_phase(eng):
            eng.drain().then_inc(phase, 1)

        def end_phase(eng, n):
            leave_phase(eng)
            eng.wait_ge(phase, 5 * n)

        block = es.enter_context(nc.Block())

        l_q, l_qs, l_k, l_ks, l_v, l_g = (sem(n) for n in ("l_q", "l_qs", "l_k", "l_ks", "l_v", "l_g"))
        tab_in, tab, iot = sem("tab_in"), sem("tab"), sem("iot")
        tab_act, tab_ok = sem("tab_act"), sem("tab_ok")
        p_qs, p_ks, p_qf = sem("p_qs"), sem("p_ks"), sem("p_qf")
        r_q, r_k, q_rot, k_rot = sem("r_q"), sem("r_k"), sem("q_rotd"), sem("k_rotd")
        kt_mm, vt_mm, kt_ev, vt_ev = sem("kt_mm"), sem("vt_mm"), sem("kt_ev"), sem("vt_ev")
        v2 = sem("v2")
        kvf_mm, kvb_mm, f_scan, b_scan = sem("kvf_mm"), sem("kvb_mm"), sem("f_scan"), sem("b_scan")
        s_mm, s_ev, y_mm, y_ev = sem("s_mm"), sem("s_ev"), sem("y_mm"), sem("y_ev")
        me_mm, cen, sqd, va_mm, std = sem("me_mm"), sem("cen"), sem("sqd"), sem("va_mm"), sem("std")
        sgd, nrm, y_st = sem("sgd"), sem("nrm"), sem("y_st")
        c_in = [sem("c_in0"), sem("c_in1")]
        c_me, c_cen, c_sq, c_va, c_std, c_nrm, c_sig = (sem(n) for n in ("c_me", "c_cen", "c_sq", "c_va", "c_std", "c_nrm", "c_sig"))
        c_st = [sem("c_st0"), sem("c_st1")]
        y_in = [sem(f"y_in{k}") for k in range(KT)]
        r_in = [sem(f"r_in{k}") for k in range(KT)]
        ysp_hi, ysp_lo = sem("ysp_hi"), sem("ysp_lo")
        hi_done, lo_done, z_up = sem("hi_done"), sem("lo_done"), sem("z_up")
        sq_done, ss_zero, ss_done = sem("sq_done"), sem("ss_zero"), sem("ss_done")
        n_mm, n_sq, n_rc = sem("n_mm"), sem("n_sq"), sem("n_rc")
        kv_in = sem("kv_in")
        sc_mm, mx_done, nb_done, p_exp, ri_done, p_nrm = (sem(n) for n in ("sc_mm", "mx_done", "nb_done", "p_exp", "ri_done", "p_nrm"))
        pt_mm, pt_hi, pt_lo, o_hi = (sem(n) for n in ("pt_mm", "pt_hi", "pt_lo", "o_hi"))
        zf, f_tr, f_cp = sem("zf"), sem("f_tr"), sem("f_cp")
        f_st = [sem("f_st0"), sem("f_st1")]

        def store_conv(sp, n):
            buf = (qb_, kb_)[n % 2]
            sp.wait_ge(c_nrm, 7 * (n + 1))
            sp.dma_start(y_d[HEADS:HEADS + CT, :, n * NC:(n + 1) * NC].rearrange("c p n -> p c n"),
                         buf[:, :].rearrange("p (c n) -> p c n", c=CT)).then_inc(c_st[n % 2], 16)

        @block.sync
        def _(sp):
            def load_weights(j, slot, src):
                sp.wait_ge(w_ready, j + 1)
                sp.dma_start(wraw[:, slot, :, :], src.rearrange("(k p) m -> p k m", p=P)).then_inc(w_full[slot], 16)

            xr = x.rearrange("b (n s p) d -> n p (b s) d", s=4, p=P)
            at = 0
            for v in (mix_norm_w, mem_norm_w, xattn_norm_w, mlp_norm_w, final_norm_w.rearrange("(a n) -> a n", a=1),
                      conv_b, conv_ln_w, conv_ln_b, ret_gn_w, ret_gn_b):
                n = v.shape[1] // P
                sp.dma_start(vrow[at:at + n, :], v.rearrange("a (k p) -> (a k) p", p=P)).then_inc(vec_in, 16)
                at += n
            sp.dma_start(trow[0:TAPS * CT, :], conv_w.rearrange("a t b (c p) -> (a t b c) p", p=P)).then_inc(vec_in, 16)
            for s in range(2):
                sp.dma_start(xt[:, s, :, :], xr[0, :, :, s * (D // 2):(s + 1) * (D // 2)]).then_inc(x_in[s], 16)
            sp.dma_start(memt[:, :, :], mem.rearrange("b (s p) d -> p (b s) d", p=P)).then_inc(mem_in, 16)
            for n in range(NS):
                for k in range(KT):
                    sp.wait_ge(xf_done, KT * n + k + 1)
                    sp.dma_start(xT_d[k, :, n, :], xf[:, k % 2, :]).then_inc(xf_st[k % 2], 16)
                    if k % 4 == 3 and n + 1 < NS:
                        s = k // 4
                        sp.wait_ge(mm_done, KT * n + k + 1)
                        sp.dma_start(xt[:, s, :, :], xr[n + 1, :, :, s * (D // 2):(s + 1) * (D // 2)]).then_inc(x_in[s], 16)
            for s in range(2):
                sp.wait_ge(xf_st[s], 16 * NS * KT // 2)
            leave_phase(sp)
            with sp.Fori(0, HEADS) as c:
                for b, (kind, col, _) in enumerate(PROJ):
                    if kind == "K":
                        src = w_xkv[0, :, bass.ds((2 * c + col) * P, P)]
                    elif kind == "V":
                        src = w_xkv[0, :, bass.ds((KT + 2 * c + col) * P, P)]
                    else:
                        src = w_in[0, :, bass.ds((c + col) * P, P)]
                    load_weights(BP * c + b, b % 2, src)
            end_phase(sp, 2)

            sp.dma_start(pos_i[:, :], positions[0:1, :].to_broadcast([P, S])).then_inc(tab_in, 16)
            sp.dma_start(freq[:, :], rope_freq).then_inc(tab_in, 16)
            sp.dma_start(dec[:, 0, :], ret_decay_f[0:1, :].to_broadcast([P, HEADS])).then_inc(tab_in, 16)
            sp.dma_start(dec[:, 1, :], ret_decay_b[0:1, :].to_broadcast([P, HEADS])).then_inc(tab_in, 16)
            H2 = P // 2

            def load_head(h):
                if h:
                    sp.wait_ge(q_rot, h)
                sp.dma_start(qb_[:, :], proj_d[h]).then_inc(l_q, 16)
                sp.dma_start(qsb[0:H2, :], proj_d[h, H2:P]).then_inc(l_qs, 16)
                sp.dma_start(qsb[H2:P, :], proj_d[h, 0:H2]).then_inc(l_qs, 16)
                if h:
                    sp.wait_ge(k_rot, h)
                sp.dma_start(kb_[:, :], proj_d[4 + h]).then_inc(l_k, 16)
                sp.dma_start(ksb[0:H2, :], proj_d[4 + h, H2:P]).then_inc(l_ks, 16)
                sp.dma_start(ksb[H2:P, :], proj_d[4 + h, 0:H2]).then_inc(l_ks, 16)
                if h:
                    sp.wait_ge(vt_mm, 4 * h)
                sp.dma_start(vb[:, :], proj_d[8 + h]).then_inc(l_v, 16)

            load_head(0)
            sp.dma_start(gb[:, :], proj_d[12]).then_inc(l_g, 16)
            for h in range(HEADS):
                if h + 1 < HEADS:
                    load_head(h + 1)
                sp.wait_ge(nrm, 20 * (h + 1))
                sp.dma_start(y_d[h], y_b[:, :, :].rearrange("p a b -> p (a b)")).then_inc(y_st, 16)
                if h + 1 < HEADS:
                    sp.dma_start(gb[:, :], proj_d[12 + h + 1]).then_inc(l_g, 16)
            for n in range(NS):
                buf = (qb_, kb_)[n % 2]
                if n < 2:
                    sp.wait_ge((q_rot, k_rot)[n], HEADS)
                else:
                    sp.wait_ge(c_st[n % 2], 16)
                sp.dma_start(buf[:, :].rearrange("p (c n) -> p c n", c=CT),
                             conv_d[:, :, n * NC:(n + 1) * NC].rearrange("c p n -> p c n")).then_inc(c_in[n % 2], 16)
                if n >= 1:
                    store_conv(sp, n - 1)
            store_conv(sp, NS - 1)
            for s in range(2):
                sp.wait_ge(c_st[s], 32)
            sp.wait_ge(y_st, 16 * HEADS)
            end_phase(sp, 3)

            with sp.Fori(0, 2) as h:
                J = J_HALF0 + J_PER_HALF * h
                with sp.Fori(0, KT // 2) as i:
                    for s in range(2):
                        load_weights(J + 2 * i + s, s, w_out[0, :, bass.ds((2 * i + s) * P, P)])
                with sp.Fori(0, KT // 2) as i:
                    for s in range(2):
                        load_weights(J + J_XQ + 2 * i + s, s, w_xq[0, :, bass.ds((2 * i + s) * P, P)])
                with sp.Fori(0, KT // 2) as i:
                    for s in range(2):
                        load_weights(J + J_XO + 2 * i + s, s, w_xo[0, :, bass.ds((2 * i + s) * P, P)])
                with sp.Fori(0, FG) as g:
                    with sp.Fori(0, KT // 2) as i:
                        for s in range(2):
                            load_weights(J + J_FF + 16 * g + 2 * i + s, s,
                                         w_ff1[0, :, bass.ds((KT * g + 2 * i + s) * P, P)])
                    with sp.Fori(0, KT // 2) as i:
                        for s in range(2):
                            load_weights(J + J_FF + 16 * g + KT + 2 * i + s, s,
                                         w_ff2[0, bass.ds(g * D, D), bass.ds((2 * i + s) * P, P)])

        @block.gpsimd
        def _(pool):
            pool.memset(ident[:, :], 0.0).then_inc(consts, 1)
            pool.memset(mean_mat[:, :], 1.0 / P).then_inc(consts, 1)
            pool.memset(eps[:, :], EPS).then_inc(consts, 1)
            pool.memset(half_pi[:, :], float(np.pi / 2)).then_inc(consts, 1)
            pool.wait_ge(consts, 4)
            pool.affine_select(out=ident[:, :], in_=ident[:, :], compare_op=ALU.not_equal, fill=1.0,
                               base=0, pattern=[[-1, P]], channel_multiplier=1).then_inc(consts, 1)
            pool.memset(junk[:, 2:3], 0.0).then_inc(w_ready, 2)
            pool.wait_ge(vec_ok, 2)
            with pool.Fori(0, NS) as n:
                for k in range(KT):
                    g = KT * n + k
                    released(pool, g)
                    pool.wait_ge(xf_st[k % 2], 16 * (4 * n + k // 2))
                    pool.tensor_tensor(xf[:, k % 2, :], xhi[:, k, n, :], xlo[:, k, n, :], ALU.add).then_inc(xf_done, 1)

            leave_phase(pool)

            def split_weights(j, full, slot, used, norm=None, count=None):
                pool.wait_ge(w_full[slot], full)
                if norm is not None:
                    pool.tensor_tensor(wraw[:, slot, :, :], wraw[:, slot, :, :],
                                       vec[:, norm:norm + KT].unsqueeze(2).to_broadcast([P, KT, P]),
                                       ALU.mult).then_inc(w_scaled, 1)
                    pool.wait_ge(w_scaled, count + 1)
                wait_alone(pool, mm_done, used)
                pool.tensor_scalar(whi[:, slot, :, :], wraw[:, slot, :, :], 1.0, 0.0, ALU.mult, ALU.add).then_inc(w_hi, 1)
                pool.wait_ge(w_hi, j + 1)
                pool.tensor_tensor(wlo[:, slot, :, :], wraw[:, slot, :, :], whi[:, slot, :, :],
                                   ALU.subtract).then_inc(w_ready, 1)

            with pool.Fori(0, HEADS) as c:
                for b, (kind, _, _) in enumerate(PROJ):
                    used = G_PROJ + GP * c + (CUM[b - 1] if b >= 2 else CUM[BP - 1 + b] - GP)
                    split_weights(BP * c + b, 16 * (5 * c + b // 2) + 16, b % 2, used,
                                  V_MEM if kind in "KV" else V_MIX, BP * c + b)
            end_phase(pool, 2)

            pool.iota(io_t[:, 0, :], pattern=[[1, P]], base=0, channel_multiplier=-1,
                      allow_small_or_imprecise_dtypes=True).then_inc(iot, 1)
            pool.iota(io_s[:, 0, :], pattern=[[1, P]], base=1, channel_multiplier=0,
                      allow_small_or_imprecise_dtypes=True).then_inc(iot, 1)
            pool.iota(io_s[:, 1, :], pattern=[[-1, P]], base=P, channel_multiplier=0,
                      allow_small_or_imprecise_dtypes=True).then_inc(iot, 1)
            pool.iota(io_c[:, 0:1], pattern=[[1, 1]], base=P - 1, channel_multiplier=-1,
                      allow_small_or_imprecise_dtypes=True).then_inc(iot, 1)
            pool.iota(io_c[:, 1:2], pattern=[[1, 1]], base=0, channel_multiplier=1,
                      allow_small_or_imprecise_dtypes=True).then_inc(iot, 1)
            pool.wait_ge(tab_ok, 2)
            with pool.Fori(0, HEADS) as h:
                pool.wait_ge(l_qs, 32 * h + 32)
                pool.tensor_tensor(qsb[:, :], qsb[:, :], sin_t[:, :], ALU.mult).then_inc(p_qs, 1)
                pool.wait_ge(l_ks, 32 * h + 32)
                pool.tensor_tensor(ksb[:, :], ksb[:, :], sin_t[:, :], ALU.mult).then_inc(p_ks, 1)
                pool.wait_ge(q_rot, h + 1)
                pool.wait_ge(y_mm, 4 * h)
                for dst, xi in ((q_f, xi_f), (q_b, xi_b)):
                    pool.tensor_tensor(dst[:, :].rearrange("p (c q) -> p c q", q=P),
                                       q_rot_b[:, :].rearrange("p (c q) -> p c q", q=P),
                                       xi[:, h, :].unsqueeze(1).to_broadcast([P, CH, P]), ALU.mult).then_inc(p_qf, 1)
            end_phase(pool, 3)

            with pool.Fori(0, 2) as h:
                J = J_HALF0 + J_PER_HALF * h
                G = G_HALF0 + G_PER_HALF * h
                N = J_HALF0 + N_PER_HALF * h
                L = 16 * (J_HALF0 // 2) + 16 * (J_PER_HALF // 2) * h + 16
                with pool.Fori(0, KT // 2) as i:
                    for s in range(2):
                        split_weights(J + 2 * i + s, L + 16 * i, s, G + 4 * i + 2 * s - 2)
                for hh in range(XH):
                    for r in range(2):
                        used = G + (2 * (KT - 2 + r) + 2 if hh == 0 else G_XQ + 8 * (hh - 1) + 2 * r + 2)
                        split_weights(J + J_XQ + 2 * hh + r, L + 16 * (4 + hh), r, used, V_XN, N + 2 * hh + r)
                for s in range(2):
                    split_weights(J + J_XO + s, L + 16 * 8, s, G + G_XQ + 24 + 2 * s + 2)
                with pool.Fori(1, KT // 2) as i:
                    for s in range(2):
                        split_weights(J + J_XO + 2 * i + s, L + 16 * 8 + 16 * i, s, G + G_XO + 4 * i + 2 * s - 2)
                with pool.Fori(0, FG) as g:
                    with pool.Fori(0, KT // 2) as i:
                        for s in range(2):
                            split_weights(J + J_FF + 16 * g + 2 * i + s, L + 16 * 12 + 128 * g + 16 * i, s,
                                          G + G_FF + 32 * g + 4 * i + 2 * s - 2, V_MLP, N + KT + KT * g + 2 * i + s)
                    with pool.Fori(0, KT // 2) as i:
                        for s in range(2):
                            split_weights(J + J_FF + 16 * g + KT + 2 * i + s, L + 16 * 12 + 128 * g + 64 + 16 * i, s,
                                          G + G_FF + 32 * g + 16 + 4 * i + 2 * s - 2)

        @block.tensor
        def _(pe):
            def gemm(bank, slot, hi, lo, n, before=None):
                o = ps[:, bank, 0:n]
                for k in range(KT):
                    if before is not None:
                        before(k)
                    nc.tensor.matmul(o, whi[:, slot, k, :], hi(k), start=(k == 0), stop=False)
                    nc.tensor.matmul(o, whi[:, slot, k, :], lo(k), start=False, stop=False)
                    last = nc.tensor.matmul(o, wlo[:, slot, k, :], hi(k), start=False, stop=(k == KT - 1))
                last.then_inc(mm_done, 1)

            def bank_ready(g):
                pe.wait_ge(bank_free, g + 1)

            pe.wait_ge(consts, 5)
            pe.wait_ge(vec_in, 16 * 11)
            pe.transpose(ps[:, 4, 0:60], vrow[0:60, :], ident[0:60, 0:60]).then_inc(vec_mm, 1)
            pe.transpose(ps[:, 5, 0:TAPS * CT], trow[0:TAPS * CT, :],
                         ident[0:TAPS * CT, 0:TAPS * CT]).then_inc(vec_mm, 1)
            with pe.Fori(0, NS) as n:
                for k in range(KT):
                    if k % 4 == 0:
                        pe.wait_ge(x_in[k // 4], 16 * n + 16)
                    bank_ready(KT * n + k)
                    for t in range(4):
                        last = pe.transpose(ps[:, k % 4, t * P:(t + 1) * P],
                                            xt[:, k // 4, t, (k % 4) * P:(k % 4 + 1) * P], ident[:, :])
                    last.then_inc(mm_done, 1)
            pe.wait_ge(mem_in, 16)
            for k in range(KT):
                bank_ready(G_MEM + k)
                for t in range(2):
                    last = pe.transpose(ps[:, k % 4, t * P:(t + 1) * P], memt[:, t, k * P:(k + 1) * P], ident[:, :])
                last.then_inc(mm_done, 1)
            pe.wait_ge(vec_ok, 2)
            for n in range(NS):
                pe.wait_ge(ssq_done, 2 + KT * (n + 1))
                pe.matmul(ps[:, 4 + n, :], mean_mat[:, :], ssq0[:, n, :], start=True, stop=True).then_inc(stat_mm, 1)
            pe.wait_ge(ssq_done, 2 + KT * (NS + 1))
            pe.wait_ge(stat_sq, 1)
            pe.matmul(ps[:, 4, 0:M], mean_mat[:, :], ssqm[:, :], start=True, stop=True).then_inc(stat_mm, 1)
            released(pe, G_PROJ - 1)
            end_phase(pe, 1)
            with pe.Fori(0, HEADS) as c:
                for b, (kind, col, groups) in enumerate(PROJ):
                    pe.wait_ge(w_ready, BP * c + b + 3)
                    for n in range(groups):
                        g = CUM[b] + n
                        bank_ready(G_PROJ + GP * c + g)
                        if kind in "KV":
                            gemm(g % 4, b % 2, lambda k: mhi[:, k, :], lambda k: mlo[:, k, :], M)
                        else:
                            gemm(g % 4, b % 2, lambda k, n=n: xhi[:, k, n, :], lambda k, n=n: xlo[:, k, n, :], NC)
                    if b >= 2 and PROJ[b - 1][0] == "V":
                        r = PROJ[b - 1][1]
                        released(pe, G_PROJ + GP * c + CUM[b - 1])
                        pe.wait_ge(kv_lo, 4 * c)
                        for t in range(2):
                            last = pe.transpose(ps[:, 6 + r, t * P:(t + 1) * P], kz[:, r, t * P:(t + 1) * P], ident[:, :])
                        last.then_inc(vt_mm0, 1)
            end_phase(pe, 2)

            with pe.Fori(0, HEADS) as h:
                pe.wait_ge(k_rot, h + 1)
                pe.wait_ge(cen, 4 * h)
                for i in range(4):
                    for c in range(4):
                        cc = 4 * i + c
                        last = pe.transpose(ps[:, i, c * P:(c + 1) * P], k_rot_b[:, cc * P:(cc + 1) * P], ident[:, :])
                    last.then_inc(kt_mm, 1)
                pe.wait_ge(l_v, 16 * h + 16)
                pe.wait_ge(std, 4 * h)
                for i in range(4):
                    for c in range(4):
                        cc = 4 * i + c
                        last = pe.transpose(ps[:, 4 + i, c * P:(c + 1) * P], vb[:, cc * P:(cc + 1) * P], ident[:, :])
                    last.then_inc(vt_mm, 1)
                pe.wait_ge(kt_ev, 4 * h + 4)
                pe.wait_ge(v2, 2 * h + 1)
                for i in range(4):
                    for c in range(4):
                        cc = 4 * i + c
                        last = pe.matmul(ps[:, i, c * P:(c + 1) * P], k_tok[:, cc, :], v_f[:, cc, :], start=True, stop=True)
                    last.then_inc(kvf_mm, 1)
                pe.wait_ge(v2, 2 * h + 2)
                for i in reversed(range(4)):
                    for c in range(4):
                        cc = 4 * i + c
                        last = pe.matmul(ps[:, 4 + i, c * P:(c + 1) * P], k_tok[:, cc, :], v_b[:, cc, :], start=True, stop=True)
                    last.then_inc(kvb_mm, 1)
                pe.wait_ge(q_rot, h + 1)
                pe.wait_ge(f_scan, 15 * h + 15)
                for i in range(4):
                    for c in range(4):
                        cc = 4 * i + c
                        last = pe.matmul(ps[:, i, c * P:(c + 1) * P], k_rot_b[:, cc * P:(cc + 1) * P],
                                         q_rot_b[:, cc * P:(cc + 1) * P], start=True, stop=True)
                    last.then_inc(s_mm, 1)
                pe.wait_ge(b_scan, 15 * h + 15)
                pe.wait_ge(p_qf, 2 * h + 2)
                for i in range(4):
                    pe.wait_ge(s_ev, 4 * h + i + 1)
                    for c in range(4):
                        cc = 4 * i + c
                        o = ps[:, 4 + i, c * P:(c + 1) * P]
                        pe.matmul(o, v_tok[:, cc, :], sT[:, cc, :], start=True, stop=False)
                        pe.matmul(o, st_f[:, cc, :], q_f[:, cc * P:(cc + 1) * P], start=False, stop=False)
                        last = pe.matmul(o, st_b[:, cc, :], q_b[:, cc * P:(cc + 1) * P], start=False, stop=True)
                    last.then_inc(y_mm, 1)
                for i in range(4):
                    pe.wait_ge(y_ev, 4 * h + i + 1)
                    pe.matmul(ps[:, i, :], mean_mat[:, :], y_b[:, i, :], start=True, stop=True).then_inc(me_mm, 1)
                for i in range(4):
                    pe.wait_ge(sqd, 4 * h + i + 1)
                    pe.matmul(ps[:, 4 + i, :], mean_mat[:, :], w1[:, i, :], start=True, stop=True).then_inc(va_mm, 1)
            pe.wait_ge(cen, 4 * HEADS)
            pe.wait_ge(std, 4 * HEADS)
            for n in range(NS):
                buf, sqb = ((qb_, qsb), (kb_, ksb))[n % 2]
                pe.wait_ge(c_in[n % 2], 16 * (n // 2) + 16)
                for c in range(CT):
                    last = pe.matmul(ps[:, n, :], mean_mat[:, :], buf[:, c * NC:(c + 1) * NC], start=(c == 0), stop=(c == CT - 1))
                last.then_inc(c_me, 1)
                pe.wait_ge(c_sq, n + 1)
                for c in range(CT):
                    last = pe.matmul(ps[:, 4 + n, :], mean_mat[:, :], sqb[:, c * NC:(c + 1) * NC], start=(c == 0), stop=(c == CT - 1))
                last.then_inc(c_va, 1)
            end_phase(pe, 3)

            def stats(h, count, first):
                pe.wait_ge(ss_done, 2 + count)
                if first is not None:
                    first()
                for n in range(NH):
                    pe.matmul(ps[:, 4 + n, :], mean_mat[:, :], ssq[:, n, :], start=True, stop=True).then_inc(n_mm, 1)

            with pe.Fori(0, 2) as h:
                G = G_HALF0 + G_PER_HALF * h
                J = J_HALF0 + J_PER_HALF * h
                H = H_PER_HALF * h

                def product(i, g, j, hi, lo, ready):
                    for s in range(2):
                        pe.wait_ge(w_ready, j + 2 * i + s + 3)
                        for n in range(NH):
                            bank_ready(g + 4 * i + 2 * s + n)
                            gemm(2 * s + n, s, lambda k: hi[:, k, n, :], lambda k: lo[:, k, n, :], NC,
                                 ready if s == 0 and n == 0 else None)

                wait_alone(pe, f_cp, 16 * h)
                with pe.Fori(0, KT // 2) as i:
                    product(i, G, J, ahi, alo, lambda k: pe.wait_ge(ysp_lo, KT * h + k + 1))
                stats(h, Q_PER_HALF * h + 16, None)
                with pe.Fori(0, XH) as hh:
                    for r in range(2):
                        pe.wait_ge(w_ready, J + J_XQ + 2 * hh + r + 3)
                        for n in range(NH):
                            bank_ready(G + G_XQ + 8 * hh + 2 * r + n)
                            gemm(2 * r + n, r, lambda k: bhi[:, k, n, :], lambda k: blo[:, k, n, :], NC,
                                 (lambda k: pe.wait_ge(lo_done, H + 2 * k + 2)) if r == n == 0 else None)
                    T = 32 * h + 8 * hh
                    pe.wait_ge(kv_in, 128 * h + 32 * hh + 32)

                    def scores(t):
                        n, tt = t // 4, t % 4
                        pe.wait_ge(lo_done, H + H_XQ + 4 * hh + 3 + n)
                        pe.wait_ge(p_exp, T + t + 1)
                        o = ps[:, 4 + t % 2, 0:M]
                        for r in range(2):
                            a, b = (q[:, 6 + r, n, tt * P:(tt + 1) * P] for q in (ahi, alo))
                            pe.matmul(o, a, kh[:, r, 0, :], start=(r == 0), stop=False)
                            pe.matmul(o, a, kh[:, r, 1, :], start=False, stop=False)
                            last = pe.matmul(o, b, kh[:, r, 0, :], start=False, stop=(r == 1))
                        last.then_inc(sc_mm, 1)

                    pe.wait_ge(n_sq, 6 * h + 2)
                    scores(0)
                    for t in range(8):
                        if t + 1 < 8:
                            scores(t + 1)
                        pe.wait_ge(p_nrm, T + t + 1)
                        pe.wait_ge(pt_lo, T + t + 1)
                        for m in range(2):
                            last = pe.transpose(ps[:, 6 + t % 2, m * P:(m + 1) * P], pr[:, t % 2, m * P:(m + 1) * P], ident[:, :])
                        last.then_inc(pt_mm, 1)
                        if t % 4 == 3:
                            n = t // 4
                            pe.wait_ge(pt_lo, T + t + 3)
                            for d in range(2):
                                bank_ready(G + G_XQ + 8 * hh + 4 + 2 * n + d)
                                o = ps[:, 2 * n + d, :]
                                for m in range(2):
                                    pe.matmul(o, vh[:, d, 0, m, :], pth[:, m, :], start=(m == 0), stop=False)
                                    pe.matmul(o, vh[:, d, 0, m, :], ptl[:, m, :], start=False, stop=False)
                                    last = pe.matmul(o, vh[:, d, 1, m, :], pth[:, m, :], start=False, stop=(m == 1))
                                last.then_inc(mm_done, 1)
                with pe.Fori(0, KT // 2) as i:
                    product(i, G + G_XO, J + J_XO, ahi, alo, lambda k: released(pe, G + G_XQ + 8 * (k // 2) + 6 + k % 2))
                stats(h, Q_PER_HALF * h + 32, lambda: pe.wait_ge(p_exp, 32 * h + 32 + 2))
                with pe.Fori(0, FG) as g:
                    with pe.Fori(0, KT // 2) as i:
                        product(i, G + G_FF + 32 * g, J + J_FF + 16 * g, bhi, blo,
                                lambda k: pe.wait_ge(lo_done, H + H_XO + 2 * k + 2))
                    with pe.Fori(0, KT // 2) as i:
                        product(i, G + G_FF + 32 * g + 16, J + J_FF + 16 * g + KT, ahi, alo,
                                lambda k: pe.wait_ge(lo_done, H + H_FF + 16 * g + 2 * k + 2))
                stats(h, Q_PER_HALF * h + 48, lambda: pe.wait_ge(n_sq, 6 * h + 4))
                pe.wait_ge(n_sq, 6 * h + 6)
                released(pe, G + G_PER_HALF - 1)
                for n in range(NH):
                    pe.wait_ge(f_cp, 16 * h + 8 * n)
                    for k in range(KT):
                        pe.wait_ge(zf, 16 * h + 8 * n + k + 1)
                        for t in range(4):
                            last = pe.transpose(ps[:, 2 * t + k // 4, (k % 4) * P:(k % 4 + 1) * P],
                                                z[:, k % 2, t * P:(t + 1) * P], ident[:, :])
                        last.then_inc(f_tr, 1)

        @block.scalar
        def _(act):
            act.wait_ge(consts, 5)
            act.activation(junk[:, 0:1], eps[:, :], ACT.Copy).then_inc(p_exp, 2)
            with act.Fori(0, NS) as n:
                for k in range(KT):
                    g = KT * n + k
                    act.wait_ge(mm_done, g + 1)
                    act.activation(xhi[:, k, n, :], ps[:, k % 4, :], ACT.Copy).then_inc(hi0, 1)
                    act.wait_ge(ssq_done, g + 1)
                    act.activation(sq0[:, k % 2, :], ps[:, k % 4, :], ACT.Square).then_inc(sq0_done, 1)
            for k in range(KT):
                g = G_MEM + k
                act.wait_ge(mm_done, g + 1)
                act.activation(mhi[:, k, :], ps[:, k % 4, 0:M], ACT.Copy).then_inc(hi0, 1)
                act.wait_ge(ssq_done, g + 1)
                act.activation(sq0[:, k % 2, 0:M], ps[:, k % 4, 0:M], ACT.Square).then_inc(sq0_done, 1)
            for n in range(NS):
                act.wait_ge(stat_mm, n + 1)
                act.activation(rs[:, n, :], ps[:, 4 + n, :], ACT.Sqrt, bias=eps[:, :], scale=P / D).then_inc(stat_sq, 1)
            act.wait_ge(stat_mm, NS + 1)
            act.activation(rsm[:, :], ps[:, 4, 0:M], ACT.Sqrt, bias=eps[:, :], scale=P / D).then_inc(stat_sq, 1)
            end_phase(act, 1)

            with act.Fori(0, HEADS) as c:
                G = G_PROJ + GP * c

                def last_of(b):
                    released(act, G + CUM[b + 1] - 1)

                def store_proj(b, tile):
                    for n in range(NS):
                        released(act, G + CUM[b] + n)
                        act.dma_start(proj_d[tile + c, :, n * NC:(n + 1) * NC], st[:, n, :]).then_inc(st_st[n], 16)

                def high(b, slot):
                    act.wait_ge(kv_st[slot], 16 * c)
                    if slot < 2:
                        act.wait_ge(vt_mm0, 2 * c + slot + 1)
                        act.activation(khl[:, slot, 0, :], ps[:, 6 + slot, 0:M], ACT.Copy).then_inc(kv_hi, 1)
                    else:
                        last_of(b)
                        act.activation(khl[:, slot, 0, :], kz[:, slot, :], ACT.Copy).then_inc(kv_hi, 1)

                def store_kv(slot, order):
                    act.wait_ge(kv_lo, 4 * c + order + 1)
                    dst = (v_d if slot < 2 else k_d)[2 * c + slot % 2]
                    act.dma_start(dst, khl[:, slot, :, :].bitcast(F32)).then_inc(kv_st[slot], 16)

                for n in range(NS):
                    released(act, G + CUM[2] + n)
                    act.activation(st[:, n, :], st[:, n, :], ACT.Sigmoid).then_inc(sig_done, 1)
                high(1, 0)
                store_kv(0, 0)
                store_proj(4, 0)
                high(3, 1)
                store_kv(1, 1)
                high(5, 2)
                store_kv(2, 2)
                store_proj(6, 4)
                high(7, 3)
                store_kv(3, 3)
                store_proj(8, 8)
                store_proj(9, 12)
                act.wait_ge(conv_step, TAPS * c + TAPS)
                act.dma_start(conv_d[c], acc[:, :]).then_inc(acc_st, 16)
            for n in range(NS):
                act.wait_ge(st_st[n], 16 * 4 * HEADS)
                act.wait_ge(kv_st[n], 16 * HEADS)
            act.wait_ge(acc_st, 16 * HEADS)
            end_phase(act, 2)

            act.wait_ge(tab, 3)
            act.activation(lg[:, 1], lg[:, 0], ACT.Exp, scale=-1.0).then_inc(tab_act, 1)
            act.wait_ge(tab, 4)
            act.activation(lg[:, 3], lg[:, 2], ACT.Ln).then_inc(tab_act, 1)
            act.wait_ge(tab, 11)
            act.wait_ge(iot, 5)
            for h in range(HEADS):
                for d, xi in ((0, xi_f), (1, xi_b)):
                    s = lg[:, 5, d, h:h + 1]
                    act.activation(xi[:, h, :], io_s[:, d, :], ACT.Exp, scale=s).then_inc(tab_act, 1)
                    act.activation(zeta[:, d, h:h + 1], io_c[:, d:d + 1], ACT.Exp, scale=s).then_inc(tab_act, 1)
            act.activation(gch[:, :, :], lg[:, 5], ACT.Exp, scale=float(P)).then_inc(tab_act, 1)
            act.wait_ge(tab, 12)
            act.wait_ge(tab, 12 + HEADS)
            act.activation(dmask[:, :, :], dmask[:, :, :], ACT.Exp).then_inc(tab_act, 1)
            act.wait_ge(tab, 21 + HEADS)
            act.activation(sin_t[:, :], q_rot_b[:, :], ACT.Sin).then_inc(tab_ok, 1)
            act.activation(cos_t[:, :], k_rot_b[:, :], ACT.Sin, bias=half_pi[:, :], scale=-1.0).then_inc(tab_ok, 1)

            with act.Fori(0, HEADS) as h:
                act.wait_ge(kvb_mm, 4 * h)
                for i in range(4):
                    act.wait_ge(kt_mm, 4 * h + i + 1)
                    act.activation(k_tok[:, 4 * i:4 * i + 4, :].rearrange("p c d -> p (c d)"), ps[:, i, :], ACT.Copy).then_inc(kt_ev, 1)
                act.wait_ge(y_mm, 4 * h)
                for i in range(4):
                    act.wait_ge(vt_mm, 4 * h + i + 1)
                    act.activation(v_tok[:, 4 * i:4 * i + 4, :].rearrange("p c d -> p (c d)"), ps[:, 4 + i, :], ACT.Copy).then_inc(vt_ev, 1)
                act.wait_ge(l_g, 16 * h + 16)
                act.wait_ge(nrm, 20 * h)
                for i in range(4):
                    act.activation(sg[:, i, :], gb[:, i * NC:(i + 1) * NC], ACT.Sigmoid).then_inc(sgd, 1)
                act.wait_ge(y_st, 16 * h)
                for i in range(4):
                    act.wait_ge(y_mm, 4 * h + i + 1)
                    act.activation(y_b[:, i, :], ps[:, 4 + i, :], ACT.Copy).then_inc(y_ev, 1)
                for i in range(4):
                    act.wait_ge(cen, 4 * h + i + 1)
                    act.activation(w1[:, i, :], y_b[:, i, :], ACT.Square).then_inc(sqd, 1)
                for i in range(4):
                    act.wait_ge(va_mm, 4 * h + i + 1)
                    act.activation(w1[:, i, :], ps[:, 4 + i, :], ACT.Sqrt, bias=eps[:, :]).then_inc(std, 1)
            for n in range(NS):
                buf, sqb = ((qb_, qsb), (kb_, ksb))[n % 2]
                act.wait_ge(c_cen, n + 1)
                act.activation(sqb[:, :], buf[:, :], ACT.Square).then_inc(c_sq, 1)
                act.wait_ge(c_va, n + 1)
                act.activation(w1[:, n, :], ps[:, 4 + n, :], ACT.Sqrt, bias=eps[:, :], scale=P / CW).then_inc(c_std, 1)
                act.wait_ge(c_nrm, 7 * n + 6)
                act.activation(sqb[:, :], buf[:, :], ACT.Sigmoid).then_inc(c_sig, 1)
            end_phase(act, 3)

            with act.Fori(0, 2) as h:
                G = G_HALF0 + G_PER_HALF * h
                H = H_PER_HALF * h
                Q = Q_PER_HALF * h
                act.wait_ge(zf, 16 * h)
                act.wait_ge(mm_done, G)
                for k in range(KT):
                    act.dma_start(res[:, k, :, :].rearrange("p a b -> p (a b)"),
                                  y_d[k, :, bass.ds(h * HALF, HALF)]).then_inc(y_in[k], 16)
                for k in range(KT):
                    act.wait_ge(y_in[k], 16 * h + 16)
                    act.activation(ahi[:, k, :, :], res[:, k, :, :], ACT.Copy).then_inc(ysp_hi, 1)
                    if k:
                        act.wait_ge(ysp_lo, KT * h + k)
                        act.dma_start(res[:, k - 1, :, :], xT_d[k - 1, :, bass.ds(2 * h, 2), :]).then_inc(r_in[k - 1], 16)
                act.wait_ge(ysp_lo, KT * h + KT)
                act.dma_start(res[:, KT - 1, :, :], xT_d[KT - 1, :, bass.ds(2 * h, 2), :]).then_inc(r_in[KT - 1], 16)
                for s in range(2):
                    act.wait_ge(f_st[s], 128 * h)

                def residual(i, u, hb, qb):
                    for s in range(2):
                        for n in range(NH):
                            e = 4 * i + 2 * s + n
                            released(act, u + 4 * i + 2 * s + n)
                            act.activation(bhi[:, 2 * i + s, n, :], res[:, 2 * i + s, n, :], ACT.Copy).then_inc(hi_done, 1)
                            wait_alone(act, ss_done, qb + e + 1)
                            act.activation(sq[:, n, :], res[:, 2 * i + s, n, :], ACT.Square).then_inc(sq_done, 1)

                def norm_sqrt(count):
                    for n in range(NH):
                        act.wait_ge(n_mm, 6 * h + count + n + 1)
                        act.activation(rstd[:, n, :], ps[:, 4 + n, :], ACT.Sqrt, bias=eps[:, :], scale=P / D).then_inc(n_sq, 1)

                with act.Fori(0, KT // 2) as i:
                    residual(i, G, H, Q)
                norm_sqrt(0)
                with act.Fori(0, XH) as hh:
                    T = 32 * h + 8 * hh
                    act.wait_ge(mm_done, G + G_XQ + 8 * hh)
                    act.dma_start(kh[:, :, :, :].bitcast(F32), k_d[bass.ds(2 * hh, 2)].rearrange("r p a m -> p r a m")).then_inc(kv_in, 16)
                    act.dma_start(vh[:, :, :, :, :].rearrange("p d a m k -> p d a (m k)").bitcast(F32),
                                  v_d[bass.ds(2 * hh, 2)].rearrange("r p a m -> p r a m")).then_inc(kv_in, 16)
                    for r in range(2):
                        for n in range(NH):
                            e = 4 * hh + 2 * r + n
                            released(act, G + G_XQ + 8 * hh + 2 * r + n)
                            act.activation(ahi[:, 6 + r, n, :], z[:, n, :], ACT.Copy).then_inc(hi_done, 1)

                    def o_high(n):
                        for d in range(2):
                            act.wait_ge(mm_done, G + G_XQ + 8 * hh + 4 + 2 * n + d + 1)
                            act.activation(ahi[:, 2 * hh + d, n, :], ps[:, 2 * n + d, :], ACT.Copy).then_inc(o_hi, 1)

                    for t in range(9):
                        if t < 8:
                            act.wait_ge(nb_done, T + t + 1)
                            act.activation(pr[:, t % 2, :], ps[:, 4 + t % 2, 0:M], ACT.Exp, bias=nb[:, t:t + 1],
                                           scale=XSCALE, accum_out=sm[:, t:t + 1]).then_inc(p_exp, 1)
                        if t >= 1:
                            u = t - 1
                            act.wait_ge(pt_mm, T + u + 1)
                            act.activation(pth[:, :, (u % 4) * P:(u % 4 + 1) * P],
                                           ps[:, 6 + u % 2, 0:M].rearrange("p (m k) -> p m k", m=2), ACT.Copy).then_inc(pt_hi, 1)
                        if t == 5:
                            o_high(0)
                        if t == 8:
                            o_high(1)
                with act.Fori(0, KT // 2) as i:
                    residual(i, G + G_XO, H + H_XO, Q + 16)
                norm_sqrt(2)
                with act.Fori(0, FG) as g:
                    with act.Fori(0, KT // 2) as i:
                        for s in range(2):
                            for n in range(NH):
                                e = 4 * i + 2 * s + n
                                act.wait_ge(z_up, 64 * h + 16 * g + e + 1)
                                act.activation(ahi[:, 2 * i + s, n, :], z[:, n, :], ACT.Copy).then_inc(hi_done, 1)
                for k in range(KT):
                    for n in range(NH):
                        e = 2 * k + n
                        if k == 0:
                            released(act, G + G_PER_HALF - 1)
                        act.wait_ge(ss_done, Q + 32 + e + 1)
                        act.activation(sq[:, n, :], res[:, k, n, :], ACT.Square).then_inc(sq_done, 1)
                norm_sqrt(4)
                for n in range(NH):
                    act.wait_ge(f_tr, 16 * h + 8 * n + 8)
                    for b in range(8):
                        act.wait_ge(f_st[b % 2], 128 * h + 64 * n + 16 * (b // 2))
                        if n == b == 0:
                            act.wait_ge(ss_done, Q + 48 + 2)
                        act.activation(sq[:, b % 2, :], ps[:, b, :], ACT.Copy).then_inc(f_cp, 1)
                        act.wait_ge(f_cp, 16 * h + 8 * n + b + 1)
                        act.dma_start(out[0, bass.ds(h * HALF + n * NC + (b // 2) * P, P), (b % 2) * NC:(b % 2 + 1) * NC],
                                      sq[:, b % 2, :]).then_inc(f_st[b % 2], 16)
            for s in range(2):
                act.wait_ge(f_st[s], 256)

        @block.vector
        def _(dve):
            dve.memset(ssq0[:, :, :], 0.0).then_inc(ssq_done, 1)
            dve.memset(ssqm[:, :], 0.0).then_inc(ssq_done, 1)
            dve.memset(junk[:, 3:4], 0.0).then_inc(bank_free, G0)
            dve.wait_ge(vec_mm, 1)
            dve.tensor_copy(vec[:, :], ps[:, 4, 0:60]).then_inc(vec_ok, 1)
            dve.wait_ge(vec_mm, 2)
            dve.tensor_copy(taps[:, :], ps[:, 5, 0:TAPS * CT]).then_inc(vec_ok, 1)
            with dve.Fori(0, NS) as n:
                for k in range(KT):
                    g = KT * n + k
                    dve.wait_ge(sq0_done, g + 1)
                    dve.tensor_tensor(xlo[:, k, n, :], ps[:, k % 4, :], xhi[:, k, n, :], ALU.subtract).then_inc(bank_free, 1)
                    dve.wait_ge(ssq_done, g + 2)
                    dve.tensor_tensor(ssq0[:, n, :], ssq0[:, n, :], sq0[:, k % 2, :], ALU.add).then_inc(ssq_done, 1)
            for k in range(KT):
                g = G_MEM + k
                dve.wait_ge(sq0_done, g + 1)
                dve.tensor_tensor(mlo[:, k, :], ps[:, k % 4, 0:M], mhi[:, k, :], ALU.subtract).then_inc(bank_free, 1)
                dve.wait_ge(ssq_done, g + 2)
                dve.tensor_tensor(ssqm[:, :], ssqm[:, :], sq0[:, k % 2, 0:M], ALU.add).then_inc(ssq_done, 1)
            for n in range(NS):
                dve.wait_ge(stat_sq, n + 1)
                dve.reciprocal(rs[:, n, :], rs[:, n, :]).then_inc(stat_rc, 1)
            dve.wait_ge(stat_sq, NS + 1)
            dve.reciprocal(rsm[:, :], rsm[:, :]).then_inc(stat_rc, 1)
            dve.wait_ge(stat_rc, NS + 1)
            end_phase(dve, 1)

            dve.memset(upad[:, :], 0.0).then_inc(pad_ok, 1)
            dve.wait_ge(pad_ok, 1)
            with dve.Fori(0, HEADS) as c:
                G = G_PROJ + GP * c

                def evac(b, n, dst):
                    g = CUM[b] + n
                    dve.wait_ge(mm_done, G + g + 1)
                    dve.tensor_tensor(dst, ps[:, g % 4, :], rs[:, n, :], ALU.mult).then_inc(bank_free, 1)

                def evac_kv(b, slot):
                    g = CUM[b]
                    dve.wait_ge(mm_done, G + g + 1)
                    dve.tensor_tensor(kz[:, slot, :], ps[:, g % 4, 0:M], rsm[:, :], ALU.mult).then_inc(bank_free, 1)

                def low(slot, order):
                    dve.wait_ge(kv_hi, 4 * c + order + 1)
                    src = ps[:, 6 + slot, 0:M] if slot < 2 else kz[:, slot, :]
                    dve.tensor_tensor(khl[:, slot, 1, :], src, khl[:, slot, 0, :], ALU.subtract).then_inc(kv_lo, 1)

                def tap(t):
                    src = upad[:, t:t + S]
                    dve.wait_ge(conv_step, TAPS * c + t)
                    if t == 0:
                        dve.wait_ge(acc_st, 16 * c)
                        ins = dve.tensor_scalar(acc[:, :], src, taps[:, bass.ds(c, 1)], vec[:, bass.ds(V_CB + c, 1)],
                                                ALU.mult, ALU.add)
                    else:
                        ins = dve.scalar_tensor_tensor(out=acc[:, :], in0=src, scalar=taps[:, bass.ds(CT * t + c, 1)],
                                                       in1=acc[:, :], op0=ALU.mult, op1=ALU.add)
                    ins.then_inc(conv_step, 1)

                dve.wait_ge(conv_step, TAPS * c)
                for n in range(NS):
                    evac(0, n, upad[:, PAD + n * NC:PAD + (n + 1) * NC])
                evac_kv(1, 0)
                for n in range(NS):
                    dve.wait_ge(st_st[n], 64 * c)
                    evac(2, n, st[:, n, :])
                for n in range(NS):
                    dve.wait_ge(sig_done, 4 * c + n + 1)
                    u = upad[:, PAD + n * NC:PAD + (n + 1) * NC]
                    dve.tensor_tensor(u, u, st[:, n, :], ALU.mult).then_inc(u_done, 1)
                dve.wait_ge(u_done, 4 * c + 4)
                low(0, 0)
                evac_kv(3, 1)
                t = 0
                for stage, b in enumerate((4, 6, 8, 9)):
                    for n in range(NS):
                        if stage:
                            dve.wait_ge(st_st[n], 64 * c + 16 * stage)
                        evac(b, n, st[:, n, :])
                        for _ in range(2):
                            if t < TAPS:
                                tap(t)
                                t += 1
                        if stage == 0 and n == 3:
                            low(1, 1)
                            evac_kv(5, 2)
                        if stage == 1 and n == 0:
                            low(2, 2)
                        if stage == 1 and n == 3:
                            evac_kv(7, 3)
                        if stage == 2 and n == 0:
                            low(3, 3)
            end_phase(dve, 2)

            def step(ins, n):
                ins.then_inc(tab, 1)
                dve.wait_ge(tab, n)
            step(dve.memset(st_f[:, 0, :], 0.0), 1)
            dve.wait_ge(tab_in, 64)
            step(dve.memset(st_b[:, CH - 1, :], 0.0), 2)
            step(dve.scalar_tensor_tensor(out=lg[:, 0], in0=dec[:, :, :], scalar=-1.0, in1=dec[:, :, :],
                                          op0=ALU.mult, op1=ALU.max), 3)
            dve.wait_ge(tab_act, 1)
            step(dve.tensor_scalar(lg[:, 2], lg[:, 1], 1.0, None, ALU.add), 4)
            step(dve.tensor_scalar(lg[:, 4], lg[:, 2], -1.0, None, ALU.add), 5)
            step(dve.tensor_tensor(lg[:, 4], lg[:, 1], lg[:, 4], ALU.subtract), 6)
            step(dve.reciprocal(lg[:, 5], lg[:, 2]), 7)
            step(dve.tensor_tensor(lg[:, 4], lg[:, 4], lg[:, 5], ALU.mult), 8)
            dve.wait_ge(tab_act, 2)
            step(dve.tensor_tensor(lg[:, 4], lg[:, 4], lg[:, 3], ALU.add), 9)
            step(dve.tensor_scalar(lg[:, 5], dec[:, :, :], 0.0, None, ALU.min), 10)
            step(dve.tensor_tensor(lg[:, 5], lg[:, 5], lg[:, 4], ALU.subtract), 11)
            dve.wait_ge(iot, 5)
            dve.tensor_scalar(io_t[:, 1, :], io_t[:, 0, :], 0.0, None, ALU.max).then_inc(r_q, 1)
            dve.wait_ge(r_q, 1)
            step(dve.tensor_scalar(io_t[:, 2, :], io_t[:, 0, :], 0.0, -1.0, ALU.min, ALU.mult), 12)
            for h in range(HEADS):
                dve.tensor_scalar(dmask[:, h, :], io_t[:, 1, :], lg[:, 5, 0, h:h + 1], None, ALU.mult).then_inc(r_k, 1)
                dve.wait_ge(r_k, h + 1)
                step(dve.scalar_tensor_tensor(out=dmask[:, h, :], in0=io_t[:, 2, :], scalar=lg[:, 5, 1, h:h + 1],
                                              in1=dmask[:, h, :], op0=ALU.mult, op1=ALU.add), 13 + h)
            n0 = 12 + HEADS
            ang, turns = q_rot_b, k_rot_b
            step(dve.tensor_copy(ang[:, :], pos_i[:, :]), n0 + 1)
            step(dve.tensor_scalar(ang[:, :], ang[:, :], freq[:, 0:1], None, ALU.mult), n0 + 2)
            step(dve.tensor_scalar(turns[:, :], ang[:, :], float(1 / (2 * np.pi)), MAGIC, ALU.mult, ALU.add), n0 + 3)
            step(dve.tensor_scalar(turns[:, :], turns[:, :], -MAGIC, None, ALU.add), n0 + 4)
            for m, part in enumerate(TWO_PI_PARTS):
                step(dve.scalar_tensor_tensor(out=ang[:, :], in0=turns[:, :], scalar=-part, in1=ang[:, :],
                                              op0=ALU.mult, op1=ALU.add), n0 + 5 + m)
            step(dve.tensor_scalar(ang[:, :], ang[:, :], 3.1415925, -3.1415925, ALU.min, ALU.max), n0 + 8)
            step(dve.scalar_tensor_tensor(out=turns[:, :], in0=ang[:, :], scalar=-1.0, in1=ang[:, :],
                                          op0=ALU.mult, op1=ALU.max), n0 + 9)
            dve.wait_ge(tab_act, 2 + 4 * HEADS + 2)
            step(dve.tensor_scalar(dmask[:, :, :], dmask[:, :, :], KSCALE, None, ALU.mult), n0 + 10)
            step(dve.tensor_scalar(zeta[:, :, :], zeta[:, :, :], KSCALE, None, ALU.mult), n0 + 11)
            dve.wait_ge(tab_ok, 2)

            def rotate(h):
                dve.wait_ge(s_mm, 4 * h)
                dve.wait_ge(p_qf, 2 * h)
                for raw, sw, dst, ld, p, r, done, base in ((qb_, qsb, q_rot_b, l_q, p_qs, r_q, q_rot, 1),
                                                           (kb_, ksb, k_rot_b, l_k, p_ks, r_k, k_rot, HEADS)):
                    dve.wait_ge(ld, 16 * h + 16)
                    dve.tensor_tensor(raw[:, :], raw[:, :], cos_t[:, :], ALU.mult).then_inc(r, 1)
                    dve.wait_ge(r, base + h + 1)
                    dve.wait_ge(p, h + 1)
                    dve.tensor_tensor(dst[:, :], raw[:, :], sw[:, :], ALU.add).then_inc(done, 1)

            def core(h):
                dve.wait_ge(vt_ev, 4 * h + 4)
                dve.wait_ge(kvb_mm, 4 * h)
                dve.tensor_scalar(v_f[:, :, :], v_tok[:, :, :], zeta[:, 0, bass.ds(h, 1)], None, ALU.mult).then_inc(v2, 1)
                dve.tensor_scalar(v_b[:, :, :], v_tok[:, :, :], zeta[:, 1, bass.ds(h, 1)], None, ALU.mult).then_inc(v2, 1)
                dve.wait_ge(y_mm, 4 * h)
                for c in range(CH - 1):
                    if c % 4 == 0:
                        dve.wait_ge(kvf_mm, 4 * h + c // 4 + 1)
                    dve.wait_ge(f_scan, 15 * h + c)
                    dve.scalar_tensor_tensor(out=st_f[:, c + 1, :], in0=st_f[:, c, :], scalar=gch[:, 0, bass.ds(h, 1)],
                                             in1=ps[:, c // 4, (c % 4) * P:(c % 4 + 1) * P],
                                             op0=ALU.mult, op1=ALU.add).then_inc(f_scan, 1)
                for m in range(CH - 1):
                    c = CH - 1 - m
                    if m % 4 == 0:
                        dve.wait_ge(kvb_mm, 4 * h + m // 4 + 1)
                    dve.wait_ge(b_scan, 15 * h + m)
                    dve.scalar_tensor_tensor(out=st_b[:, c - 1, :], in0=st_b[:, c, :], scalar=gch[:, 1, bass.ds(h, 1)],
                                             in1=ps[:, 4 + c // 4, (c % 4) * P:(c % 4 + 1) * P],
                                             op0=ALU.mult, op1=ALU.add).then_inc(b_scan, 1)
                for i in range(4):
                    dve.wait_ge(s_mm, 4 * h + i + 1)
                    dve.tensor_tensor(sT[:, 4 * i:4 * i + 4, :], ps[:, i, :].rearrange("p (c q) -> p c q", c=4),
                                      dmask[:, h, :].unsqueeze(1).to_broadcast([P, 4, P]), ALU.mult).then_inc(s_ev, 1)

            def norm(h):
                B = 20 * h
                for i in range(4):
                    dve.wait_ge(me_mm, 4 * h + i + 1)
                    dve.tensor_tensor(y_b[:, i, :], y_b[:, i, :], ps[:, i, :], ALU.subtract).then_inc(cen, 1)
                for i in range(4):
                    dve.wait_ge(sgd, 4 * h + i + 1)
                    g = gb[:, i * NC:(i + 1) * NC]
                    dve.tensor_tensor(sg[:, i, :], g, sg[:, i, :], ALU.mult).then_inc(nrm, 1)
                for i in range(4):
                    dve.wait_ge(std, 4 * h + i + 1)
                    dve.reciprocal(w1[:, i, :], w1[:, i, :]).then_inc(nrm, 1)
                for i in range(4):
                    dve.wait_ge(nrm, B + 5 + i)
                    dve.tensor_tensor(y_b[:, i, :], y_b[:, i, :], w1[:, i, :], ALU.mult).then_inc(nrm, 1)
                for i in range(4):
                    dve.wait_ge(nrm, B + 9 + i)
                    dve.tensor_scalar(y_b[:, i, :], y_b[:, i, :], vec[:, bass.ds(V_GNW + h, 1)], vec[:, bass.ds(V_GNB + h, 1)],
                                      ALU.mult, ALU.add).then_inc(nrm, 1)
                for i in range(4):
                    dve.wait_ge(nrm, B + 13 + i)
                    dve.tensor_tensor(y_b[:, i, :], y_b[:, i, :], sg[:, i, :], ALU.mult).then_inc(nrm, 1)

            rotate(0)
            with dve.Fori(0, HEADS - 1) as h:
                core(h)
                rotate(h + 1)
                norm(h)
            core(HEADS - 1)
            norm(HEADS - 1)
            for n in range(NS):
                buf, sqb = ((qb_, qsb), (kb_, ksb))[n % 2]
                B = 7 * n
                b4 = buf[:, :].rearrange("p (c n) -> p c n", c=CT)
                dve.wait_ge(c_me, n + 1)
                for c in range(CT):
                    o = buf[:, c * NC:(c + 1) * NC]
                    ins = dve.scalar_tensor_tensor(out=o, in0=ps[:, n, :], scalar=-float(P) / CW, in1=o, op0=ALU.mult, op1=ALU.add)
                ins.then_inc(c_cen, 1)
                dve.wait_ge(c_std, n + 1)
                dve.reciprocal(w1[:, n, :], w1[:, n, :]).then_inc(c_nrm, 1)
                dve.wait_ge(c_nrm, B + 1)
                dve.tensor_tensor(b4, b4, w1[:, n, :].unsqueeze(1).to_broadcast([P, CT, NC]), ALU.mult).then_inc(c_nrm, 1)
                dve.wait_ge(c_nrm, B + 2)
                for c in range(CT):
                    dve.tensor_scalar(b4[:, c, :], b4[:, c, :], vec[:, V_LNW + c:V_LNW + c + 1], vec[:, V_LNB + c:V_LNB + c + 1],
                                      ALU.mult, ALU.add).then_inc(c_nrm, 1)
                dve.wait_ge(c_sig, n + 1)
                dve.wait_ge(c_nrm, B + 6)
                dve.tensor_tensor(buf[:, :], buf[:, :], sqb[:, :], ALU.mult).then_inc(c_nrm, 1)
            end_phase(dve, 3)

            dve.memset(junk[:, 4:5], 0.0).then_inc(ss_done, 2)
            dve.memset(junk[:, 5:6], 0.0).then_inc(pt_lo, 2)
            with dve.Fori(0, 2) as h:
                G = G_HALF0 + G_PER_HALF * h
                H = H_PER_HALF * h
                Q = Q_PER_HALF * h
                for k in range(KT):
                    dve.wait_ge(ysp_hi, KT * h + k + 1)
                    dve.tensor_tensor(alo[:, k, :, :], res[:, k, :, :], ahi[:, k, :, :], ALU.subtract).then_inc(ysp_lo, 1)

                def residual(i, g, hb, qb):
                    for s in range(2):
                        for n in range(NH):
                            e = 4 * i + 2 * s + n
                            m = 2 * i + s
                            dve.wait_ge(mm_done, g + e + 1)
                            dve.tensor_tensor(res[:, m, n, :], ps[:, 2 * s + n, :], res[:, m, n, :], ALU.add).then_inc(bank_free, 1)
                            dve.wait_ge(hi_done, hb + e + 1)
                            dve.tensor_tensor(blo[:, m, n, :], res[:, m, n, :], bhi[:, m, n, :], ALU.subtract).then_inc(lo_done, 1)
                            dve.wait_ge(sq_done, qb + e + 1)
                            dve.wait_ge(ss_done, qb + e + 1)
                            dve.tensor_tensor(ssq[:, n, :], ssq[:, n, :], sq[:, n, :], ALU.add).then_inc(ss_done, 1)

                def norm_recip(count):
                    for n in range(NH):
                        dve.wait_ge(n_sq, 6 * h + count + n + 1)
                        dve.reciprocal(rstd[:, n, :], rstd[:, n, :]).then_inc(n_rc, 1)
                    dve.wait_ge(n_rc, 6 * h + count + 2)

                def zero_sums(count):
                    dve.memset(ssq[:, :, :], 0.0).then_inc(ss_zero, 1)
                    wait_alone(dve, ss_zero, 3 * h + count + 1)

                zero_sums(0)
                for k in range(KT):
                    wait_alone(dve, r_in[k], 16 * h + 16)
                with dve.Fori(0, KT // 2) as i:
                    residual(i, G, H, Q)
                norm_recip(0)
                zero_sums(1)
                with dve.Fori(0, XH) as hh:
                    T = 32 * h + 8 * hh
                    for r in range(2):
                        for n in range(NH):
                            e = 2 * r + n
                            dve.wait_ge(mm_done, G + G_XQ + 8 * hh + e + 1)
                            dve.tensor_tensor(z[:, n, :], ps[:, e, :], rstd[:, n, :], ALU.mult).then_inc(bank_free, 1)
                            dve.wait_ge(hi_done, H + H_XQ + 4 * hh + e + 1)
                            dve.tensor_tensor(alo[:, 6 + r, n, :], z[:, n, :], ahi[:, 6 + r, n, :], ALU.subtract).then_inc(lo_done, 1)

                    def row_max(t):
                        dve.wait_ge(sc_mm, T + t + 1)
                        dve.tensor_reduce(mx[:, t:t + 1], ps[:, 4 + t % 2, 0:M], AX.X, ALU.max).then_inc(mx_done, 1)
                        dve.wait_ge(mx_done, T + t + 1)
                        dve.tensor_scalar(nb[:, t:t + 1], mx[:, t:t + 1], -XSCALE, None, ALU.mult).then_inc(nb_done, 1)

                    def o_low(n):
                        for d in range(2):
                            dve.wait_ge(o_hi, 16 * h + 4 * hh + 2 * n + d + 1)
                            dve.tensor_tensor(alo[:, 2 * hh + d, n, :], ps[:, 2 * n + d, :], ahi[:, 2 * hh + d, n, :],
                                              ALU.subtract).then_inc(bank_free, 1)

                    row_max(0)
                    for t in range(9):
                        if t < 8:
                            dve.wait_ge(p_exp, T + t + 3)
                            dve.reciprocal(ri[:, t:t + 1], sm[:, t:t + 1]).then_inc(ri_done, 1)
                            dve.wait_ge(ri_done, T + t + 1)
                            dve.tensor_scalar(pr[:, t % 2, :], pr[:, t % 2, :], ri[:, t:t + 1], None, ALU.mult).then_inc(p_nrm, 1)
                        if t >= 1:
                            u = t - 1
                            dve.wait_ge(pt_hi, T + u + 1)
                            cols = slice((u % 4) * P, (u % 4 + 1) * P)
                            dve.tensor_tensor(ptl[:, :, cols], ps[:, 6 + u % 2, 0:M].rearrange("p (m k) -> p m k", m=2),
                                              pth[:, :, cols], ALU.subtract).then_inc(pt_lo, 1)
                        if t == 5:
                            o_low(0)
                        if t == 8:
                            o_low(1)
                        if t + 1 < 8:
                            row_max(t + 1)
                with dve.Fori(0, KT // 2) as i:
                    residual(i, G + G_XO, H + H_XO, Q + 16)
                norm_recip(2)
                zero_sums(2)
                with dve.Fori(0, FG) as g:
                    with dve.Fori(0, KT // 2) as i:
                        for s in range(2):
                            for n in range(NH):
                                e = 4 * i + 2 * s + n
                                gg = G + G_FF + 32 * g + e
                                dve.wait_ge(mm_done, gg + 1)
                                dve.tensor_tensor(z[:, n, :], ps[:, 2 * s + n, :], rstd[:, n, :], ALU.mult).then_inc(bank_free, 1)
                                released(dve, gg)
                                dve.scalar_tensor_tensor(out=z[:, n, :], in0=z[:, n, :], scalar=0.0, in1=z[:, n, :],
                                                         op0=ALU.max, op1=ALU.mult).then_inc(z_up, 1)
                                dve.wait_ge(hi_done, H + H_FF + 16 * g + e + 1)
                                dve.tensor_tensor(alo[:, 2 * i + s, n, :], z[:, n, :], ahi[:, 2 * i + s, n, :],
                                                  ALU.subtract).then_inc(lo_done, 1)
                    with dve.Fori(0, KT // 2) as i:
                        for s in range(2):
                            for n in range(NH):
                                e = 4 * i + 2 * s + n
                                m = 2 * i + s
                                gg = G + G_FF + 32 * g + 16 + e
                                dve.wait_ge(mm_done, gg + 1)
                                dve.tensor_tensor(res[:, m, n, :], ps[:, 2 * s + n, :], res[:, m, n, :], ALU.add).then_inc(bank_free, 1)
                for k in range(KT):
                    for n in range(NH):
                        e = 2 * k + n
                        dve.wait_ge(sq_done, Q + 32 + e + 1)
                        dve.wait_ge(ss_done, Q + 32 + e + 1)
                        dve.tensor_tensor(ssq[:, n, :], ssq[:, n, :], sq[:, n, :], ALU.add).then_inc(ss_done, 1)
                norm_recip(4)
                for n in range(NH):
                    for k in range(KT):
                        e = 8 * n + k
                        if e >= 2:
                            dve.wait_ge(f_tr, 16 * h + e - 1)
                        dve.scalar_tensor_tensor(out=z[:, k % 2, :], in0=res[:, k, n, :], scalar=vec[:, V_FIN + k:V_FIN + k + 1],
                                                 in1=rstd[:, n, :], op0=ALU.mult, op1=ALU.mult).then_inc(zf, 1)


_INS = ['x', 'mem', 'positions', 'mix_norm_w', 'w_in', 'ret_decay_f', 'ret_decay_b', 'ret_gn_w', 'ret_gn_b',
        'conv_w', 'conv_b', 'conv_ln_w', 'conv_ln_b', 'w_out', 'xattn_norm_w', 'mem_norm_w',
        'w_xq', 'w_xkv', 'w_xo', 'mlp_norm_w', 'w_ff1', 'w_ff2', 'final_norm_w']


def kernel(**inputs):
    import concourse.bacc as _bacc
    from concourse.bass_utils import run_bass_kernel_spmd as _run

    nc = _bacc.Bacc("TRN2", target_bir_lowering=False, num_devices=1, dynamic_dma_scratch_size=1024)
    arrays, args = {}, []
    for name in _INS:
        a = np.ascontiguousarray(inputs[name])
        arrays[f"in_{name}"] = a
        args.append(nc.dram_tensor(f"in_{name}", a.shape, mybir.dt.from_np(a.dtype), kind="ExternalInput").ap())
    half = 64
    f = (np.float32(ROPE_THETA) ** (-np.arange(half, dtype=np.float32) / np.float32(half))).astype(np.float32)
    arrays["rope_freq"] = np.concatenate([-f, f]).reshape(2 * half, 1)
    args.append(nc.dram_tensor("rope_freq", (2 * half, 1), F32, kind="ExternalInput").ap())
    out = nc.dram_tensor("out", (1, 2048, 1024), F32, kind="ExternalOutput").ap()
    build(nc, *args, out)
    r = _run(nc, [arrays], core_ids=[0])
    return r.results[0]["out"]
```

```python
from contextlib import ExitStack

import numpy as np
import concourse.bass as bass
from concourse import mybir

F32 = mybir.dt.float32
F32R = mybir.dt.float32r
I32 = mybir.dt.int32
ALU = mybir.AluOpType
ACT = mybir.ActivationFunctionType
AX = mybir.AxisListType

P = 128
ROPE_THETA = 10000.0
EPS = 1e-6
MAGIC = 1.5 * 2.0 ** 23
TWO_PI_PARTS = (6.28125, 0.0019340515136718750, 1.2556440196931362e-06)


def build(nc, x, mem, positions, mix_norm_w, w_in, ret_decay_f, ret_decay_b, ret_gn_w, ret_gn_b,
          conv_w, conv_b, conv_ln_w, conv_ln_b, w_out, xattn_norm_w, mem_norm_w,
          w_xq, w_xkv, w_xo, mlp_norm_w, w_ff1, w_ff2, final_norm_w, rope_freq, out):
    S, D = x.shape[1], x.shape[2]
    M = mem.shape[1]
    KT = D // P
    NC = 512
    NS = S // NC
    HALF = S // 2
    NH = HALF // NC
    R = ret_gn_w.shape[1]
    CW = conv_b.shape[1]
    CT = CW // P
    TAPS = conv_w.shape[1]
    PAD = TAPS // 2
    HEADS = ret_decay_f.shape[1]
    HD = R // HEADS
    CH = S // P
    XH = 4
    XHD = D // XH
    FF = w_ff1.shape[2]
    FG = FF // D
    KSCALE = float(HD) ** -0.5
    XSCALE = float(XHD) ** -0.5
    assert HD == P and CT == HEADS == XH == NS == 4 and KT == 8 and NH == 2 and M == 2 * P and TAPS == 31

    G_MEM = NS * KT
    G_PROJ = G_MEM + KT
    PROJ = [("a", 16, 4), ("V", 0, 1), ("b", 20, 4), ("V", 1, 1), ("q", 0, 4), ("K", 0, 1),
            ("k", 4, 4), ("K", 1, 1), ("v", 8, 4), ("g", 12, 4)]
    GP = sum(b[2] for b in PROJ)
    BP = len(PROJ)
    CUM = [sum(b[2] for b in PROJ[:i]) for i in range(BP + 1)]
    G_HALF0 = G_PROJ + HEADS * GP
    G_XQ = NH * KT
    G_XO = G_XQ + XH * 8
    G_FF = G_XO + NH * KT
    G_PER_HALF = G_FF + FG * 2 * NH * KT
    J_HALF0 = HEADS * BP
    J_XQ, J_XO, J_FF = KT, 2 * KT, 3 * KT
    J_PER_HALF = J_FF + FG * 2 * KT
    N_PER_HALF = KT + FG * KT
    H_XQ, H_XO, H_FF = 16, 32, 48
    H_PER_HALF = H_FF + FG * 16
    Q_PER_HALF = 48

    xT_d = nc.dram_tensor("xT_d", [KT, P, NS, NC], F32).ap()
    proj_d = nc.dram_tensor("proj_d", [16, P, S], F32).ap()
    conv_d = nc.dram_tensor("conv_d", [CT, P, S], F32).ap()
    y_d = nc.dram_tensor("y_d", [KT, P, S], F32).ap()
    k_d = nc.dram_tensor("k_d", [KT, P, 2, M], F32).ap()
    v_d = nc.dram_tensor("v_d", [KT, P, 2, M], F32).ap()

    tab_d = nc.dram_tensor("tab_d", [2, P, S], F32).ap()

    es = ExitStack()
    with es:
        def sem(name):
            return es.enter_context(nc.semaphore(name))

        def alloc(stack, name, shape, dt):
            return stack.enter_context(nc.sbuf_tensor(name, shape, dt))

        wraw = alloc(es, "wraw", [P, 2, KT, P], F32)
        whi = alloc(es, "whi", [P, 2, KT, P], F32R)
        wlo = alloc(es, "wlo", [P, 2, KT, P], F32R)
        ident = alloc(es, "ident", [P, P], F32)
        mean_mat = alloc(es, "mean_mat", [P, P], F32)
        vec = alloc(es, "vec", [P, 60], F32)
        taps = alloc(es, "taps", [P, TAPS * CT], F32)
        eps = alloc(es, "eps", [P, 1], F32)
        sel = alloc(es, "sel", [P, P], F32)
        freq = alloc(es, "freq", [P, 1], F32)
        dec = alloc(es, "dec", [P, 2, HEADS], F32)
        lg = alloc(es, "lg", [P, 6, 2, HEADS], F32)
        zeta = alloc(es, "zeta", [P, 2, HEADS], F32)
        gch = alloc(es, "gch", [P, 2, HEADS], F32)
        io_c = alloc(es, "io_c", [P, 2], F32)
        half_pi = alloc(es, "half_pi", [P, 1], F32)
        junk = alloc(es, "junk", [P, 8], F32)
        V_MIX, V_MEM, V_XN, V_MLP, V_FIN, V_CB, V_LNW, V_LNB, V_GNW, V_GNB = 0, 8, 16, 24, 32, 40, 44, 48, 52, 56
        ps = es.enter_context(nc.psum_tensor("ps", [P, 8, NC], F32))

        with ExitStack() as s1:
            xhi = alloc(s1, "xhi", [P, KT, NS, NC], F32R)
            xlo = alloc(s1, "xlo", [P, KT, NS, NC], F32R)
            rs = alloc(s1, "rs", [P, NS, NC], F32)
            rsm = alloc(s1, "rsm", [P, M], F32)
            mhi = alloc(s1, "mhi", [P, KT, M], F32R)
            mlo = alloc(s1, "mlo", [P, KT, M], F32R)
            with ExitStack() as s0:
                xt = alloc(s0, "xt", [P, 2, 4, D // 2], F32)
                memt = alloc(s0, "memt", [P, 2, D], F32)
                xf = alloc(s0, "xf", [P, 2, NC], F32)
                sq0 = alloc(s0, "sq0", [P, 2, NC], F32)
                ssq0 = alloc(s0, "ssq0", [P, NS, NC], F32)
                ssqm = alloc(s0, "ssqm", [P, M], F32)
                vrow, trow = xf[:, 0, 0:P], xf[:, 1, 0:P]
            kz = alloc(s1, "kz", [P, 4, M], F32)
            khl = alloc(s1, "khl", [P, 4, 2, M], F32R)
            ang = alloc(s1, "ang", [P, NC], F32)
            turns = alloc(s1, "turns", [P, NC], F32)
            pos_i = alloc(s1, "pos_i", [P, NC], I32)
            upad = alloc(s1, "upad", [P, S + 2 * PAD], F32)
            acc = alloc(s1, "acc", [P, S], F32)
            st = alloc(s1, "st", [P, NS, NC], F32)

        with ExitStack() as s2:
            def b2(name, shape=(P, S), dt=F32):
                return alloc(s2, name, list(shape), dt)
            qb_, qsb, vb, gb = (b2(n) for n in ("q_in", "q_sw", "v_in", "g_in"))
            q_rot_b, k_rot_b, q_f, q_b = (b2(n) for n in ("q_rot", "k_rot", "q_f", "q_b"))
            k_tok, v_tok, v_f, v_b = (b2(n, (P, CH, P)) for n in ("k_tok", "v_tok", "v_f", "v_b"))
            sT = b2("sT", (P, CH, P))
            io_t = sT[:, 0:3, :]
            y_b = b2("y_b", (P, NS, NC))
            st_f = b2("st_f", (P, CH, P))
            dmask = b2("dmask", (P, HEADS, P))
            xi_f, xi_b = b2("xi_f", (P, HEADS, P)), b2("xi_b", (P, HEADS, P))
            rec = b2("rec", (P, NC))
            st_b = b2("st_b", (P, CH, P))
            io_s = b2("io_s", (P, 2, P))
            cos_t, sin_t = b2("cos_t"), b2("sin_t")
            kb_, ksb = b2("k_in"), b2("k_sw")
            sg = b2("sg", (P, NS, NC))
            w1 = b2("w1", (P, 2, NC))
            cv = b2("cv", (P, CT, NC))
            cv_w = b2("cv_w", (P, 2, NC))
            cv_r = b2("cv_r", (P, NC))

        with ExitStack() as s3:
            def b3(name, shape, dt=F32):
                return alloc(s3, name, list(shape), dt)
            ahi, alo, bhi, blo = (b3(n, (P, KT, NH, NC), F32R) for n in ("ahi", "alo", "bhi", "blo"))
            res = b3("res", (P, KT, NH, NC))
            kh = b3("kh", (P, 2, 2, M), F32R)
            vh = b3("vh", (P, 2, 2, 2, P), F32R)
            pth, ptl = b3("pth", (P, 2, NC), F32R), b3("ptl", (P, 2, NC), F32R)
            rstd = b3("rstd", (P, NH, NC))
            sq = b3("sq", (P, 2, NC))
            ssq = b3("ssq", (P, NH, NC))
            z = b3("z", (P, 2, NC))
            pr = b3("pr", (P, 2, M))
            mx, nb, sm, ri = (b3(n, (P, 8)) for n in ("mx", "nb", "sm", "ri"))

        phase = sem("phase")
        passed = sem("passed")
        consts = sem("consts")
        vec_in, vec_mm, vec_ok = sem("vec_in"), sem("vec_mm"), sem("vec_ok")
        w_full = [sem("w_full0"), sem("w_full1")]
        w_scaled = sem("w_scaled")
        w_hi = sem("w_hi")
        w_ready = sem("w_ready")
        mm_done = sem("mm_done")
        bank_free = sem("bank_free")
        x_in = [sem("x_in0"), sem("x_in1")]
        mem_in = sem("mem_in")
        hi0, sq0_done, ssq_done = sem("hi0"), sem("sq0_done"), sem("ssq_done")
        xf_done = sem("xf_done")
        xf_st = [sem("xf_st0"), sem("xf_st1")]
        stat_mm, stat_sq, stat_rc = sem("stat_mm"), sem("stat_sq"), sem("stat_rc")
        sig_done, u_done, pad_ok = sem("sig_done"), sem("u_done"), sem("pad_ok")
        conv_step, acc_st = sem("conv_step"), sem("acc_st")
        st_st = [sem(f"st_st{n}") for n in range(NS)]
        kv_hi, kv_lo, vt_mm0 = sem("kv_hi"), sem("kv_lo"), sem("vt_mm0")
        kv_st = [sem(f"kv_st{n}") for n in range(4)]

        G0 = 4

        def released(eng, g):
            eng.wait_ge(bank_free, g + 1 + G0)

        def wait_alone(eng, which, value):
            eng.wait_ge(which, value)
            eng.sem_inc(passed, 1)

        def leave_phase(eng):
            eng.drain().then_inc(phase, 1)

        def end_phase(eng, n):
            leave_phase(eng)
            eng.wait_ge(phase, 5 * n)

        block = es.enter_context(nc.Block())

        l_q, l_qs, l_k, l_ks, l_v, l_g = (sem(n) for n in ("l_q", "l_qs", "l_k", "l_ks", "l_v", "l_g"))
        tab_in, tab, tab_sin, tab_st = (sem(n) for n in ("tab_in", "tab", "tab_sin", "tab_st"))
        dec_in, iot, dec_dve, dec_act = (sem(n) for n in ("dec_in", "iot", "dec_dve", "dec_act"))
        l_tab, dpos, dlin, zero_st = sem("l_tab"), sem("dpos"), sem("dlin"), sem("zero_st")
        p_qs, p_ks, p_qf = sem("p_qs"), sem("p_ks"), sem("p_qf")
        r_q, r_k, q_rot, k_rot = sem("r_q"), sem("r_k"), sem("q_rotd"), sem("k_rotd")
        kt_mm, vt_mm, kt_ev, vt_ev = sem("kt_mm"), sem("vt_mm"), sem("kt_ev"), sem("vt_ev")
        v2 = sem("v2")
        kvf_mm, kvb_mm, f_scan, b_scan = sem("kvf_mm"), sem("kvb_mm"), sem("f_scan"), sem("b_scan")
        s_mm, s_ev, y_mm, y_ev = sem("s_mm"), sem("s_ev"), sem("y_mm"), sem("y_ev")
        me_mm, cen, sqd, va_mm, std = sem("me_mm"), sem("cen"), sem("sqd"), sem("va_mm"), sem("std")
        rc, bc_mm, y_mul, y_aff, y_out = (sem(n) for n in ("rc", "bc_mm", "y_mul", "y_aff", "y_out"))
        sgd, gate, y_st = sem("sgd"), sem("gate"), sem("y_st")
        c_in, c_me, c_cen, c_sq, c_va, c_std, c_rc, c_mul, c_aff, c_sig, c_out, c_st = (
            sem(n) for n in ("c_in", "c_me", "c_cen", "c_sq", "c_va", "c_std", "c_rc", "c_mul", "c_aff", "c_sig", "c_out", "c_st"))
        y_in = [sem(f"y_in{k}") for k in range(KT)]
        r_in = [sem(f"r_in{k}") for k in range(KT)]
        ysp_hi, ysp_lo = sem("ysp_hi"), sem("ysp_lo")
        hi_done, lo_done, z_up = sem("hi_done"), sem("lo_done"), sem("z_up")
        sq_done, ss_zero, ss_done = sem("sq_done"), sem("ss_zero"), sem("ss_done")
        n_mm, n_sq, n_rc = sem("n_mm"), sem("n_sq"), sem("n_rc")
        kv_in = sem("kv_in")
        sc_mm, mx_done, nb_done, p_exp, ri_done, p_nrm = (sem(n) for n in ("sc_mm", "mx_done", "nb_done", "p_exp", "ri_done", "p_nrm"))
        pt_mm, pt_hi, pt_lo, o_hi = (sem(n) for n in ("pt_mm", "pt_hi", "pt_lo", "o_hi"))
        zf, f_tr, f_cp = sem("zf"), sem("f_tr"), sem("f_cp")
        f_st = [sem("f_st0"), sem("f_st1")]

        @block.sync
        def _(sp):
            def load_weights(j, slot, src):
                sp.wait_ge(w_ready, j + 1)
                sp.dma_start(wraw[:, slot, :, :], src.rearrange("(k p) m -> p k m", p=P)).then_inc(w_full[slot], 16)

            xr = x.rearrange("b (n s p) d -> n p (b s) d", s=4, p=P)
            for s in range(2):
                sp.dma_start(xt[:, s, :, :], xr[0, :, :, s * (D // 2):(s + 1) * (D // 2)]).then_inc(x_in[s], 16)
            sp.dma_start(memt[:, :, :], mem.rearrange("b (s p) d -> p (b s) d", p=P)).then_inc(mem_in, 16)
            sp.dma_start(freq[:, :], rope_freq).then_inc(tab_in, 16)
            sp.dma_start(dec[:, 0, :], ret_decay_f[0:1, :].to_broadcast([P, HEADS])).then_inc(dec_in, 16)
            sp.dma_start(dec[:, 1, :], ret_decay_b[0:1, :].to_broadcast([P, HEADS])).then_inc(dec_in, 16)
            with sp.Fori(0, NS) as n:
                for k in range(KT):
                    sp.wait_ge(xf_done, KT * n + k + 1)
                    sp.dma_start(xT_d[k, :, n, :], xf[:, k % 2, :]).then_inc(xf_st[k % 2], 16)
            for s in range(2):
                sp.wait_ge(xf_st[s], 16 * NS * KT // 2)
            leave_phase(sp)
            with sp.Fori(0, HEADS) as c:
                for b, (kind, col, _) in enumerate(PROJ):
                    if kind == "K":
                        src = w_xkv[0, :, bass.ds((2 * c + col) * P, P)]
                    elif kind == "V":
                        src = w_xkv[0, :, bass.ds((KT + 2 * c + col) * P, P)]
                    else:
                        src = w_in[0, :, bass.ds((c + col) * P, P)]
                    load_weights(BP * c + b, b % 2, src)

            H2 = P // 2

            def load_k(h):
                sp.dma_start(kb_[:, :], proj_d[4 + h]).then_inc(l_k, 16)
                sp.dma_start(ksb[0:H2, :], proj_d[4 + h, H2:P]).then_inc(l_ks, 16)
                sp.dma_start(ksb[H2:P, :], proj_d[4 + h, 0:H2]).then_inc(l_ks, 16)

            def load_v(h):
                sp.dma_start(vb[:, :], proj_d[8 + h]).then_inc(l_v, 16)

            def load_q(h):
                sp.dma_start(qb_[:, :], proj_d[h]).then_inc(l_q, 16)
                sp.dma_start(qsb[0:H2, :], proj_d[h, H2:P]).then_inc(l_qs, 16)
                sp.dma_start(qsb[H2:P, :], proj_d[h, 0:H2]).then_inc(l_qs, 16)

            def load_g(h):
                sp.dma_start(gb[:, :], proj_d[12 + h]).then_inc(l_g, 16)

            def load_conv(n):
                sp.dma_start(cv[:, :, :], conv_chunk(conv_d, n)).then_inc(c_in, 16)

            def conv_chunk(d, n):
                return d[:, :, n * NC:(n + 1) * NC].rearrange("c p n -> p c n")

            sp.wait_ge(mm_done, G_PROJ + GP * (HEADS - 1) + CUM[8])
            sp.wait_ge(tab_st, 32 * HEADS)
            sp.dma_start(sin_t[:, :], tab_d[0]).then_inc(l_tab, 16)
            sp.dma_start(cos_t[:, :], tab_d[1]).then_inc(l_tab, 16)
            for n in range(4):
                sp.wait_ge(kv_st[n], 16 * HEADS)
            for n in range(NS):
                sp.wait_ge(st_st[n], 16 * 4)
            load_k(0)
            sp.wait_ge(mm_done, G_HALF0)
            load_v(0)
            load_q(0)
            load_g(0)
            for n in range(NS):
                sp.wait_ge(st_st[n], 16 * 4 * HEADS)
            sp.wait_ge(acc_st, 16 * HEADS)
            leave_phase(sp)
            sp.wait_ge(phase, 5 * 2)
            load_conv(0)
            sp.wait_ge(k_rot, 1)
            load_k(1)
            sp.wait_ge(vt_mm, 4)
            load_v(1)
            sp.wait_ge(q_rot, 1)
            load_q(1)
            for h in range(HEADS):
                if h + 1 < HEADS:
                    sp.wait_ge(gate, 4 * (h + 1))
                    load_g(h + 1)
                if h + 2 < HEADS:
                    sp.wait_ge(k_rot, h + 2)
                    load_k(h + 2)
                    sp.wait_ge(vt_mm, 4 * (h + 2))
                    load_v(h + 2)
                    sp.wait_ge(q_rot, h + 2)
                    load_q(h + 2)
                sp.wait_ge(y_out, 4 * (h + 1))
                sp.dma_start(y_d[h], y_b[:, :, :].rearrange("p a b -> p (a b)")).then_inc(y_st, 16)
                sp.wait_ge(c_out, CT * (h + 1))
                sp.dma_start(conv_chunk(y_d[HEADS:HEADS + CT], h), cv[:, :, :]).then_inc(c_st, 16)
                if h + 1 < HEADS:
                    sp.wait_ge(c_st, 16 * (h + 1))
                    load_conv(h + 1)
            sp.wait_ge(c_st, 16 * HEADS)
            sp.wait_ge(y_st, 16 * HEADS)
            end_phase(sp, 3)

            with sp.Fori(0, 2) as h:
                J = J_HALF0 + J_PER_HALF * h
                with sp.Fori(0, KT // 2) as i:
                    for s in range(2):
                        load_weights(J + 2 * i + s, s, w_out[0, :, bass.ds((2 * i + s) * P, P)])
                with sp.Fori(0, KT // 2) as i:
                    for s in range(2):
                        load_weights(J + J_XQ + 2 * i + s, s, w_xq[0, :, bass.ds((2 * i + s) * P, P)])
                with sp.Fori(0, KT // 2) as i:
                    for s in range(2):
                        load_weights(J + J_XO + 2 * i + s, s, w_xo[0, :, bass.ds((2 * i + s) * P, P)])
                with sp.Fori(0, FG) as g:
                    with sp.Fori(0, KT // 2) as i:
                        for s in range(2):
                            load_weights(J + J_FF + 16 * g + 2 * i + s, s,
                                         w_ff1[0, :, bass.ds((KT * g + 2 * i + s) * P, P)])
                    with sp.Fori(0, KT // 2) as i:
                        for s in range(2):
                            load_weights(J + J_FF + 16 * g + KT + 2 * i + s, s,
                                         w_ff2[0, bass.ds(g * D, D), bass.ds((2 * i + s) * P, P)])

        @block.gpsimd
        def _(pool):
            pool.memset(ident[:, :], 0.0).then_inc(consts, 1)
            pool.memset(mean_mat[:, :], 1.0 / P).then_inc(consts, 1)
            pool.memset(eps[:, :], EPS).then_inc(consts, 1)
            pool.memset(half_pi[:, :], float(np.pi / 2)).then_inc(consts, 1)
            pool.memset(sel[:, :], 0.0).then_inc(consts, 1)
            pool.wait_ge(consts, 5)
            for i in range(4):
                pool.memset(sel[32 * i:32 * i + 1, :], 1.0).then_inc(consts, 1)
            pool.wait_ge(consts, 9)
            pool.affine_select(out=ident[:, :], in_=ident[:, :], compare_op=ALU.not_equal, fill=1.0,
                               base=0, pattern=[[-1, P]], channel_multiplier=1).then_inc(consts, 1)
            pool.memset(junk[:, 2:3], 0.0).then_inc(w_ready, 2)
            pool.wait_ge(vec_ok, 2)
            with pool.Fori(0, NS) as n:
                for k in range(KT):
                    g = KT * n + k
                    released(pool, g)
                    pool.wait_ge(xf_st[k % 2], 16 * (4 * n + k // 2))
                    pool.tensor_tensor(xf[:, k % 2, :], xhi[:, k, n, :], xlo[:, k, n, :], ALU.add).then_inc(xf_done, 1)

            leave_phase(pool)

            def split_weights(j, full, slot, used, norm=None, count=None):
                pool.wait_ge(w_full[slot], full)
                if norm is not None:
                    pool.tensor_tensor(wraw[:, slot, :, :], wraw[:, slot, :, :],
                                       vec[:, norm:norm + KT].unsqueeze(2).to_broadcast([P, KT, P]),
                                       ALU.mult).then_inc(w_scaled, 1)
                    pool.wait_ge(w_scaled, count + 1)
                wait_alone(pool, mm_done, used)
                pool.tensor_scalar(whi[:, slot, :, :], wraw[:, slot, :, :], 1.0, 0.0, ALU.mult, ALU.add).then_inc(w_hi, 1)
                pool.wait_ge(w_hi, j + 1)
                pool.tensor_tensor(wlo[:, slot, :, :], wraw[:, slot, :, :], whi[:, slot, :, :],
                                   ALU.subtract).then_inc(w_ready, 1)

            with pool.Fori(0, HEADS) as c:
                for b, (kind, _, _) in enumerate(PROJ):
                    used = G_PROJ + GP * c + (CUM[b - 1] if b >= 2 else CUM[BP - 1 + b] - GP)
                    split_weights(BP * c + b, 16 * (5 * c + b // 2) + 16, b % 2, used,
                                  V_MEM if kind in "KV" else V_MIX, BP * c + b)
            leave_phase(pool)

            def swapped_k(h):
                pool.wait_ge(l_ks, 32 * h + 32)
                pool.tensor_tensor(ksb[:, :], ksb[:, :], sin_t[:, :], ALU.mult).then_inc(p_ks, 1)

            def swapped(h):
                swapped_k(h)
                pool.wait_ge(l_qs, 32 * h + 32)
                pool.tensor_tensor(qsb[:, :], qsb[:, :], sin_t[:, :], ALU.mult).then_inc(p_qs, 1)

            def decayed_q(h):
                pool.wait_ge(q_rot, h + 1)
                if not isinstance(h, int):
                    pool.wait_ge(y_mm, 4 * h)
                for dst, xi in ((q_f, xi_f), (q_b, xi_b)):
                    pool.tensor_tensor(dst[:, :].rearrange("p (c q) -> p c q", q=P),
                                       q_rot_b[:, :].rearrange("p (c q) -> p c q", q=P),
                                       xi[:, bass.ds(h, 1), :].to_broadcast([P, CH, P]), ALU.mult).then_inc(p_qf, 1)

            def silu(h):
                for i in range(4):
                    pool.wait_ge(sgd, 4 * h + i + 1)
                    pool.tensor_tensor(sg[:, i, :], gb[:, i * NC:(i + 1) * NC], sg[:, i, :], ALU.mult).then_inc(gate, 1)

            def gated(h):
                for i in range(4):
                    pool.wait_ge(gate, 4 * h + i + 1)
                    pool.wait_ge(y_aff, 4 * h + i + 1)
                    pool.tensor_tensor(y_b[:, i, :], y_b[:, i, :], sg[:, i, :], ALU.mult).then_inc(y_out, 1)
                for c in range(CT):
                    pool.wait_ge(c_sig, CT * h + c + 1)
                    pool.tensor_tensor(cv[:, c, :], cv[:, c, :], cv_w[:, c % 2, :], ALU.mult).then_inc(c_out, 1)

            pool.wait_ge(l_tab, 32)
            swapped_k(0)
            pool.wait_ge(mm_done, G_HALF0)
            pool.wait_ge(bank_free, G_HALF0 + G0)
            pool.iota(io_t[:, 0, :], pattern=[[1, P]], base=0, channel_multiplier=-1,
                      allow_small_or_imprecise_dtypes=True).then_inc(iot, 1)
            pool.iota(io_s[:, 0, :], pattern=[[1, P]], base=1, channel_multiplier=0,
                      allow_small_or_imprecise_dtypes=True).then_inc(iot, 1)
            pool.iota(io_s[:, 1, :], pattern=[[-1, P]], base=P, channel_multiplier=0,
                      allow_small_or_imprecise_dtypes=True).then_inc(iot, 1)
            pool.iota(io_c[:, 0:1], pattern=[[1, 1]], base=P - 1, channel_multiplier=-1,
                      allow_small_or_imprecise_dtypes=True).then_inc(iot, 1)
            pool.iota(io_c[:, 1:2], pattern=[[1, 1]], base=0, channel_multiplier=1,
                      allow_small_or_imprecise_dtypes=True).then_inc(iot, 1)
            pool.wait_ge(l_qs, 32)
            pool.tensor_tensor(qsb[:, :], qsb[:, :], sin_t[:, :], ALU.mult).then_inc(p_qs, 1)
            pool.wait_ge(dec_act, 2 + 4 * HEADS)
            decayed_q(0)
            silu(0)
            with pool.Fori(0, HEADS - 1) as h:
                swapped(h + 1)
                decayed_q(h + 1)
                gated(h)
                silu(h + 1)
            gated(HEADS - 1)
            end_phase(pool, 3)

            with pool.Fori(0, 2) as h:
                J = J_HALF0 + J_PER_HALF * h
                G = G_HALF0 + G_PER_HALF * h
                N = J_HALF0 + N_PER_HALF * h
                L = 16 * (J_HALF0 // 2) + 16 * (J_PER_HALF // 2) * h + 16
                with pool.Fori(0, KT // 2) as i:
                    for s in range(2):
                        split_weights(J + 2 * i + s, L + 16 * i, s, G + 4 * i + 2 * s - 2)
                for hh in range(XH):
                    for r in range(2):
                        used = G + (2 * (KT - 2 + r) + 2 if hh == 0 else G_XQ + 8 * (hh - 1) + 2 * r + 2)
                        split_weights(J + J_XQ + 2 * hh + r, L + 16 * (4 + hh), r, used, V_XN, N + 2 * hh + r)
                for s in range(2):
                    split_weights(J + J_XO + s, L + 16 * 8, s, G + G_XQ + 24 + 2 * s + 2)
                with pool.Fori(1, KT // 2) as i:
                    for s in range(2):
                        split_weights(J + J_XO + 2 * i + s, L + 16 * 8 + 16 * i, s, G + G_XO + 4 * i + 2 * s - 2)
                with pool.Fori(0, FG) as g:
                    with pool.Fori(0, KT // 2) as i:
                        for s in range(2):
                            split_weights(J + J_FF + 16 * g + 2 * i + s, L + 16 * 12 + 128 * g + 16 * i, s,
                                          G + G_FF + 32 * g + 4 * i + 2 * s - 2, V_MLP, N + KT + KT * g + 2 * i + s)
                    with pool.Fori(0, KT // 2) as i:
                        for s in range(2):
                            split_weights(J + J_FF + 16 * g + KT + 2 * i + s, L + 16 * 12 + 128 * g + 64 + 16 * i, s,
                                          G + G_FF + 32 * g + 16 + 4 * i + 2 * s - 2)

        @block.tensor
        def _(pe):
            def gemm(bank, slot, hi, lo, n, before=None):
                o = ps[:, bank, 0:n]
                for k in range(KT):
                    if before is not None:
                        before(k)
                    nc.tensor.matmul(o, whi[:, slot, k, :], hi(k), start=(k == 0), stop=False)
                    nc.tensor.matmul(o, whi[:, slot, k, :], lo(k), start=False, stop=False)
                    last = nc.tensor.matmul(o, wlo[:, slot, k, :], hi(k), start=False, stop=(k == KT - 1))
                last.then_inc(mm_done, 1)

            def bank_ready(g):
                pe.wait_ge(bank_free, g + 1)

            pe.wait_ge(consts, 10)
            pe.wait_ge(vec_in, 16 * 11)
            pe.transpose(ps[:, 4, 0:60], vrow[0:60, :], ident[0:60, 0:60]).then_inc(vec_mm, 1)
            pe.transpose(ps[:, 5, 0:TAPS * CT], trow[0:TAPS * CT, :],
                         ident[0:TAPS * CT, 0:TAPS * CT]).then_inc(vec_mm, 1)
            with pe.Fori(0, NS) as n:
                for k in range(KT):
                    if k % 4 == 0:
                        pe.wait_ge(x_in[k // 4], 16 * n + 16)
                    bank_ready(KT * n + k)
                    for t in range(4):
                        last = pe.transpose(ps[:, k % 4, t * P:(t + 1) * P],
                                            xt[:, k // 4, t, (k % 4) * P:(k % 4 + 1) * P], ident[:, :])
                    last.then_inc(mm_done, 1)
            pe.wait_ge(mem_in, 16)
            for k in range(KT):
                bank_ready(G_MEM + k)
                for t in range(2):
                    last = pe.transpose(ps[:, k % 4, t * P:(t + 1) * P], memt[:, t, k * P:(k + 1) * P], ident[:, :])
                last.then_inc(mm_done, 1)
            pe.wait_ge(vec_ok, 2)
            for n in range(NS):
                pe.wait_ge(ssq_done, 2 + KT * (n + 1))
                pe.matmul(ps[:, 4 + n, :], mean_mat[:, :], ssq0[:, n, :], start=True, stop=True).then_inc(stat_mm, 1)
            pe.wait_ge(ssq_done, 2 + KT * (NS + 1))
            pe.wait_ge(stat_sq, 1)
            pe.matmul(ps[:, 4, 0:M], mean_mat[:, :], ssqm[:, :], start=True, stop=True).then_inc(stat_mm, 1)
            released(pe, G_PROJ - 1)
            leave_phase(pe)
            with pe.Fori(0, HEADS) as c:
                for b, (kind, col, groups) in enumerate(PROJ):
                    pe.wait_ge(w_ready, BP * c + b + 3)
                    for n in range(groups):
                        g = CUM[b] + n
                        bank_ready(G_PROJ + GP * c + g)
                        if kind in "KV":
                            gemm(g % 4, b % 2, lambda k: mhi[:, k, :], lambda k: mlo[:, k, :], M)
                        else:
                            gemm(g % 4, b % 2, lambda k, n=n: xhi[:, k, n, :], lambda k, n=n: xlo[:, k, n, :], NC)
                    if b >= 2 and PROJ[b - 1][0] == "V":
                        r = PROJ[b - 1][1]
                        released(pe, G_PROJ + GP * c + CUM[b - 1])
                        pe.wait_ge(kv_lo, 4 * c)
                        for t in range(2):
                            last = pe.transpose(ps[:, 6 + r, t * P:(t + 1) * P], kz[:, r, t * P:(t + 1) * P], ident[:, :])
                        last.then_inc(vt_mm0, 1)
            leave_phase(pe)

            def key_tokens(h):
                pe.wait_ge(k_rot, h + 1)
                for i in range(4):
                    for c in range(4):
                        cc = 4 * i + c
                        last = pe.transpose(ps[:, 4 + i, c * P:(c + 1) * P], k_rot_b[:, cc * P:(cc + 1) * P], ident[:, :])
                    last.then_inc(kt_mm, 1)

            def value_tokens(h):
                pe.wait_ge(l_v, 16 * h + 16)
                for i in range(4):
                    pe.wait_ge(kt_ev, 4 * h + i + 1)
                    for c in range(4):
                        cc = 4 * i + c
                        last = pe.transpose(ps[:, 4 + i, c * P:(c + 1) * P], vb[:, cc * P:(cc + 1) * P], ident[:, :])
                    last.then_inc(vt_mm, 1)

            def core(h):
                pe.wait_ge(v2, 2 * h + 1)
                if not isinstance(h, int) or h:
                    pe.wait_ge(std, h)
                    pe.wait_ge(c_std, h)
                for i in range(4):
                    for c in range(4):
                        cc = 4 * i + c
                        last = pe.matmul(ps[:, i, c * P:(c + 1) * P], k_tok[:, cc, :], v_f[:, cc, :], start=True, stop=True)
                    last.then_inc(kvf_mm, 1)
                pe.wait_ge(v2, 2 * h + 2)
                if not isinstance(h, int) or h:
                    pe.wait_ge(y_mul, 4 * h)
                for i in reversed(range(4)):
                    for c in range(4):
                        cc = 4 * i + c
                        last = pe.matmul(ps[:, 4 + i, c * P:(c + 1) * P], k_tok[:, cc, :], v_b[:, cc, :], start=True, stop=True)
                    last.then_inc(kvb_mm, 1)
                pe.wait_ge(q_rot, h + 1)
                pe.wait_ge(f_scan, 15 * h + 15)
                for i in range(4):
                    for c in range(4):
                        cc = 4 * i + c
                        last = pe.matmul(ps[:, i, c * P:(c + 1) * P], k_rot_b[:, cc * P:(cc + 1) * P],
                                         q_rot_b[:, cc * P:(cc + 1) * P], start=True, stop=True)
                    last.then_inc(s_mm, 1)
                pe.wait_ge(b_scan, 15 * h + 15)
                pe.wait_ge(p_qf, 2 * h + 2)
                for i in range(4):
                    pe.wait_ge(s_ev, 4 * h + i + 1)
                    for c in range(4):
                        cc = 4 * i + c
                        o = ps[:, 4 + i, c * P:(c + 1) * P]
                        pe.matmul(o, v_tok[:, cc, :], sT[:, cc, :], start=True, stop=False)
                        pe.matmul(o, st_f[:, cc, :], q_f[:, cc * P:(cc + 1) * P], start=False, stop=False)
                        last = pe.matmul(o, st_b[:, cc, :], q_b[:, cc * P:(cc + 1) * P], start=False, stop=True)
                    last.then_inc(y_mm, 1)
                for i in range(4):
                    pe.wait_ge(y_ev, 4 * h + i + 1)
                    pe.matmul(ps[:, i, :], mean_mat[:, :], y_b[:, i, :], start=True, stop=True).then_inc(me_mm, 1)

            def norms(h):
                pe.wait_ge(c_in, 16 * h + 16)
                pe.wait_ge(cen, 4 * h + 4)
                for c in range(CT):
                    last = pe.matmul(ps[:, 1, :], mean_mat[:, :], cv[:, c, :], start=(c == 0), stop=(c == CT - 1))
                last.then_inc(c_me, 1)
                for i in range(4):
                    pe.wait_ge(sqd, 4 * h + i + 1)
                    pe.matmul(ps[32 * i:32 * i + 32, 0, :], mean_mat[:, 0:32], w1[:, i % 2, :], start=True, stop=True).then_inc(va_mm, 1)
                for c in range(CT):
                    pe.wait_ge(c_sq, CT * h + c + 1)
                    pe.matmul(ps[:, 2, :], mean_mat[:, :], cv_w[:, c % 2, :], start=(c == 0), stop=(c == CT - 1)).then_inc(c_va, 1)

            def spread(h):
                pe.wait_ge(rc, h + 1)
                for i in range(4):
                    pe.matmul(ps[:, 4 + i, :], sel[32 * i:32 * i + 32, :], rec[32 * i:32 * i + 32, :], start=True, stop=True).then_inc(bc_mm, 1)

            key_tokens(0)
            value_tokens(0)
            with pe.Fori(0, HEADS - 1) as h:
                core(h)
                key_tokens(h + 1)
                value_tokens(h + 1)
                norms(h)
                pe.wait_ge(vt_ev, 4 * h + 8)
                spread(h)
            core(HEADS - 1)
            norms(HEADS - 1)
            spread(HEADS - 1)
            end_phase(pe, 3)

            def stats(h, count, first):
                pe.wait_ge(ss_done, 2 + count)
                if first is not None:
                    first()
                for n in range(NH):
                    pe.matmul(ps[:, 4 + n, :], mean_mat[:, :], ssq[:, n, :], start=True, stop=True).then_inc(n_mm, 1)

            with pe.Fori(0, 2) as h:
                G = G_HALF0 + G_PER_HALF * h
                J = J_HALF0 + J_PER_HALF * h
                H = H_PER_HALF * h

                def product(i, g, j, hi, lo, ready):
                    for s in range(2):
                        pe.wait_ge(w_ready, j + 2 * i + s + 3)
                        for n in range(NH):
                            bank_ready(g + 4 * i + 2 * s + n)
                            gemm(2 * s + n, s, lambda k: hi[:, k, n, :], lambda k: lo[:, k, n, :], NC,
                                 ready if s == 0 and n == 0 else None)

                wait_alone(pe, f_cp, 16 * h)
                with pe.Fori(0, KT // 2) as i:
                    product(i, G, J, ahi, alo, lambda k: pe.wait_ge(ysp_lo, KT * h + k + 1))
                stats(h, Q_PER_HALF * h + 16, None)
                with pe.Fori(0, XH) as hh:
                    for r in range(2):
                        pe.wait_ge(w_ready, J + J_XQ + 2 * hh + r + 3)
                        for n in range(NH):
                            bank_ready(G + G_XQ + 8 * hh + 2 * r + n)
                            gemm(2 * r + n, r, lambda k: bhi[:, k, n, :], lambda k: blo[:, k, n, :], NC,
                                 (lambda k: pe.wait_ge(lo_done, H + 2 * k + 2)) if r == n == 0 else None)
                    T = 32 * h + 8 * hh
                    pe.wait_ge(kv_in, 128 * h + 32 * hh + 32)

                    def scores(t):
                        n, tt = t // 4, t % 4
                        pe.wait_ge(lo_done, H + H_XQ + 4 * hh + 3 + n)
                        pe.wait_ge(p_exp, T + t + 1)
                        o = ps[:, 4 + t % 2, 0:M]
                        for r in range(2):
                            a, b = (q[:, 6 + r, n, tt * P:(tt + 1) * P] for q in (ahi, alo))
                            pe.matmul(o, a, kh[:, r, 0, :], start=(r == 0), stop=False)
                            pe.matmul(o, a, kh[:, r, 1, :], start=False, stop=False)
                            last = pe.matmul(o, b, kh[:, r, 0, :], start=False, stop=(r == 1))
                        last.then_inc(sc_mm, 1)

                    pe.wait_ge(n_sq, 6 * h + 2)
                    scores(0)
                    for t in range(8):
                        if t + 1 < 8:
                            scores(t + 1)
                        pe.wait_ge(p_nrm, T + t + 1)
                        pe.wait_ge(pt_lo, T + t + 1)
                        for m in range(2):
                            last = pe.transpose(ps[:, 6 + t % 2, m * P:(m + 1) * P], pr[:, t % 2, m * P:(m + 1) * P], ident[:, :])
                        last.then_inc(pt_mm, 1)
                        if t % 4 == 3:
                            n = t // 4
                            pe.wait_ge(pt_lo, T + t + 3)
                            for d in range(2):
                                bank_ready(G + G_XQ + 8 * hh + 4 + 2 * n + d)
                                o = ps[:, 2 * n + d, :]
                                for m in range(2):
                                    pe.matmul(o, vh[:, d, 0, m, :], pth[:, m, :], start=(m == 0), stop=False)
                                    pe.matmul(o, vh[:, d, 0, m, :], ptl[:, m, :], start=False, stop=False)
                                    last = pe.matmul(o, vh[:, d, 1, m, :], pth[:, m, :], start=False, stop=(m == 1))
                                last.then_inc(mm_done, 1)
                with pe.Fori(0, KT // 2) as i:
                    product(i, G + G_XO, J + J_XO, ahi, alo, lambda k: released(pe, G + G_XQ + 8 * (k // 2) + 6 + k % 2))
                stats(h, Q_PER_HALF * h + 32, lambda: pe.wait_ge(p_exp, 32 * h + 32 + 2))
                with pe.Fori(0, FG) as g:
                    with pe.Fori(0, KT // 2) as i:
                        product(i, G + G_FF + 32 * g, J + J_FF + 16 * g, bhi, blo,
                                lambda k: pe.wait_ge(lo_done, H + H_XO + 2 * k + 2))
                    with pe.Fori(0, KT // 2) as i:
                        product(i, G + G_FF + 32 * g + 16, J + J_FF + 16 * g + KT, ahi, alo,
                                lambda k: pe.wait_ge(lo_done, H + H_FF + 16 * g + 2 * k + 2))
                stats(h, Q_PER_HALF * h + 48, lambda: pe.wait_ge(n_sq, 6 * h + 4))
                pe.wait_ge(n_sq, 6 * h + 6)
                released(pe, G + G_PER_HALF - 1)
                for n in range(NH):
                    pe.wait_ge(f_cp, 16 * h + 8 * n)
                    for k in range(KT):
                        pe.wait_ge(zf, 16 * h + 8 * n + k + 1)
                        for t in range(4):
                            last = pe.transpose(ps[:, 2 * t + k // 4, (k % 4) * P:(k % 4 + 1) * P],
                                                z[:, k % 2, t * P:(t + 1) * P], ident[:, :])
                        last.then_inc(f_tr, 1)

        @block.scalar
        def _(act):
            at = 0
            for v in (mix_norm_w, mem_norm_w, xattn_norm_w, mlp_norm_w, final_norm_w.rearrange("(a n) -> a n", a=1),
                      conv_b, conv_ln_w, conv_ln_b, ret_gn_w, ret_gn_b):
                n = v.shape[1] // P
                act.dma_start(vrow[at:at + n, :], v.rearrange("a (k p) -> (a k) p", p=P)).then_inc(vec_in, 16)
                at += n
            act.dma_start(trow[0:TAPS * CT, :], conv_w.rearrange("a t b (c p) -> (a t b c) p", p=P)).then_inc(vec_in, 16)
            act.wait_ge(consts, 10)
            act.activation(junk[:, 0:1], eps[:, :], ACT.Copy).then_inc(p_exp, 2)
            act.wait_ge(dec_dve, 1)
            act.activation(lg[:, 1], lg[:, 0], ACT.Exp, scale=-1.0).then_inc(dec_act, 1)
            act.wait_ge(dec_dve, 2)
            act.activation(lg[:, 3], lg[:, 2], ACT.Ln).then_inc(dec_act, 1)
            act.wait_ge(dec_dve, 9)
            xr = x.rearrange("b (n s p) d -> n p (b s) d", s=4, p=P)
            for n in range(NS):
                for k in range(KT):
                    g = KT * n + k
                    act.wait_ge(mm_done, g + 1)
                    if k % 4 == 3 and n + 1 < NS:
                        s = k // 4
                        act.dma_start(xt[:, s, :, :], xr[n + 1, :, :, s * (D // 2):(s + 1) * (D // 2)]).then_inc(x_in[s], 16)
                    act.activation(xhi[:, k, n, :], ps[:, k % 4, :], ACT.Copy).then_inc(hi0, 1)
                    act.wait_ge(ssq_done, g + 1)
                    act.activation(sq0[:, k % 2, :], ps[:, k % 4, :], ACT.Square).then_inc(sq0_done, 1)
            for k in range(KT):
                g = G_MEM + k
                act.wait_ge(mm_done, g + 1)
                act.activation(mhi[:, k, :], ps[:, k % 4, 0:M], ACT.Copy).then_inc(hi0, 1)
                act.wait_ge(ssq_done, g + 1)
                act.activation(sq0[:, k % 2, 0:M], ps[:, k % 4, 0:M], ACT.Square).then_inc(sq0_done, 1)
            for n in range(NS):
                act.wait_ge(stat_mm, n + 1)
                act.activation(rs[:, n, :], ps[:, 4 + n, :], ACT.Sqrt, bias=eps[:, :], scale=P / D).then_inc(stat_sq, 1)
            act.wait_ge(stat_mm, NS + 1)
            act.activation(rsm[:, :], ps[:, 4, 0:M], ACT.Sqrt, bias=eps[:, :], scale=P / D).then_inc(stat_sq, 1)
            end_phase(act, 1)

            with act.Fori(0, HEADS) as c:
                G = G_PROJ + GP * c

                def last_of(b):
                    released(act, G + CUM[b + 1] - 1)

                def store_proj(b, tile):
                    for n in range(NS):
                        released(act, G + CUM[b] + n)
                        act.dma_start(proj_d[tile + c, :, n * NC:(n + 1) * NC], st[:, n, :]).then_inc(st_st[n], 16)

                def high(b, slot):
                    act.wait_ge(kv_st[slot], 16 * c)
                    if slot < 2:
                        act.wait_ge(vt_mm0, 2 * c + slot + 1)
                        act.activation(khl[:, slot, 0, :], ps[:, 6 + slot, 0:M], ACT.Copy).then_inc(kv_hi, 1)
                    else:
                        last_of(b)
                        act.activation(khl[:, slot, 0, :], kz[:, slot, :], ACT.Copy).then_inc(kv_hi, 1)

                def store_kv(slot, order):
                    act.wait_ge(kv_lo, 4 * c + order + 1)
                    dst = (v_d if slot < 2 else k_d)[2 * c + slot % 2]
                    act.dma_start(dst, khl[:, slot, :, :].bitcast(F32)).then_inc(kv_st[slot], 16)

                act.wait_ge(tab_st, 32 * c)
                act.dma_start(pos_i[:, :], positions[0:1, bass.ds(c * NC, NC)].to_broadcast([P, NC])).then_inc(tab_in, 16)
                act.wait_ge(tab, 9 * c + 9)
                act.activation(ang[:, :], ang[:, :], ACT.Sin).then_inc(tab_sin, 1)
                act.activation(turns[:, :], turns[:, :], ACT.Sin, bias=half_pi[:, :], scale=-1.0).then_inc(tab_sin, 1)
                act.wait_ge(tab_sin, 2 * c + 2)
                act.dma_start(tab_d[0, :, bass.ds(c * NC, NC)], ang[:, :]).then_inc(tab_st, 16)
                act.dma_start(tab_d[1, :, bass.ds(c * NC, NC)], turns[:, :]).then_inc(tab_st, 16)
                for n in range(NS):
                    released(act, G + CUM[2] + n)
                    act.activation(st[:, n, :], st[:, n, :], ACT.Sigmoid).then_inc(sig_done, 1)
                high(1, 0)
                store_kv(0, 0)
                store_proj(4, 0)
                high(3, 1)
                store_kv(1, 1)
                high(5, 2)
                store_kv(2, 2)
                store_proj(6, 4)
                high(7, 3)
                store_kv(3, 3)
                store_proj(8, 8)
                store_proj(9, 12)
                act.wait_ge(conv_step, TAPS * c + TAPS)
                act.dma_start(conv_d[c], acc[:, :]).then_inc(acc_st, 16)
            leave_phase(act)

            act.wait_ge(iot, 5)
            for h in range(HEADS):
                for d, xi in ((0, xi_f), (1, xi_b)):
                    s = lg[:, 5, d, h:h + 1]
                    act.activation(xi[:, h, :], io_s[:, d, :], ACT.Exp, scale=s).then_inc(dec_act, 1)
                    act.activation(zeta[:, d, h:h + 1], io_c[:, d:d + 1], ACT.Exp, scale=s).then_inc(dec_act, 1)
            act.activation(gch[:, :, :], lg[:, 5], ACT.Exp, scale=float(P)).then_inc(dec_act, 1)

            def key_evac(h):
                act.wait_ge(kvb_mm, 4 * h)
                for i in range(4):
                    act.wait_ge(kt_mm, 4 * h + i + 1)
                    act.activation(k_tok[:, 4 * i:4 * i + 4, :].rearrange("p c d -> p (c d)"), ps[:, 4 + i, :], ACT.Copy).then_inc(kt_ev, 1)

            def value_evac(h):
                act.wait_ge(y_mm, 4 * h)
                for i in range(4):
                    act.wait_ge(vt_mm, 4 * h + i + 1)
                    act.activation(v_tok[:, 4 * i:4 * i + 4, :].rearrange("p c d -> p (c d)"), ps[:, 4 + i, :], ACT.Copy).then_inc(vt_ev, 1)

            def gates(h):
                act.wait_ge(l_g, 16 * h + 16)
                act.wait_ge(y_out, 4 * h)
                for i in range(4):
                    act.activation(sg[:, i, :], gb[:, i * NC:(i + 1) * NC], ACT.Sigmoid).then_inc(sgd, 1)
                act.wait_ge(y_st, 16 * h)
                for i in range(4):
                    act.wait_ge(y_mm, 4 * h + i + 1)
                    act.activation(y_b[:, i, :], ps[:, 4 + i, :], ACT.Copy).then_inc(y_ev, 1)

            def spreads(h):
                for i in range(4):
                    act.wait_ge(cen, 4 * h + i + 1)
                    if i >= 2:
                        act.wait_ge(va_mm, 4 * h + i - 1)
                    act.activation(w1[:, i % 2, :], y_b[:, i, :], ACT.Square).then_inc(sqd, 1)
                for c in range(CT):
                    act.wait_ge(c_cen, CT * h + c + 1)
                    if c >= 2:
                        act.wait_ge(c_va, CT * h + c - 1)
                    act.activation(cv_w[:, c % 2, :], cv[:, c, :], ACT.Square).then_inc(c_sq, 1)
                    if c == 1:
                        act.wait_ge(va_mm, 4 * h + 4)
                        act.activation(rec[:, :], ps[:, 0, :], ACT.Sqrt, bias=eps[:, :]).then_inc(std, 1)
                act.wait_ge(c_va, CT * h + CT)
                act.activation(cv_r[:, :], ps[:, 2, :], ACT.Sqrt, bias=eps[:, :], scale=P / CW).then_inc(c_std, 1)

            def conv_gates(h):
                for c in range(CT):
                    act.wait_ge(c_aff, CT * h + c + 1)
                    if c >= 2:
                        act.wait_ge(c_out, CT * h + c - 1)
                    act.activation(cv_w[:, c % 2, :], cv[:, c, :], ACT.Sigmoid).then_inc(c_sig, 1)

            for i in range(4):
                act.wait_ge(kt_mm, i + 1)
                act.activation(k_tok[:, 4 * i:4 * i + 4, :].rearrange("p c d -> p (c d)"), ps[:, 4 + i, :], ACT.Copy).then_inc(kt_ev, 1)
            for i in range(4):
                act.wait_ge(vt_mm, i + 1)
                act.activation(v_tok[:, 4 * i:4 * i + 4, :].rearrange("p c d -> p (c d)"), ps[:, 4 + i, :], ACT.Copy).then_inc(vt_ev, 1)
            act.wait_ge(dec_dve, 10 + HEADS)
            act.activation(dmask[:, :, :], dmask[:, :, :], ACT.Exp).then_inc(dec_act, 1)
            act.wait_ge(phase, 5 * 2)
            with act.Fori(0, HEADS - 1) as h:
                gates(h)
                key_evac(h + 1)
                value_evac(h + 1)
                spreads(h)
                conv_gates(h)
            gates(HEADS - 1)
            spreads(HEADS - 1)
            conv_gates(HEADS - 1)
            end_phase(act, 3)

            with act.Fori(0, 2) as h:
                G = G_HALF0 + G_PER_HALF * h
                H = H_PER_HALF * h
                Q = Q_PER_HALF * h
                act.wait_ge(zf, 16 * h)
                act.wait_ge(mm_done, G)
                for k in range(KT):
                    act.dma_start(res[:, k, :, :].rearrange("p a b -> p (a b)"),
                                  y_d[k, :, bass.ds(h * HALF, HALF)]).then_inc(y_in[k], 16)
                for k in range(KT):
                    act.wait_ge(y_in[k], 16 * h + 16)
                    act.activation(ahi[:, k, :, :], res[:, k, :, :], ACT.Copy).then_inc(ysp_hi, 1)
                    if k:
                        act.wait_ge(ysp_lo, KT * h + k)
                        act.dma_start(res[:, k - 1, :, :], xT_d[k - 1, :, bass.ds(2 * h, 2), :]).then_inc(r_in[k - 1], 16)
                act.wait_ge(ysp_lo, KT * h + KT)
                act.dma_start(res[:, KT - 1, :, :], xT_d[KT - 1, :, bass.ds(2 * h, 2), :]).then_inc(r_in[KT - 1], 16)
                for s in range(2):
                    act.wait_ge(f_st[s], 128 * h)

                def residual(i, u, hb, qb):
                    for s in range(2):
                        for n in range(NH):
                            e = 4 * i + 2 * s + n
                            released(act, u + 4 * i + 2 * s + n)
                            act.activation(bhi[:, 2 * i + s, n, :], res[:, 2 * i + s, n, :], ACT.Copy).then_inc(hi_done, 1)
                            wait_alone(act, ss_done, qb + e + 1)
                            act.activation(sq[:, n, :], res[:, 2 * i + s, n, :], ACT.Square).then_inc(sq_done, 1)

                def norm_sqrt(count):
                    for n in range(NH):
                        act.wait_ge(n_mm, 6 * h + count + n + 1)
                        act.activation(rstd[:, n, :], ps[:, 4 + n, :], ACT.Sqrt, bias=eps[:, :], scale=P / D).then_inc(n_sq, 1)

                with act.Fori(0, KT // 2) as i:
                    residual(i, G, H, Q)
                norm_sqrt(0)
                with act.Fori(0, XH) as hh:
                    T = 32 * h + 8 * hh
                    act.wait_ge(mm_done, G + G_XQ + 8 * hh)
                    act.dma_start(kh[:, :, :, :].bitcast(F32), k_d[bass.ds(2 * hh, 2)].rearrange("r p a m -> p r a m")).then_inc(kv_in, 16)
                    act.dma_start(vh[:, :, :, :, :].rearrange("p d a m k -> p d a (m k)").bitcast(F32),
                                  v_d[bass.ds(2 * hh, 2)].rearrange("r p a m -> p r a m")).then_inc(kv_in, 16)
                    for r in range(2):
                        for n in range(NH):
                            e = 4 * hh + 2 * r + n
                            released(act, G + G_XQ + 8 * hh + 2 * r + n)
                            act.activation(ahi[:, 6 + r, n, :], z[:, n, :], ACT.Copy).then_inc(hi_done, 1)

                    def o_high(n):
                        for d in range(2):
                            act.wait_ge(mm_done, G + G_XQ + 8 * hh + 4 + 2 * n + d + 1)
                            act.activation(ahi[:, 2 * hh + d, n, :], ps[:, 2 * n + d, :], ACT.Copy).then_inc(o_hi, 1)

                    for t in range(9):
                        if t < 8:
                            act.wait_ge(nb_done, T + t + 1)
                            act.activation(pr[:, t % 2, :], ps[:, 4 + t % 2, 0:M], ACT.Exp, bias=nb[:, t:t + 1],
                                           scale=XSCALE, accum_out=sm[:, t:t + 1]).then_inc(p_exp, 1)
                        if t >= 1:
                            u = t - 1
                            act.wait_ge(pt_mm, T + u + 1)
                            act.activation(pth[:, :, (u % 4) * P:(u % 4 + 1) * P],
                                           ps[:, 6 + u % 2, 0:M].rearrange("p (m k) -> p m k", m=2), ACT.Copy).then_inc(pt_hi, 1)
                        if t == 5:
                            o_high(0)
                        if t == 8:
                            o_high(1)
                with act.Fori(0, KT // 2) as i:
                    residual(i, G + G_XO, H + H_XO, Q + 16)
                norm_sqrt(2)
                with act.Fori(0, FG) as g:
                    with act.Fori(0, KT // 2) as i:
                        for s in range(2):
                            for n in range(NH):
                                e = 4 * i + 2 * s + n
                                act.wait_ge(z_up, 64 * h + 16 * g + e + 1)
                                act.activation(ahi[:, 2 * i + s, n, :], z[:, n, :], ACT.Copy).then_inc(hi_done, 1)
                for k in range(KT):
                    for n in range(NH):
                        e = 2 * k + n
                        if k == 0:
                            released(act, G + G_PER_HALF - 1)
                        act.wait_ge(ss_done, Q + 32 + e + 1)
                        act.activation(sq[:, n, :], res[:, k, n, :], ACT.Square).then_inc(sq_done, 1)
                norm_sqrt(4)
                for n in range(NH):
                    act.wait_ge(f_tr, 16 * h + 8 * n + 8)
                    for b in range(8):
                        act.wait_ge(f_st[b % 2], 128 * h + 64 * n + 16 * (b // 2))
                        if n == b == 0:
                            act.wait_ge(ss_done, Q + 48 + 2)
                        act.activation(sq[:, b % 2, :], ps[:, b, :], ACT.Copy).then_inc(f_cp, 1)
                        act.wait_ge(f_cp, 16 * h + 8 * n + b + 1)
                        act.dma_start(out[0, bass.ds(h * HALF + n * NC + (b // 2) * P, P), (b % 2) * NC:(b % 2 + 1) * NC],
                                      sq[:, b % 2, :]).then_inc(f_st[b % 2], 16)
            for s in range(2):
                act.wait_ge(f_st[s], 256)

        @block.vector
        def _(dve):
            dve.memset(ssq0[:, :, :], 0.0).then_inc(ssq_done, 1)
            dve.memset(ssqm[:, :], 0.0).then_inc(ssq_done, 1)
            dve.memset(junk[:, 3:4], 0.0).then_inc(bank_free, G0)
            def step(ins, n):
                ins.then_inc(dec_dve, 1)
                dve.wait_ge(dec_dve, n)
            dve.wait_ge(dec_in, 32)
            step(dve.scalar_tensor_tensor(out=lg[:, 0], in0=dec[:, :, :], scalar=-1.0, in1=dec[:, :, :],
                                          op0=ALU.mult, op1=ALU.max), 1)
            dve.wait_ge(dec_act, 1)
            step(dve.tensor_scalar(lg[:, 2], lg[:, 1], 1.0, None, ALU.add), 2)
            step(dve.tensor_scalar(lg[:, 4], lg[:, 2], -1.0, None, ALU.add), 3)
            step(dve.tensor_tensor(lg[:, 4], lg[:, 1], lg[:, 4], ALU.subtract), 4)
            step(dve.reciprocal(lg[:, 5], lg[:, 2]), 5)
            step(dve.tensor_tensor(lg[:, 4], lg[:, 4], lg[:, 5], ALU.mult), 6)
            dve.wait_ge(dec_act, 2)
            step(dve.tensor_tensor(lg[:, 4], lg[:, 4], lg[:, 3], ALU.add), 7)
            step(dve.tensor_scalar(lg[:, 5], dec[:, :, :], 0.0, None, ALU.min), 8)
            step(dve.tensor_tensor(lg[:, 5], lg[:, 5], lg[:, 4], ALU.subtract), 9)
            dve.wait_ge(vec_mm, 1)
            dve.tensor_copy(vec[:, :], ps[:, 4, 0:60]).then_inc(vec_ok, 1)
            dve.wait_ge(vec_mm, 2)
            dve.tensor_copy(taps[:, :], ps[:, 5, 0:TAPS * CT]).then_inc(vec_ok, 1)
            with dve.Fori(0, NS) as n:
                for k in range(KT):
                    g = KT * n + k
                    dve.wait_ge(sq0_done, g + 1)
                    dve.tensor_tensor(xlo[:, k, n, :], ps[:, k % 4, :], xhi[:, k, n, :], ALU.subtract).then_inc(bank_free, 1)
                    dve.wait_ge(ssq_done, g + 2)
                    dve.tensor_tensor(ssq0[:, n, :], ssq0[:, n, :], sq0[:, k % 2, :], ALU.add).then_inc(ssq_done, 1)
            for k in range(KT):
                g = G_MEM + k
                dve.wait_ge(sq0_done, g + 1)
                dve.tensor_tensor(mlo[:, k, :], ps[:, k % 4, 0:M], mhi[:, k, :], ALU.subtract).then_inc(bank_free, 1)
                dve.wait_ge(ssq_done, g + 2)
                dve.tensor_tensor(ssqm[:, :], ssqm[:, :], sq0[:, k % 2, 0:M], ALU.add).then_inc(ssq_done, 1)
            for n in range(NS):
                dve.wait_ge(stat_sq, n + 1)
                dve.reciprocal(rs[:, n, :], rs[:, n, :]).then_inc(stat_rc, 1)
            dve.wait_ge(stat_sq, NS + 1)
            dve.reciprocal(rsm[:, :], rsm[:, :]).then_inc(stat_rc, 1)
            dve.wait_ge(stat_rc, NS + 1)
            end_phase(dve, 1)

            dve.memset(upad[:, :], 0.0).then_inc(pad_ok, 1)
            dve.wait_ge(pad_ok, 1)
            with dve.Fori(0, HEADS) as c:
                G = G_PROJ + GP * c

                def evac(b, n, dst):
                    g = CUM[b] + n
                    dve.wait_ge(mm_done, G + g + 1)
                    dve.tensor_tensor(dst, ps[:, g % 4, :], rs[:, n, :], ALU.mult).then_inc(bank_free, 1)

                def evac_kv(b, slot):
                    g = CUM[b]
                    dve.wait_ge(mm_done, G + g + 1)
                    dve.tensor_tensor(kz[:, slot, :], ps[:, g % 4, 0:M], rsm[:, :], ALU.mult).then_inc(bank_free, 1)

                def low(slot, order):
                    dve.wait_ge(kv_hi, 4 * c + order + 1)
                    src = ps[:, 6 + slot, 0:M] if slot < 2 else kz[:, slot, :]
                    dve.tensor_tensor(khl[:, slot, 1, :], src, khl[:, slot, 0, :], ALU.subtract).then_inc(kv_lo, 1)

                def tap(t):
                    src = upad[:, t:t + S]
                    dve.wait_ge(conv_step, TAPS * c + t)
                    if t == 0:
                        dve.wait_ge(acc_st, 16 * c)
                        ins = dve.tensor_scalar(acc[:, :], src, taps[:, bass.ds(c, 1)], vec[:, bass.ds(V_CB + c, 1)],
                                                ALU.mult, ALU.add)
                    else:
                        ins = dve.scalar_tensor_tensor(out=acc[:, :], in0=src, scalar=taps[:, bass.ds(CT * t + c, 1)],
                                                       in1=acc[:, :], op0=ALU.mult, op1=ALU.add)
                    ins.then_inc(conv_step, 1)

                dve.wait_ge(conv_step, TAPS * c)
                for n in range(NS):
                    evac(0, n, upad[:, PAD + n * NC:PAD + (n + 1) * NC])
                evac_kv(1, 0)

                def turn(m, ins):
                    ins.then_inc(tab, 1)
                    dve.wait_ge(tab, 9 * c + m + 1)
                dve.wait_ge(tab_in, 16 * c + 32)
                turn(0, dve.tensor_copy(ang[:, :], pos_i[:, :]))
                turn(1, dve.tensor_scalar(ang[:, :], ang[:, :], freq[:, 0:1], None, ALU.mult))
                turn(2, dve.tensor_scalar(turns[:, :], ang[:, :], float(1 / (2 * np.pi)), MAGIC, ALU.mult, ALU.add))
                turn(3, dve.tensor_scalar(turns[:, :], turns[:, :], -MAGIC, None, ALU.add))
                for m, part in enumerate(TWO_PI_PARTS):
                    turn(4 + m, dve.scalar_tensor_tensor(out=ang[:, :], in0=turns[:, :], scalar=-part, in1=ang[:, :],
                                                         op0=ALU.mult, op1=ALU.add))
                turn(7, dve.tensor_scalar(ang[:, :], ang[:, :], 3.1415925, -3.1415925, ALU.min, ALU.max))
                turn(8, dve.scalar_tensor_tensor(out=turns[:, :], in0=ang[:, :], scalar=-1.0, in1=ang[:, :],
                                                 op0=ALU.mult, op1=ALU.max))
                for n in range(NS):
                    dve.wait_ge(st_st[n], 64 * c)
                    evac(2, n, st[:, n, :])
                for n in range(NS):
                    dve.wait_ge(sig_done, 4 * c + n + 1)
                    u = upad[:, PAD + n * NC:PAD + (n + 1) * NC]
                    dve.tensor_tensor(u, u, st[:, n, :], ALU.mult).then_inc(u_done, 1)
                dve.wait_ge(u_done, 4 * c + 4)
                low(0, 0)
                evac_kv(3, 1)
                t = 0
                for stage, b in enumerate((4, 6, 8, 9)):
                    for n in range(NS):
                        if stage:
                            dve.wait_ge(st_st[n], 64 * c + 16 * stage)
                        evac(b, n, st[:, n, :])
                        for _ in range(2):
                            if t < TAPS:
                                tap(t)
                                t += 1
                        if stage == 0 and n == 3:
                            low(1, 1)
                            evac_kv(5, 2)
                        if stage == 1 and n == 0:
                            low(2, 2)
                        if stage == 1 and n == 3:
                            evac_kv(7, 3)
                        if stage == 2 and n == 0:
                            low(3, 3)
            leave_phase(dve)

            def decay_masks():
                dve.wait_ge(iot, 5)
                dve.tensor_scalar(io_t[:, 1, :], io_t[:, 0, :], 0.0, None, ALU.max).then_inc(dpos, 1)
                dve.wait_ge(dpos, 1)
                step(dve.tensor_scalar(io_t[:, 2, :], io_t[:, 0, :], 0.0, -1.0, ALU.min, ALU.mult), 10)
                for h in range(HEADS):
                    dve.tensor_scalar(dmask[:, h, :], io_t[:, 1, :], lg[:, 5, 0, h:h + 1], None, ALU.mult).then_inc(dlin, 1)
                    dve.wait_ge(dlin, h + 1)
                    step(dve.scalar_tensor_tensor(out=dmask[:, h, :], in0=io_t[:, 2, :], scalar=lg[:, 5, 1, h:h + 1],
                                                  in1=dmask[:, h, :], op0=ALU.mult, op1=ALU.add), 11 + h)
                dve.wait_ge(dec_act, 2 + 4 * HEADS + 1)
                step(dve.tensor_scalar(zeta[:, :, :], zeta[:, :, :], KSCALE, None, ALU.mult), 11 + HEADS)

            def rotate_k(h):
                dve.wait_ge(l_k, 16 * h + 16)
                dve.tensor_tensor(kb_[:, :], kb_[:, :], cos_t[:, :], ALU.mult).then_inc(r_k, 1)
                dve.wait_ge(r_k, h + 1)
                dve.wait_ge(p_ks, h + 1)
                dve.tensor_tensor(k_rot_b[:, :], kb_[:, :], ksb[:, :], ALU.add).then_inc(k_rot, 1)

            def rotate_q(h):
                dve.wait_ge(l_q, 16 * h + 16)
                dve.tensor_tensor(qb_[:, :], qb_[:, :], cos_t[:, :], ALU.mult).then_inc(r_q, 1)
                dve.wait_ge(r_q, h + 1)
                dve.wait_ge(p_qs, h + 1)
                dve.tensor_tensor(q_rot_b[:, :], qb_[:, :], qsb[:, :], ALU.add).then_inc(q_rot, 1)

            def weighted_values(h):
                dve.wait_ge(vt_ev, 4 * h + 4)
                if not isinstance(h, int):
                    dve.wait_ge(kvb_mm, 4 * h)
                dve.tensor_scalar(v_f[:, :, :], v_tok[:, :, :], zeta[:, 0, bass.ds(h, 1)], None, ALU.mult).then_inc(v2, 1)
                dve.tensor_scalar(v_b[:, :, :], v_tok[:, :, :], zeta[:, 1, bass.ds(h, 1)], None, ALU.mult).then_inc(v2, 1)

            def core(h):
                dve.wait_ge(y_mm, 4 * h)
                for c in range(CH - 1):
                    if c % 4 == 0:
                        dve.wait_ge(kvf_mm, 4 * h + c // 4 + 1)
                    dve.wait_ge(f_scan, 15 * h + c)
                    dve.scalar_tensor_tensor(out=st_f[:, c + 1, :], in0=st_f[:, c, :], scalar=gch[:, 0, bass.ds(h, 1)],
                                             in1=ps[:, c // 4, (c % 4) * P:(c % 4 + 1) * P],
                                             op0=ALU.mult, op1=ALU.add).then_inc(f_scan, 1)
                for m in range(CH - 1):
                    c = CH - 1 - m
                    if m % 4 == 0:
                        dve.wait_ge(kvb_mm, 4 * h + m // 4 + 1)
                    dve.wait_ge(b_scan, 15 * h + m)
                    dve.scalar_tensor_tensor(out=st_b[:, c - 1, :], in0=st_b[:, c, :], scalar=gch[:, 1, bass.ds(h, 1)],
                                             in1=ps[:, 4 + c // 4, (c % 4) * P:(c % 4 + 1) * P],
                                             op0=ALU.mult, op1=ALU.add).then_inc(b_scan, 1)
                for i in range(4):
                    dve.wait_ge(s_mm, 4 * h + i + 1)
                    dve.tensor_tensor(sT[:, 4 * i:4 * i + 4, :], ps[:, i, :].rearrange("p (c q) -> p c q", c=4),
                                      dmask[:, h, :].unsqueeze(1).to_broadcast([P, 4, P]), ALU.mult).then_inc(s_ev, 1)

            def norm(h, between=None):
                for i in range(4):
                    dve.wait_ge(me_mm, 4 * h + i + 1)
                    dve.tensor_tensor(y_b[:, i, :], y_b[:, i, :], ps[:, i, :], ALU.subtract).then_inc(cen, 1)
                dve.wait_ge(c_me, h + 1)
                for c in range(CT):
                    dve.scalar_tensor_tensor(out=cv[:, c, :], in0=ps[:, 1, :], scalar=-float(P) / CW, in1=cv[:, c, :],
                                             op0=ALU.mult, op1=ALU.add).then_inc(c_cen, 1)
                if between is not None:
                    between()
                dve.wait_ge(std, h + 1)
                dve.reciprocal(rec[:, :], rec[:, :]).then_inc(rc, 1)
                dve.wait_ge(c_std, h + 1)
                dve.reciprocal(cv_r[:, :], cv_r[:, :]).then_inc(c_rc, 1)
                for i in range(4):
                    dve.wait_ge(bc_mm, 4 * h + i + 1)
                    dve.tensor_tensor(y_b[:, i, :], y_b[:, i, :], ps[:, 4 + i, :], ALU.mult).then_inc(y_mul, 1)
                dve.wait_ge(c_rc, h + 1)
                for c in range(CT):
                    dve.tensor_tensor(cv[:, c, :], cv[:, c, :], cv_r[:, :], ALU.mult).then_inc(c_mul, 1)
                for i in range(4):
                    dve.wait_ge(y_mul, 4 * h + i + 1)
                    dve.tensor_scalar(y_b[:, i, :], y_b[:, i, :], vec[:, bass.ds(V_GNW + h, 1)], vec[:, bass.ds(V_GNB + h, 1)],
                                      ALU.mult, ALU.add).then_inc(y_aff, 1)
                for c in range(CT):
                    dve.wait_ge(c_mul, CT * h + c + 1)
                    dve.tensor_scalar(cv[:, c, :], cv[:, c, :], vec[:, V_LNW + c:V_LNW + c + 1], vec[:, V_LNB + c:V_LNB + c + 1],
                                      ALU.mult, ALU.add).then_inc(c_aff, 1)

            dve.wait_ge(l_tab, 32)
            rotate_k(0)
            decay_masks()
            dve.memset(st_f[:, 0, :], 0.0).then_inc(zero_st, 1)
            dve.memset(st_b[:, CH - 1, :], 0.0).then_inc(zero_st, 1)
            rotate_q(0)
            weighted_values(0)
            dve.wait_ge(dec_act, 2 + 4 * HEADS + 2)
            step(dve.tensor_scalar(dmask[:, :, :], dmask[:, :, :], KSCALE, None, ALU.mult), 12 + HEADS)
            dve.wait_ge(zero_st, 2)
            with dve.Fori(0, HEADS - 1) as h:
                core(h)
                dve.wait_ge(s_mm, 4 * h + 4)
                dve.wait_ge(p_qf, 2 * h + 2)
                rotate_k(h + 1)
                rotate_q(h + 1)
                norm(h, lambda: weighted_values(h + 1))
            core(HEADS - 1)
            norm(HEADS - 1)
            end_phase(dve, 3)

            dve.memset(junk[:, 4:5], 0.0).then_inc(ss_done, 2)
            dve.memset(junk[:, 5:6], 0.0).then_inc(pt_lo, 2)
            with dve.Fori(0, 2) as h:
                G = G_HALF0 + G_PER_HALF * h
                H = H_PER_HALF * h
                Q = Q_PER_HALF * h
                for k in range(KT):
                    dve.wait_ge(ysp_hi, KT * h + k + 1)
                    dve.tensor_tensor(alo[:, k, :, :], res[:, k, :, :], ahi[:, k, :, :], ALU.subtract).then_inc(ysp_lo, 1)

                def residual(i, g, hb, qb):
                    for s in range(2):
                        for n in range(NH):
                            e = 4 * i + 2 * s + n
                            m = 2 * i + s
                            dve.wait_ge(mm_done, g + e + 1)
                            dve.tensor_tensor(res[:, m, n, :], ps[:, 2 * s + n, :], res[:, m, n, :], ALU.add).then_inc(bank_free, 1)
                            dve.wait_ge(hi_done, hb + e + 1)
                            dve.tensor_tensor(blo[:, m, n, :], res[:, m, n, :], bhi[:, m, n, :], ALU.subtract).then_inc(lo_done, 1)
                            dve.wait_ge(sq_done, qb + e + 1)
                            dve.wait_ge(ss_done, qb + e + 1)
                            dve.tensor_tensor(ssq[:, n, :], ssq[:, n, :], sq[:, n, :], ALU.add).then_inc(ss_done, 1)

                def norm_recip(count):
                    for n in range(NH):
                        dve.wait_ge(n_sq, 6 * h + count + n + 1)
                        dve.reciprocal(rstd[:, n, :], rstd[:, n, :]).then_inc(n_rc, 1)
                    dve.wait_ge(n_rc, 6 * h + count + 2)

                def zero_sums(count):
                    dve.memset(ssq[:, :, :], 0.0).then_inc(ss_zero, 1)
                    wait_alone(dve, ss_zero, 3 * h + count + 1)

                zero_sums(0)
                for k in range(KT):
                    wait_alone(dve, r_in[k], 16 * h + 16)
                with dve.Fori(0, KT // 2) as i:
                    residual(i, G, H, Q)
                norm_recip(0)
                zero_sums(1)
                with dve.Fori(0, XH) as hh:
                    T = 32 * h + 8 * hh
                    for r in range(2):
                        for n in range(NH):
                            e = 2 * r + n
                            dve.wait_ge(mm_done, G + G_XQ + 8 * hh + e + 1)
                            dve.tensor_tensor(z[:, n, :], ps[:, e, :], rstd[:, n, :], ALU.mult).then_inc(bank_free, 1)
                            dve.wait_ge(hi_done, H + H_XQ + 4 * hh + e + 1)
                            dve.tensor_tensor(alo[:, 6 + r, n, :], z[:, n, :], ahi[:, 6 + r, n, :], ALU.subtract).then_inc(lo_done, 1)

                    def row_max(t):
                        dve.wait_ge(sc_mm, T + t + 1)
                        dve.tensor_reduce(mx[:, t:t + 1], ps[:, 4 + t % 2, 0:M], AX.X, ALU.max).then_inc(mx_done, 1)
                        dve.wait_ge(mx_done, T + t + 1)
                        dve.tensor_scalar(nb[:, t:t + 1], mx[:, t:t + 1], -XSCALE, None, ALU.mult).then_inc(nb_done, 1)

                    def o_low(n):
                        for d in range(2):
                            dve.wait_ge(o_hi, 16 * h + 4 * hh + 2 * n + d + 1)
                            dve.tensor_tensor(alo[:, 2 * hh + d, n, :], ps[:, 2 * n + d, :], ahi[:, 2 * hh + d, n, :],
                                              ALU.subtract).then_inc(bank_free, 1)

                    row_max(0)
                    for t in range(9):
                        if t < 8:
                            dve.wait_ge(p_exp, T + t + 3)
                            dve.reciprocal(ri[:, t:t + 1], sm[:, t:t + 1]).then_inc(ri_done, 1)
                            dve.wait_ge(ri_done, T + t + 1)
                            dve.tensor_scalar(pr[:, t % 2, :], pr[:, t % 2, :], ri[:, t:t + 1], None, ALU.mult).then_inc(p_nrm, 1)
                        if t >= 1:
                            u = t - 1
                            dve.wait_ge(pt_hi, T + u + 1)
                            cols = slice((u % 4) * P, (u % 4 + 1) * P)
                            dve.tensor_tensor(ptl[:, :, cols], ps[:, 6 + u % 2, 0:M].rearrange("p (m k) -> p m k", m=2),
                                              pth[:, :, cols], ALU.subtract).then_inc(pt_lo, 1)
                        if t == 5:
                            o_low(0)
                        if t == 8:
                            o_low(1)
                        if t + 1 < 8:
                            row_max(t + 1)
                with dve.Fori(0, KT // 2) as i:
                    residual(i, G + G_XO, H + H_XO, Q + 16)
                norm_recip(2)
                zero_sums(2)
                with dve.Fori(0, FG) as g:
                    with dve.Fori(0, KT // 2) as i:
                        for s in range(2):
                            for n in range(NH):
                                e = 4 * i + 2 * s + n
                                gg = G + G_FF + 32 * g + e
                                dve.wait_ge(mm_done, gg + 1)
                                dve.tensor_tensor(z[:, n, :], ps[:, 2 * s + n, :], rstd[:, n, :], ALU.mult).then_inc(bank_free, 1)
                                released(dve, gg)
                                dve.scalar_tensor_tensor(out=z[:, n, :], in0=z[:, n, :], scalar=0.0, in1=z[:, n, :],
                                                         op0=ALU.max, op1=ALU.mult).then_inc(z_up, 1)
                                dve.wait_ge(hi_done, H + H_FF + 16 * g + e + 1)
                                dve.tensor_tensor(alo[:, 2 * i + s, n, :], z[:, n, :], ahi[:, 2 * i + s, n, :],
                                                  ALU.subtract).then_inc(lo_done, 1)
                    with dve.Fori(0, KT // 2) as i:
                        for s in range(2):
                            for n in range(NH):
                                e = 4 * i + 2 * s + n
                                m = 2 * i + s
                                gg = G + G_FF + 32 * g + 16 + e
                                dve.wait_ge(mm_done, gg + 1)
                                dve.tensor_tensor(res[:, m, n, :], ps[:, 2 * s + n, :], res[:, m, n, :], ALU.add).then_inc(bank_free, 1)
                for k in range(KT):
                    for n in range(NH):
                        e = 2 * k + n
                        dve.wait_ge(sq_done, Q + 32 + e + 1)
                        dve.wait_ge(ss_done, Q + 32 + e + 1)
                        dve.tensor_tensor(ssq[:, n, :], ssq[:, n, :], sq[:, n, :], ALU.add).then_inc(ss_done, 1)
                norm_recip(4)
                for n in range(NH):
                    for k in range(KT):
                        e = 8 * n + k
                        if e >= 2:
                            dve.wait_ge(f_tr, 16 * h + e - 1)
                        dve.scalar_tensor_tensor(out=z[:, k % 2, :], in0=res[:, k, n, :], scalar=vec[:, V_FIN + k:V_FIN + k + 1],
                                                 in1=rstd[:, n, :], op0=ALU.mult, op1=ALU.mult).then_inc(zf, 1)


_INS = ['x', 'mem', 'positions', 'mix_norm_w', 'w_in', 'ret_decay_f', 'ret_decay_b', 'ret_gn_w', 'ret_gn_b',
        'conv_w', 'conv_b', 'conv_ln_w', 'conv_ln_b', 'w_out', 'xattn_norm_w', 'mem_norm_w',
        'w_xq', 'w_xkv', 'w_xo', 'mlp_norm_w', 'w_ff1', 'w_ff2', 'final_norm_w']


def kernel(**inputs):
    import concourse.bacc as _bacc
    from concourse.bass_utils import run_bass_kernel_spmd as _run

    nc = _bacc.Bacc("TRN2", target_bir_lowering=False, num_devices=1, dynamic_dma_scratch_size=1024)
    arrays, args = {}, []
    for name in _INS:
        a = np.ascontiguousarray(inputs[name])
        arrays[f"in_{name}"] = a
        args.append(nc.dram_tensor(f"in_{name}", a.shape, mybir.dt.from_np(a.dtype), kind="ExternalInput").ap())
    half = 64
    f = (np.float32(ROPE_THETA) ** (-np.arange(half, dtype=np.float32) / np.float32(half))).astype(np.float32)
    arrays["rope_freq"] = np.concatenate([-f, f]).reshape(2 * half, 1)
    args.append(nc.dram_tensor("rope_freq", (2 * half, 1), F32, kind="ExternalInput").ap())
    out = nc.dram_tensor("out", (1, 2048, 1024), F32, kind="ExternalOutput").ap()
    build(nc, *args, out)
    r = _run(nc, [arrays], core_ids=[0])
    return r.results[0]["out"]
```

```python
from contextlib import ExitStack

import numpy as np
import concourse.bass as bass
from concourse import mybir

F32 = mybir.dt.float32
F32R = mybir.dt.float32r
I32 = mybir.dt.int32
ALU = mybir.AluOpType
ACT = mybir.ActivationFunctionType
AX = mybir.AxisListType

P = 128
ROPE_THETA = 10000.0
EPS = 1e-6
MAGIC = 1.5 * 2.0 ** 23
TWO_PI_PARTS = (6.28125, 0.0019340515136718750, 1.2556440196931362e-06)


def build(nc, x, mem, positions, mix_norm_w, w_in, ret_decay_f, ret_decay_b, ret_gn_w, ret_gn_b,
          conv_w, conv_b, conv_ln_w, conv_ln_b, w_out, xattn_norm_w, mem_norm_w,
          w_xq, w_xkv, w_xo, mlp_norm_w, w_ff1, w_ff2, final_norm_w, rope_freq, out):
    S, D = x.shape[1], x.shape[2]
    M = mem.shape[1]
    KT = D // P
    NC = 512
    NS = S // NC
    HALF = S // 2
    NH = HALF // NC
    R = ret_gn_w.shape[1]
    CW = conv_b.shape[1]
    CT = CW // P
    TAPS = conv_w.shape[1]
    PAD = TAPS // 2
    HEADS = ret_decay_f.shape[1]
    HD = R // HEADS
    CH = S // P
    XH = 4
    XHD = D // XH
    FF = w_ff1.shape[2]
    FG = FF // D
    KSCALE = float(HD) ** -0.5
    XSCALE = float(XHD) ** -0.5
    assert HD == P and CT == HEADS == XH == NS == 4 and KT == 8 and NH == 2 and M == 2 * P and TAPS == 31

    G_MEM = NS * KT
    G_PROJ = G_MEM + KT
    PROJ = [("a", 16, 4), ("V", 0, 1), ("b", 20, 4), ("V", 1, 1), ("q", 0, 4), ("K", 0, 1),
            ("k", 4, 4), ("K", 1, 1), ("v", 8, 4), ("g", 12, 4)]
    GP = sum(b[2] for b in PROJ)
    BP = len(PROJ)
    CUM = [sum(b[2] for b in PROJ[:i]) for i in range(BP + 1)]
    G_HALF0 = G_PROJ + HEADS * GP
    G_XQ = NH * KT
    G_XO = G_XQ + XH * 8
    G_FF = G_XO + NH * KT
    G_PER_HALF = G_FF + FG * 2 * NH * KT
    J_HALF0 = HEADS * BP
    J_XQ, J_XO, J_FF = KT, 2 * KT, 3 * KT
    J_PER_HALF = J_FF + FG * 2 * KT
    N_PER_HALF = KT + FG * KT
    H_XQ, H_XO, H_FF = 16, 32, 48
    H_PER_HALF = H_FF + FG * 16
    Q_PER_HALF = 48

    xT_d = nc.dram_tensor("xT_d", [KT, P, NS, NC], F32).ap()
    proj_d = nc.dram_tensor("proj_d", [16, P, S], F32).ap()
    conv_d = nc.dram_tensor("conv_d", [CT, P, S], F32).ap()
    y_d = nc.dram_tensor("y_d", [KT, P, S], F32).ap()
    k_d = nc.dram_tensor("k_d", [KT, P, 2, M], F32).ap()
    v_d = nc.dram_tensor("v_d", [KT, P, 2, M], F32).ap()

    tab_d = nc.dram_tensor("tab_d", [2, P, S], F32).ap()

    es = ExitStack()
    with es:
        def sem(name):
            return es.enter_context(nc.semaphore(name))

        def alloc(stack, name, shape, dt):
            return stack.enter_context(nc.sbuf_tensor(name, shape, dt))

        wraw = alloc(es, "wraw", [P, 2, KT, P], F32)
        whi = alloc(es, "whi", [P, 2, KT, P], F32R)
        wlo = alloc(es, "wlo", [P, 2, KT, P], F32R)
        ident = alloc(es, "ident", [P, P], F32)
        mean_mat = alloc(es, "mean_mat", [P, P], F32)
        vec = alloc(es, "vec", [P, 60], F32)
        taps = alloc(es, "taps", [P, TAPS * CT], F32)
        eps = alloc(es, "eps", [P, 1], F32)
        sel = alloc(es, "sel", [P, P], F32)
        freq = alloc(es, "freq", [P, 1], F32)
        dec = alloc(es, "dec", [P, 2, HEADS], F32)
        lg = alloc(es, "lg", [P, 6, 2, HEADS], F32)
        zeta = alloc(es, "zeta", [P, 2, HEADS], F32)
        gch = alloc(es, "gch", [P, 2, HEADS], F32)
        io_c = alloc(es, "io_c", [P, 2], F32)
        half_pi = alloc(es, "half_pi", [P, 1], F32)
        junk = alloc(es, "junk", [P, 8], F32)
        V_MIX, V_MEM, V_XN, V_MLP, V_FIN, V_CB, V_LNW, V_LNB, V_GNW, V_GNB = 0, 8, 16, 24, 32, 40, 44, 48, 52, 56
        ps = es.enter_context(nc.psum_tensor("ps", [P, 8, NC], F32))

        with ExitStack() as s1:
            xhi = alloc(s1, "xhi", [P, KT, NS, NC], F32R)
            xlo = alloc(s1, "xlo", [P, KT, NS, NC], F32R)
            rs = alloc(s1, "rs", [P, NS, NC], F32)
            rsm = alloc(s1, "rsm", [P, M], F32)
            mhi = alloc(s1, "mhi", [P, KT, M], F32R)
            mlo = alloc(s1, "mlo", [P, KT, M], F32R)
            with ExitStack() as s0:
                xt = alloc(s0, "xt", [P, 2, 4, D // 2], F32)
                memt = alloc(s0, "memt", [P, 2, D], F32)
                gap = alloc(s0, "gap", [P, NC + 2 * PAD], F32)
                xf = alloc(s0, "xf", [P, 4, NC], F32)
                sq0 = alloc(s0, "sq0", [P, 2, NC], F32)
                vrow, trow = xf[:, 0, 0:P], xf[:, 1, 0:P]
            kz = alloc(s1, "kz", [P, 4, M], F32)
            khl = alloc(s1, "khl", [P, 4, 2, M], F32R)
            ang = alloc(s1, "ang", [P, NC], F32)
            turns = alloc(s1, "turns", [P, NC], F32)
            pos_i = alloc(s1, "pos_i", [P, NC], I32)
            upad = alloc(s1, "upad", [P, S + 2 * PAD], F32)
            acc = alloc(s1, "acc", [P, S], F32)
            st = alloc(s1, "st", [P, NS, NC], F32)

        with ExitStack() as s2:
            def b2(name, shape=(P, S), dt=F32):
                return alloc(s2, name, list(shape), dt)
            qb_, qsb, vb, gb = (b2(n) for n in ("q_in", "q_sw", "v_in", "g_in"))
            q_rot_b, k_rot_b, q_f, q_b = (b2(n) for n in ("q_rot", "k_rot", "q_f", "q_b"))
            k_tok, v_tok, v_f, v_b = (b2(n, (P, CH, P)) for n in ("k_tok", "v_tok", "v_f", "v_b"))
            sT = b2("sT", (P, CH, P))
            io_t = sT[:, 0:3, :]
            y_b = b2("y_b", (P, NS, NC))
            st_f = b2("st_f", (P, CH, P))
            dmask = b2("dmask", (P, HEADS, P))
            xi_f, xi_b = b2("xi_f", (P, HEADS, P)), b2("xi_b", (P, HEADS, P))
            rec = b2("rec", (P, NC))
            st_b = b2("st_b", (P, CH, P))
            io_s = b2("io_s", (P, 2, P))
            cos_t, sin_t = b2("cos_t"), b2("sin_t")
            kb_, ksb = b2("k_in"), b2("k_sw")
            sg = b2("sg", (P, NS, NC))
            w1 = b2("w1", (P, 2, NC))
            cv = b2("cv", (P, CT, NC))
            cv_w = b2("cv_w", (P, 2, NC))
            cv_r = b2("cv_r", (P, NC))

        with ExitStack() as s3:
            def b3(name, shape, dt=F32, stack=s3):
                return alloc(stack, name, list(shape), dt)
            with ExitStack() as over:
                y_stage = b3("y_stage", (P, KT, NH, NC), F32, over)
            bhi, ahi, alo = (b3(n, (P, KT, NH, NC), F32R) for n in ("bhi", "ahi", "alo"))
            with ExitStack() as over:
                zfin = b3("zfin", (P, KT, NH, NC), F32, over)
            blo = b3("blo", (P, KT, NH, NC), F32R)
            res = b3("res", (P, KT, NH, NC))
            kh = b3("kh", (P, 2, 2, M), F32R)
            vh = b3("vh", (P, 2, 2, 2, P), F32R)
            with ExitStack() as over:
                rows = b3("rows", (P, 2, D), F32, over)
            pth, ptl = b3("pth", (P, 2, NC), F32R), b3("ptl", (P, 2, NC), F32R)
            rstd = b3("rstd", (P, NH, NC))
            sq = b3("sq", (P, 2, NC))
            ssq = b3("ssq", (P, NH, NC))
            z = b3("z", (P, 2, NC))
            pr = b3("pr", (P, 2, 2, M))
            mx, nb, sm, ri = (b3(n, (P, 8)) for n in ("mx", "nb", "sm", "ri"))
            Y_ORDER = [4, 5, 6, 7, 0, 1, 2, 3]

        phase = sem("phase")
        passed = sem("passed")
        consts = sem("consts")
        vec_in, vec_mm, vec_ok = sem("vec_in"), sem("vec_mm"), sem("vec_ok")
        w_full = [sem("w_full0"), sem("w_full1")]
        w_scaled = sem("w_scaled")
        w_hi = sem("w_hi")
        w_ready = sem("w_ready")
        mm_done = sem("mm_done")
        bank_free = sem("bank_free")
        x_in = [sem("x_in0"), sem("x_in1")]
        mem_in = sem("mem_in")
        hi0, sq0_done, ssq_done = sem("hi0"), sem("sq0_done"), sem("ssq_done")
        xf_done = sem("xf_done")
        xf_st = [sem(f"xf_st{n}") for n in range(4)]
        stat_mm, stat_sq, stat_rc = sem("stat_mm"), sem("stat_sq"), sem("stat_rc")
        sig_done, u_done, pad_ok = sem("sig_done"), sem("u_done"), sem("pad_ok")
        conv_step, acc_st = sem("conv_step"), sem("acc_st")
        st_st = [sem(f"st_st{n}") for n in range(NS)]
        kv_hi, kv_lo, vt_mm0 = sem("kv_hi"), sem("kv_lo"), sem("vt_mm0")
        kv_st = [sem(f"kv_st{n}") for n in range(4)]

        G0 = 4

        def released(eng, g):
            eng.wait_ge(bank_free, g + 1 + G0)

        def wait_alone(eng, which, value):
            eng.wait_ge(which, value)
            eng.sem_inc(passed, 1)

        def leave_phase(eng):
            eng.drain().then_inc(phase, 1)

        def first(h):
            return isinstance(h, int) and h == 0

        def last(h):
            return isinstance(h, int) and h == HEADS - 1

        def start_at_one(eng, *semaphores):
            for which in semaphores:
                eng.sem_inc(which, 1)

        block = es.enter_context(nc.Block())

        l_q, l_qs, l_k, l_ks, l_v, l_g = (sem(n) for n in ("l_q", "l_qs", "l_k", "l_ks", "l_v", "l_g"))
        tab_in, tab, tab_sin, tab_st = (sem(n) for n in ("tab_in", "tab", "tab_sin", "tab_st"))
        dec_in, iot, dec_dve, dec_act = (sem(n) for n in ("dec_in", "iot", "dec_dve", "dec_act"))
        l_tab, dpos, dlin, zero_st = sem("l_tab"), sem("dpos"), sem("dlin"), sem("zero_st")
        p_qs, p_ks, p_qf = sem("p_qs"), sem("p_ks"), sem("p_qf")
        r_q, r_k, q_rot, k_rot = sem("r_q"), sem("r_k"), sem("q_rotd"), sem("k_rotd")
        kt_mm, vt_mm, kt_ev, vt_ev = sem("kt_mm"), sem("vt_mm"), sem("kt_ev"), sem("vt_ev")
        v2 = sem("v2")
        kvf_mm, kvb_mm, f_scan, b_scan = sem("kvf_mm"), sem("kvb_mm"), sem("f_scan"), sem("b_scan")
        s_mm, s_ev, y_mm, y_ev = sem("s_mm"), sem("s_ev"), sem("y_mm"), sem("y_ev")
        me_mm, cen, sqd, va_mm, std = sem("me_mm"), sem("cen"), sem("sqd"), sem("va_mm"), sem("std")
        rc, bc_mm, y_mul, y_aff, y_out = (sem(n) for n in ("rc", "bc_mm", "y_mul", "y_aff", "y_out"))
        sgd, gate, y_st = sem("sgd"), sem("gate"), sem("y_st")
        c_in, c_me, c_cen, c_sq, c_va, c_std, c_rc, c_mul, c_gat, c_sig, c_out, c_st = (
            sem(n) for n in ("c_in", "c_me", "c_cen", "c_sq", "c_va", "c_std", "c_rc", "c_mul", "c_gat", "c_sig", "c_out", "c_st"))
        y_in = [sem(f"y_in{k}") for k in range(KT)]
        r_in = [sem(f"r_in{k}") for k in range(KT)]
        ysp_hi, ysp_lo = sem("ysp_hi"), sem("ysp_lo")
        hi_done, lo_done, z_up = sem("hi_done"), sem("lo_done"), sem("z_up")
        sq_done, ss_zero, ss_done = sem("sq_done"), sem("ss_zero"), sem("ss_done")
        n_mm, n_sq, n_rc = sem("n_mm"), sem("n_sq"), sem("n_rc")
        kv_in = sem("kv_in")
        sc_mm, mx_done, nb_done, p_exp, ri_done, p_nrm = (sem(n) for n in ("sc_mm", "mx_done", "nb_done", "p_exp", "ri_done", "p_nrm"))
        pt_mm, pt_hi, pt_lo, o_hi = (sem(n) for n in ("pt_mm", "pt_hi", "pt_lo", "o_hi"))
        zf, f_tr, f_cp = sem("zf"), sem("f_tr"), sem("f_cp")
        f_st = [sem("f_st0"), sem("f_st1")]

        @block.sync
        def _(sp):
            start_at_one(sp, *xf_st)

            def load_weights(j, slot, src):
                sp.wait_ge(w_ready, j + 1)
                sp.dma_start(wraw[:, slot, :, :], src.rearrange("(k p) m -> p k m", p=P)).then_inc(w_full[slot], 16)

            xr = x.rearrange("b (n s p) d -> n p (b s) d", s=4, p=P)
            for s in range(2):
                sp.dma_start(xt[:, s, :, :], xr[0, :, :, s * (D // 2):(s + 1) * (D // 2)]).then_inc(x_in[s], 16)
            sp.wait_ge(x_in[0], 16)
            sp.dma_start(memt[:, :, :], mem.rearrange("b (s p) d -> p (b s) d", p=P)).then_inc(mem_in, 16)
            sp.dma_start(freq[:, :], rope_freq).then_inc(tab_in, 16)
            sp.dma_start(dec[:, 0, :], ret_decay_f[0:1, :].to_broadcast([P, HEADS])).then_inc(dec_in, 16)
            sp.dma_start(dec[:, 1, :], ret_decay_b[0:1, :].to_broadcast([P, HEADS])).then_inc(dec_in, 16)

            def proj_weights(c, b):
                kind, col, _ = PROJ[b]
                if kind == "K":
                    src = w_xkv[0, :, bass.ds((2 * c + col) * P, P)]
                elif kind == "V":
                    src = w_xkv[0, :, bass.ds((KT + 2 * c + col) * P, P)]
                else:
                    src = w_in[0, :, bass.ds((c + col) * P, P)]
                load_weights(BP * c + b, b % 2, src)

            proj_weights(0, 0)
            proj_weights(0, 1)
            with sp.Fori(0, NS) as n:
                for k in range(KT):
                    sp.wait_ge(xf_done, KT * n + k + 1)
                    sp.dma_start(xT_d[k, :, n, :], xf[:, k % 4, :]).then_inc(xf_st[k % 4], 16)
            for b in range(2, BP):
                proj_weights(0, b)
            with sp.Fori(1, HEADS) as c:
                for b in range(BP):
                    proj_weights(c, b)
            for s in range(4):
                sp.wait_ge(xf_st[s], 1 + 16 * NS * KT // 4)

            H2 = P // 2

            def load_k(h):
                sp.dma_start(kb_[:, :], proj_d[4 + h]).then_inc(l_k, 16)
                sp.dma_start(ksb[0:H2, :], proj_d[4 + h, H2:P]).then_inc(l_ks, 16)
                sp.dma_start(ksb[H2:P, :], proj_d[4 + h, 0:H2]).then_inc(l_ks, 16)

            def load_v(h):
                sp.dma_start(vb[:, :], proj_d[8 + h]).then_inc(l_v, 16)

            def load_q(h):
                sp.dma_start(qb_[:, :], proj_d[h]).then_inc(l_q, 16)
                sp.dma_start(qsb[0:H2, :], proj_d[h, H2:P]).then_inc(l_qs, 16)
                sp.dma_start(qsb[H2:P, :], proj_d[h, 0:H2]).then_inc(l_qs, 16)

            def load_g(h):
                sp.dma_start(gb[:, :], proj_d[12 + h]).then_inc(l_g, 16)

            def load_conv(n):
                sp.dma_start(cv[:, :, :], conv_chunk(conv_d, n)).then_inc(c_in, 16)

            def conv_chunk(d, n):
                return d[:, :, n * NC:(n + 1) * NC].rearrange("c p n -> p c n")

            sp.wait_ge(mm_done, G_PROJ + GP * (HEADS - 1) + CUM[8])
            sp.wait_ge(tab_st, 1 + 32 * HEADS)
            sp.dma_start(sin_t[:, :], tab_d[0]).then_inc(l_tab, 16)
            sp.dma_start(cos_t[:, :], tab_d[1]).then_inc(l_tab, 16)
            for n in range(4):
                sp.wait_ge(kv_st[n], 1 + 16 * HEADS)
            for n in range(NS):
                sp.wait_ge(st_st[n], 1 + 16 * 4)
            load_k(0)
            sp.wait_ge(mm_done, G_HALF0)
            load_v(0)
            load_q(0)
            load_g(0)
            for n in range(NS):
                sp.wait_ge(st_st[n], 1 + 16 * 4 * HEADS)
            sp.wait_ge(acc_st, 1 + 16 * HEADS)
            leave_phase(sp)
            sp.wait_ge(phase, 5 * 1)
            load_conv(0)
            for s in range(2):
                load_weights(J_HALF0 + s, s, w_out[0, :, s * P:(s + 1) * P])
            sp.wait_ge(k_rot, 1)
            load_k(1)
            sp.wait_ge(vt_mm, 4)
            load_v(1)
            sp.wait_ge(q_rot, 1)
            load_q(1)
            for h in range(HEADS):
                if h + 1 < HEADS:
                    sp.wait_ge(gate, 4 * (h + 1))
                    load_g(h + 1)
                if h + 2 < HEADS:
                    sp.wait_ge(k_rot, h + 2)
                    load_k(h + 2)
                    sp.wait_ge(vt_mm, 4 * (h + 2))
                    load_v(h + 2)
                    sp.wait_ge(q_rot, h + 2)
                    load_q(h + 2)
                if h + 1 == HEADS:
                    sp.wait_ge(q_rot, HEADS)
                    sp.wait_ge(vt_mm, 4 * HEADS)
                    sp.wait_ge(gate, 4 * HEADS)
                    sp.wait_ge(y_st, 16 * (HEADS - 1))
                    for k in Y_ORDER[:KT - 1]:
                        sp.dma_start(y_stage[:, k, :, :].rearrange("p a b -> p (a b)"), y_d[k, :, 0:HALF]).then_inc(y_in[k], 16)
                sp.wait_ge(y_out, 4 * (h + 1))
                n = NH if h + 1 == HEADS else 0
                sp.dma_start(y_d[h, :, n * NC:S], y_b[:, n:NS, :].rearrange("p a b -> p (a b)")).then_inc(y_st, 16)
                sp.wait_ge(c_out, CT * (h + 1))
                sp.dma_start(conv_chunk(y_d[HEADS:HEADS + CT], h), cv[:, :, :]).then_inc(c_st, 16)
                if h + 1 < HEADS:
                    sp.wait_ge(c_st, 16 * (h + 1))
                    load_conv(h + 1)
            sp.wait_ge(y_st, 16 * HEADS)
            sp.wait_ge(c_st, 16 * HEADS)
            leave_phase(sp)

            for h in range(2):
                J = J_HALF0 + J_PER_HALF * h
                with sp.Fori(1 - h, KT // 2) as i:
                    for s in range(2):
                        load_weights(J + 2 * i + s, s, w_out[0, :, bass.ds((2 * i + s) * P, P)])
                with sp.Fori(0, KT // 2) as i:
                    for s in range(2):
                        load_weights(J + J_XQ + 2 * i + s, s, w_xq[0, :, bass.ds((2 * i + s) * P, P)])
                with sp.Fori(0, KT // 2) as i:
                    for s in range(2):
                        load_weights(J + J_XO + 2 * i + s, s, w_xo[0, :, bass.ds((2 * i + s) * P, P)])
                with sp.Fori(0, FG) as g:
                    with sp.Fori(0, KT // 2) as i:
                        for s in range(2):
                            load_weights(J + J_FF + 16 * g + 2 * i + s, s,
                                         w_ff1[0, :, bass.ds((KT * g + 2 * i + s) * P, P)])
                    with sp.Fori(0, KT // 2) as i:
                        for s in range(2):
                            load_weights(J + J_FF + 16 * g + KT + 2 * i + s, s,
                                         w_ff2[0, bass.ds(g * D, D), bass.ds((2 * i + s) * P, P)])

        @block.gpsimd
        def _(pool):
            pool.memset(ident[:, :], 0.0).then_inc(consts, 1)
            pool.memset(mean_mat[:, :], 1.0 / P).then_inc(consts, 1)
            pool.memset(eps[:, :], EPS).then_inc(consts, 1)
            pool.memset(half_pi[:, :], float(np.pi / 2)).then_inc(consts, 1)
            pool.memset(sel[:, :], 0.0).then_inc(consts, 1)
            pool.wait_ge(consts, 5)
            for i in range(4):
                pool.memset(sel[32 * i:32 * i + 1, :], 1.0).then_inc(consts, 1)
            pool.wait_ge(consts, 9)
            pool.affine_select(out=ident[:, :], in_=ident[:, :], compare_op=ALU.not_equal, fill=1.0,
                               base=0, pattern=[[-1, P]], channel_multiplier=1).then_inc(consts, 1)
            pool.memset(junk[:, 2:3], 0.0).then_inc(w_ready, 2)
            pool.wait_ge(vec_ok, 2)
            def split_weights(j, full, slot, used, norm=None, count=None):
                pool.wait_ge(w_full[slot], full)
                if norm is not None:
                    pool.tensor_tensor(wraw[:, slot, :, :], wraw[:, slot, :, :],
                                       vec[:, norm:norm + KT].unsqueeze(2).to_broadcast([P, KT, P]),
                                       ALU.mult).then_inc(w_scaled, 1)
                    pool.wait_ge(w_scaled, count + 1)
                if used is not None:
                    wait_alone(pool, mm_done, used)
                pool.tensor_scalar(whi[:, slot, :, :], wraw[:, slot, :, :], 1.0, 0.0, ALU.mult, ALU.add).then_inc(w_hi, 1)
                pool.wait_ge(w_hi, j + 1)
                pool.tensor_tensor(wlo[:, slot, :, :], wraw[:, slot, :, :], whi[:, slot, :, :],
                                   ALU.subtract).then_inc(w_ready, 1)

            def proj_split(c, b):
                free = first(c) and b < 2
                used = G_PROJ + GP * c + (CUM[b - 1] if b >= 2 else CUM[BP - 1 + b] - GP)
                split_weights(BP * c + b, 16 * (5 * c + b // 2) + 16, b % 2, None if free else used,
                              V_MEM if PROJ[b][0] in "KV" else V_MIX, BP * c + b)

            proj_split(0, 0)
            proj_split(0, 1)
            with pool.Fori(0, NS) as n:
                for k in range(KT):
                    g = KT * n + k
                    released(pool, g)
                    pool.wait_ge(xf_st[k % 4], 1 + 16 * (2 * n + k // 4))
                    pool.tensor_tensor(xf[:, k % 4, :], xhi[:, k, n, :], xlo[:, k, n, :], ALU.add).then_inc(xf_done, 1)
            for b in range(2, BP):
                proj_split(0, b)
            with pool.Fori(1, HEADS) as c:
                for b in range(BP):
                    proj_split(c, b)
            leave_phase(pool)

            def swapped_k(h):
                pool.wait_ge(l_ks, 32 * h + 32)
                pool.tensor_tensor(ksb[:, :], ksb[:, :], sin_t[:, :], ALU.mult).then_inc(p_ks, 1)

            def swapped_q(h):
                pool.wait_ge(l_qs, 32 * h + 32)
                pool.tensor_tensor(qsb[:, :], qsb[:, :], sin_t[:, :], ALU.mult).then_inc(p_qs, 1)

            def decayed_q(h):
                pool.wait_ge(q_rot, h + 1)
                if not first(h):
                    pool.wait_ge(y_mm, 4 * h)
                for dst, xi in ((q_f, xi_f), (q_b, xi_b)):
                    pool.tensor_tensor(dst[:, :].rearrange("p (c q) -> p c q", q=P),
                                       q_rot_b[:, :].rearrange("p (c q) -> p c q", q=P),
                                       xi[:, bass.ds(h, 1), :].to_broadcast([P, CH, P]), ALU.mult).then_inc(p_qf, 1)

            def silu(h):
                for i in range(4):
                    pool.wait_ge(sgd, 4 * h + i + 1)
                    pool.tensor_tensor(sg[:, i, :], gb[:, i * NC:(i + 1) * NC], sg[:, i, :], ALU.mult).then_inc(gate, 1)

            def gated(h):
                for i in range(4):
                    pool.wait_ge(gate, 4 * h + i + 1)
                    pool.wait_ge(y_aff, 4 * h + i + 1)
                    dst = y_stage[:, HEADS - 1, i, :] if last(h) and i < NH else y_b[:, i, :]
                    pool.tensor_tensor(dst, y_b[:, i, :], sg[:, i, :], ALU.mult).then_inc(y_out, 1)

            def conv_silu(h):
                for c in range(CT):
                    pool.wait_ge(c_sig, CT * h + c + 1)
                    pool.tensor_tensor(cv[:, c, :], cv[:, c, :], (w1 if c < 2 else cv_w)[:, c % 2, :], ALU.mult).then_inc(c_out, 1)

            pool.wait_ge(l_tab, 32)
            swapped_k(0)
            pool.wait_ge(mm_done, G_HALF0)
            pool.wait_ge(bank_free, G_HALF0 + G0)
            pool.iota(io_t[:, 0, :], pattern=[[1, P]], base=0, channel_multiplier=-1,
                      allow_small_or_imprecise_dtypes=True).then_inc(iot, 1)
            pool.iota(io_s[:, 0, :], pattern=[[1, P]], base=1, channel_multiplier=0,
                      allow_small_or_imprecise_dtypes=True).then_inc(iot, 1)
            pool.iota(io_s[:, 1, :], pattern=[[-1, P]], base=P, channel_multiplier=0,
                      allow_small_or_imprecise_dtypes=True).then_inc(iot, 1)
            pool.iota(io_c[:, 0:1], pattern=[[1, 1]], base=P - 1, channel_multiplier=-1,
                      allow_small_or_imprecise_dtypes=True).then_inc(iot, 1)
            pool.iota(io_c[:, 1:2], pattern=[[1, 1]], base=0, channel_multiplier=1,
                      allow_small_or_imprecise_dtypes=True).then_inc(iot, 1)
            pool.wait_ge(l_qs, 32)
            pool.tensor_tensor(qsb[:, :], qsb[:, :], sin_t[:, :], ALU.mult).then_inc(p_qs, 1)
            pool.wait_ge(dec_act, 2 + 4 * HEADS)
            decayed_q(0)
            silu(0)
            for s in range(2):
                split_weights(J_HALF0 + s, 16 * (J_HALF0 // 2) + 16, s, G_HALF0)
            swapped_k(1)
            swapped_q(1)
            with pool.Fori(0, HEADS - 2) as h:
                decayed_q(h + 1)
                gated(h)
                swapped_k(h + 2)
                conv_silu(h)
                swapped_q(h + 2)
                silu(h + 1)
            decayed_q(HEADS - 1)
            gated(HEADS - 2)
            conv_silu(HEADS - 2)
            silu(HEADS - 1)
            gated(HEADS - 1)
            conv_silu(HEADS - 1)
            leave_phase(pool)

            for h in range(2):
                J = J_HALF0 + J_PER_HALF * h
                G = G_HALF0 + G_PER_HALF * h
                N = J_HALF0 + N_PER_HALF * h
                L = 16 * (J_HALF0 // 2) + 16 * (J_PER_HALF // 2) * h + 16
                with pool.Fori(1 - h, KT // 2) as i:
                    for s in range(2):
                        split_weights(J + 2 * i + s, L + 16 * i, s, G + 4 * i + 2 * s - 2)
                for hh in range(XH):
                    for r in range(2):
                        used = G + (2 * (KT - 2 + r) + 2 if hh == 0 else G_XQ + 8 * (hh - 1) + 2 * r + 2)
                        split_weights(J + J_XQ + 2 * hh + r, L + 16 * (4 + hh), r, used, V_XN, N + 2 * hh + r)
                for s in range(2):
                    split_weights(J + J_XO + s, L + 16 * 8, s, G + G_XQ + 24 + 2 * s + 2)
                with pool.Fori(1, KT // 2) as i:
                    for s in range(2):
                        split_weights(J + J_XO + 2 * i + s, L + 16 * 8 + 16 * i, s, G + G_XO + 4 * i + 2 * s - 2)
                with pool.Fori(0, FG) as g:
                    with pool.Fori(0, KT // 2) as i:
                        for s in range(2):
                            split_weights(J + J_FF + 16 * g + 2 * i + s, L + 16 * 12 + 128 * g + 16 * i, s,
                                          G + G_FF + 32 * g + 4 * i + 2 * s - 2, V_MLP, N + KT + KT * g + 2 * i + s)
                    with pool.Fori(0, KT // 2) as i:
                        for s in range(2):
                            split_weights(J + J_FF + 16 * g + KT + 2 * i + s, L + 16 * 12 + 128 * g + 64 + 16 * i, s,
                                          G + G_FF + 32 * g + 16 + 4 * i + 2 * s - 2)

        @block.tensor
        def _(pe):
            def gemm(bank, slot, hi, lo, n, before=None, order=range(KT), block=None):
                o = ps[:, bank, 0:n]
                if block is not None:
                    pe.wait_ge(w_hi, block + 1)
                for k in order:
                    if before is not None:
                        before(k)
                    nc.tensor.matmul(o, whi[:, slot, k, :], hi(k), start=(k == order[0]), stop=False)
                    nc.tensor.matmul(o, whi[:, slot, k, :], lo(k), start=False, stop=False)
                if block is not None:
                    pe.wait_ge(w_ready, block + 3)
                for k in order:
                    last = nc.tensor.matmul(o, wlo[:, slot, k, :], hi(k), start=False, stop=(k == order[-1]))
                last.then_inc(mm_done, 1)

            def bank_ready(g):
                pe.wait_ge(bank_free, g + 1)

            pe.wait_ge(consts, 10)
            pe.wait_ge(vec_in, 16 * 11)
            pe.transpose(ps[:, 4, 0:60], vrow[0:60, :], ident[0:60, 0:60]).then_inc(vec_mm, 1)
            pe.transpose(ps[:, 5, 0:TAPS * CT], trow[0:TAPS * CT, :],
                         ident[0:TAPS * CT, 0:TAPS * CT]).then_inc(vec_mm, 1)
            with pe.Fori(0, NS) as n:
                for k in range(KT):
                    if k % 4 == 0:
                        pe.wait_ge(x_in[k // 4], 16 * n + 16)
                    bank_ready(KT * n + k)
                    for t in range(4):
                        last = pe.transpose(ps[:, k % 4, t * P:(t + 1) * P],
                                            xt[:, k // 4, t, (k % 4) * P:(k % 4 + 1) * P], ident[:, :])
                    last.then_inc(mm_done, 1)
            pe.wait_ge(mem_in, 16)
            for k in range(KT):
                bank_ready(G_MEM + k)
                for t in range(2):
                    last = pe.transpose(ps[:, k % 4, t * P:(t + 1) * P], memt[:, t, k * P:(k + 1) * P], ident[:, :])
                last.then_inc(mm_done, 1)
            pe.wait_ge(vec_ok, 2)
            for n in range(NS):
                pe.wait_ge(ssq_done, 2 + KT * (n + 1))
                pe.matmul(ps[:, 4 + n, :], mean_mat[:, :], rs[:, n, :], start=True, stop=True).then_inc(stat_mm, 1)
            pe.wait_ge(ssq_done, 2 + KT * (NS + 1))
            pe.wait_ge(stat_sq, 1)
            pe.matmul(ps[:, 4, 0:M], mean_mat[:, :], rsm[:, :], start=True, stop=True).then_inc(stat_mm, 1)
            released(pe, G_PROJ - 1)
            with pe.Fori(0, HEADS) as c:
                for b, (kind, col, groups) in enumerate(PROJ):
                    for n in range(groups):
                        g = CUM[b] + n
                        bank_ready(G_PROJ + GP * c + g)
                        fresh = BP * c + b if n == 0 else None
                        if kind in "KV":
                            gemm(g % 4, b % 2, lambda k: mhi[:, k, :], lambda k: mlo[:, k, :], M, block=fresh)
                        else:
                            gemm(g % 4, b % 2, lambda k, n=n: xhi[:, k, n, :], lambda k, n=n: xlo[:, k, n, :], NC, block=fresh)
                    if b >= 2 and PROJ[b - 1][0] == "V":
                        r = PROJ[b - 1][1]
                        released(pe, G_PROJ + GP * c + CUM[b - 1])
                        pe.wait_ge(kv_lo, 1 + 4 * c)
                        for t in range(2):
                            last = pe.transpose(ps[:, 6 + r, t * P:(t + 1) * P], kz[:, r, t * P:(t + 1) * P], ident[:, :])
                        last.then_inc(vt_mm0, 1)
            leave_phase(pe)

            def key_tokens(h):
                pe.wait_ge(k_rot, h + 1)
                for i in range(4):
                    for c in range(4):
                        cc = 4 * i + c
                        last = pe.transpose(ps[:, 4 + i, c * P:(c + 1) * P], k_rot_b[:, cc * P:(cc + 1) * P], ident[:, :])
                    last.then_inc(kt_mm, 1)

            def value_tokens(h):
                pe.wait_ge(l_v, 16 * h + 16)
                for i in range(4):
                    pe.wait_ge(kt_ev, 4 * h + i + 1)
                    for c in range(4):
                        cc = 4 * i + c
                        last = pe.transpose(ps[:, 4 + i, c * P:(c + 1) * P], vb[:, cc * P:(cc + 1) * P], ident[:, :])
                    last.then_inc(vt_mm, 1)

            def core(h):
                pe.wait_ge(v2, 2 * h + 1)
                if not first(h):
                    pe.wait_ge(std, 1 + h)
                    pe.wait_ge(c_std, 1 + h)
                for i in range(4):
                    for c in range(4):
                        cc = 4 * i + c
                        last = pe.matmul(ps[:, i, c * P:(c + 1) * P], k_tok[:, cc, :], v_f[:, cc, :], start=True, stop=True)
                    last.then_inc(kvf_mm, 1)
                pe.wait_ge(v2, 2 * h + 2)
                if not first(h):
                    pe.wait_ge(y_mul, 1 + 4 * h)
                for i in reversed(range(4)):
                    for c in range(4):
                        cc = 4 * i + c
                        last = pe.matmul(ps[:, 4 + i, c * P:(c + 1) * P], k_tok[:, cc, :], v_b[:, cc, :], start=True, stop=True)
                    last.then_inc(kvb_mm, 1)
                pe.wait_ge(q_rot, h + 1)
                pe.wait_ge(f_scan, 15 * h + 15)
                for i in range(4):
                    for c in range(4):
                        cc = 4 * i + c
                        last = pe.matmul(ps[:, i, c * P:(c + 1) * P], k_rot_b[:, cc * P:(cc + 1) * P],
                                         q_rot_b[:, cc * P:(cc + 1) * P], start=True, stop=True)
                    last.then_inc(s_mm, 1)
                pe.wait_ge(b_scan, 15 * h + 15)
                pe.wait_ge(p_qf, 2 * h + 2)
                for i in range(4):
                    pe.wait_ge(s_ev, 4 * h + i + 1)
                    for c in range(4):
                        cc = 4 * i + c
                        o = ps[:, 4 + i, c * P:(c + 1) * P]
                        pe.matmul(o, v_tok[:, cc, :], sT[:, cc, :], start=True, stop=False)
                        pe.matmul(o, st_f[:, cc, :], q_f[:, cc * P:(cc + 1) * P], start=False, stop=False)
                        last = pe.matmul(o, st_b[:, cc, :], q_b[:, cc * P:(cc + 1) * P], start=False, stop=True)
                    last.then_inc(y_mm, 1)
                for i in range(4):
                    pe.wait_ge(y_ev, 4 * h + i + 1)
                    pe.matmul(ps[:, i, :], mean_mat[:, :], y_b[:, i, :], start=True, stop=True).then_inc(me_mm, 1)

            def norms(h):
                pe.wait_ge(c_in, 16 * h + 16)
                pe.wait_ge(cen, 4 * h + 4)
                for c in range(CT):
                    last = pe.matmul(ps[:, 1, :], mean_mat[:, :], cv[:, c, :], start=(c == 0), stop=(c == CT - 1))
                last.then_inc(c_me, 1)
                for i in range(4):
                    pe.wait_ge(sqd, 4 * h + i + 1)
                    pe.matmul(ps[32 * i:32 * i + 32, 0, :], mean_mat[:, 0:32], w1[:, i % 2, :], start=True, stop=True).then_inc(va_mm, 1)
                for c in range(CT):
                    pe.wait_ge(c_sq, CT * h + c + 1)
                    pe.matmul(ps[:, 2, :], mean_mat[:, :], cv_w[:, c % 2, :], start=(c == 0), stop=(c == CT - 1)).then_inc(c_va, 1)

            def spread(h):
                pe.wait_ge(rc, h + 1)
                for i in range(4):
                    pe.matmul(ps[:, 4 + i, :], sel[32 * i:32 * i + 32, :], rec[32 * i:32 * i + 32, :], start=True, stop=True).then_inc(bc_mm, 1)

            key_tokens(0)
            value_tokens(0)
            with pe.Fori(0, HEADS - 1) as h:
                core(h)
                key_tokens(h + 1)
                value_tokens(h + 1)
                norms(h)
                pe.wait_ge(vt_ev, 4 * h + 8)
                spread(h)
            core(HEADS - 1)
            norms(HEADS - 1)
            spread(HEADS - 1)
            leave_phase(pe)

            def stats(h, count, first):
                pe.wait_ge(ss_done, 2 + count)
                if first is not None:
                    first()
                for n in range(NH):
                    pe.matmul(ps[:, 4 + n, :], mean_mat[:, :], ssq[:, n, :], start=True, stop=True).then_inc(n_mm, 1)

            for h in range(2):
                G = G_HALF0 + G_PER_HALF * h
                J = J_HALF0 + J_PER_HALF * h
                H = H_PER_HALF * h

                def product(i, g, j, hi, lo, ready, order=range(KT)):
                    for s in range(2):
                        for n in range(NH):
                            bank_ready(g + 4 * i + 2 * s + n)
                            gemm(2 * s + n, s, lambda k: hi[:, k, n, :], lambda k: lo[:, k, n, :], NC,
                                 ready if s == 0 and n == 0 else None, order, j + 2 * i + s if n == 0 else None)

                def mix(i, h=h, ready=None):
                    product(i, G_HALF0 + G_PER_HALF * h, J_HALF0 + J_PER_HALF * h, ahi, alo, ready, Y_ORDER)

                def split_done(k, h=h):
                    pe.wait_ge(ysp_lo, KT * h + Y_ORDER.index(k) + 1)

                if h == 0:
                    mix(0, ready=split_done)
                with pe.Fori(1, KT // 2) as i:
                    mix(i)
                stats(h, Q_PER_HALF * h + 16, (lambda: pe.wait_ge(f_cp, 16 * h)) if h else None)
                with pe.Fori(0, XH) as hh:
                    for r in range(2):
                        for n in range(NH):
                            bank_ready(G + G_XQ + 8 * hh + 2 * r + n)
                            gemm(2 * r + n, r, lambda k: bhi[:, k, n, :], lambda k: blo[:, k, n, :], NC,
                                 (lambda k: pe.wait_ge(lo_done, H + 2 * k + 2)) if r == n == 0 else None,
                                 block=J + J_XQ + 2 * hh + r if n == 0 else None)
                    U = 16 * h + 4 * hh
                    pe.wait_ge(kv_in, 128 * h + 32 * hh + 32)

                    def scores(u):
                        n = u // 2
                        pe.wait_ge(lo_done, H + H_XQ + 4 * hh + 3 + n)
                        pe.wait_ge(p_exp, 2 * U + 2 * u + 2)
                        for t in range(2):
                            o = ps[:, 4 + u % 2, t * M:(t + 1) * M]
                            tt = 2 * (u % 2) + t
                            for r in range(2):
                                a, b = (q[:, 6 + r, n, tt * P:(tt + 1) * P] for q in (ahi, alo))
                                pe.matmul(o, a, kh[:, r, 0, :], start=(r == 0), stop=False)
                                pe.matmul(o, a, kh[:, r, 1, :], start=False, stop=False)
                                last = pe.matmul(o, b, kh[:, r, 0, :], start=False, stop=(r == 1))
                        last.then_inc(sc_mm, 1)

                    def turn_probs(u):
                        pe.wait_ge(p_nrm, 2 * U + 2 * u + 2)
                        pe.wait_ge(pt_lo, U + u + 1)
                        for m in range(2):
                            for t in range(2):
                                last = pe.transpose(ps[:, 6 + u % 2, (2 * m + t) * P:(2 * m + t + 1) * P],
                                                    pr[:, u % 2, t, m * P:(m + 1) * P], ident[:, :])
                        last.then_inc(pt_mm, 1)

                    def outputs(n):
                        pe.wait_ge(pt_lo, U + 2 * n + 4)
                        for d in range(2):
                            bank_ready(G + G_XQ + 8 * hh + 4 + 2 * n + d)
                            o = ps[:, 2 * n + d, :]
                            for m in range(2):
                                pe.matmul(o, vh[:, d, 0, m, :], pth[:, m, :], start=(m == 0), stop=False)
                                pe.matmul(o, vh[:, d, 0, m, :], ptl[:, m, :], start=False, stop=False)
                                last = pe.matmul(o, vh[:, d, 1, m, :], pth[:, m, :], start=False, stop=(m == 1))
                            last.then_inc(mm_done, 1)

                    pe.wait_ge(n_sq, 6 * h + 2)
                    scores(0)
                    scores(1)
                    turn_probs(0)
                    scores(2)
                    turn_probs(1)
                    scores(3)
                    outputs(0)
                    turn_probs(2)
                    turn_probs(3)
                    outputs(1)
                with pe.Fori(0, KT // 2) as i:
                    product(i, G + G_XO, J + J_XO, ahi, alo, lambda k: released(pe, G + G_XQ + 8 * (k // 2) + 6 + k % 2))
                stats(h, Q_PER_HALF * h + 32, lambda: pe.wait_ge(p_exp, 32 * h + 32 + 4))
                with pe.Fori(0, FG) as g:
                    with pe.Fori(0, KT // 2) as i:
                        product(i, G + G_FF + 32 * g, J + J_FF + 16 * g, bhi, blo,
                                lambda k: pe.wait_ge(lo_done, H + H_XO + 2 * k + 2))
                    with pe.Fori(0, KT // 2) as i:
                        product(i, G + G_FF + 32 * g + 16, J + J_FF + 16 * g + KT, ahi, alo,
                                lambda k: pe.wait_ge(lo_done, H + H_FF + 16 * g + 2 * k + 2))
                stats(h, Q_PER_HALF * h + 48, lambda: pe.wait_ge(n_sq, 6 * h + 4))
                if h == 0:
                    mix(0, 1, lambda k: pe.wait_ge(ysp_lo, KT + Y_ORDER.index(k) + 1))
                pe.wait_ge(n_sq, 6 * h + 6)
                for n in range(NH):
                    pe.wait_ge(zf, 16 * h + (16 if h == 0 else 8 * n + 8))
                    for t in range(4):
                        f = 8 * h + 4 * n + t
                        if f >= 2:
                            pe.wait_ge(f_cp, 2 * f - 2)
                        for k in range(KT):
                            last = pe.transpose(ps[:, 4 + 2 * (t % 2) + k // 4, (k % 4) * P:(k % 4 + 1) * P],
                                                zfin[:, k, n, t * P:(t + 1) * P], ident[:, :])
                            if k % 4 == 3:
                                last.then_inc(f_tr, 1)

        @block.scalar
        def _(act):
            start_at_one(act, std, c_std, tab_st, acc_st, *kv_st, *st_st)
            at = 0
            for v in (mix_norm_w, mem_norm_w, xattn_norm_w, mlp_norm_w, final_norm_w.rearrange("(a n) -> a n", a=1),
                      conv_b, conv_ln_w, conv_ln_b, ret_gn_w, ret_gn_b):
                n = v.shape[1] // P
                act.dma_start(vrow[at:at + n, :], v.rearrange("a (k p) -> (a k) p", p=P)).then_inc(vec_in, 16)
                at += n
            act.dma_start(trow[0:TAPS * CT, :], conv_w.rearrange("a t b (c p) -> (a t b c) p", p=P)).then_inc(vec_in, 16)
            act.wait_ge(consts, 10)
            act.activation(junk[:, 0:1], eps[:, :], ACT.Copy).then_inc(p_exp, 4)
            act.wait_ge(dec_dve, 1)
            act.activation(lg[:, 1], lg[:, 0], ACT.Exp, scale=-1.0).then_inc(dec_act, 1)
            act.wait_ge(dec_dve, 2)
            act.activation(lg[:, 3], lg[:, 2], ACT.Ln).then_inc(dec_act, 1)
            act.wait_ge(dec_dve, 9)
            xr = x.rearrange("b (n s p) d -> n p (b s) d", s=4, p=P)
            for n in range(NS):
                for k in range(KT):
                    g = KT * n + k
                    act.wait_ge(mm_done, g + 1)
                    if k % 4 == 3 and n + 1 < NS:
                        s = k // 4
                        act.dma_start(xt[:, s, :, :], xr[n + 1, :, :, s * (D // 2):(s + 1) * (D // 2)]).then_inc(x_in[s], 16)
                    act.activation(xhi[:, k, n, :], ps[:, k % 4, :], ACT.Copy).then_inc(hi0, 1)
                    act.wait_ge(ssq_done, g + 1)
                    act.activation(sq0[:, k % 2, :], ps[:, k % 4, :], ACT.Square).then_inc(sq0_done, 1)
            for k in range(KT):
                g = G_MEM + k
                act.wait_ge(mm_done, g + 1)
                act.activation(mhi[:, k, :], ps[:, k % 4, 0:M], ACT.Copy).then_inc(hi0, 1)
                act.wait_ge(ssq_done, g + 1)
                act.activation(sq0[:, k % 2, 0:M], ps[:, k % 4, 0:M], ACT.Square).then_inc(sq0_done, 1)
            for n in range(NS):
                act.wait_ge(stat_mm, n + 1)
                act.activation(rs[:, n, :], ps[:, 4 + n, :], ACT.Sqrt, bias=eps[:, :], scale=P / D).then_inc(stat_sq, 1)
            act.wait_ge(stat_mm, NS + 1)
            act.activation(rsm[:, :], ps[:, 4, 0:M], ACT.Sqrt, bias=eps[:, :], scale=P / D).then_inc(stat_sq, 1)
            with act.Fori(0, HEADS) as c:
                G = G_PROJ + GP * c

                def last_of(b):
                    released(act, G + CUM[b + 1] - 1)

                def store_proj(b, tile):
                    for n in range(NS):
                        released(act, G + CUM[b] + n)
                        act.dma_start(proj_d[tile + c, :, n * NC:(n + 1) * NC], st[:, n, :]).then_inc(st_st[n], 16)

                def high(b, slot):
                    act.wait_ge(kv_st[slot], 1 + 16 * c)
                    if slot < 2:
                        act.wait_ge(vt_mm0, 2 * c + slot + 1)
                        act.activation(khl[:, slot, 0, :], ps[:, 6 + slot, 0:M], ACT.Copy).then_inc(kv_hi, 1)
                    else:
                        last_of(b)
                        act.activation(khl[:, slot, 0, :], kz[:, slot, :], ACT.Copy).then_inc(kv_hi, 1)

                def store_kv(slot, order):
                    act.wait_ge(kv_lo, 1 + 4 * c + order + 1)
                    dst = (v_d if slot < 2 else k_d)[2 * c + slot % 2]
                    act.dma_start(dst, khl[:, slot, :, :].bitcast(F32)).then_inc(kv_st[slot], 16)

                act.wait_ge(tab_st, 1 + 32 * c)
                act.dma_start(pos_i[:, :], positions[0:1, bass.ds(c * NC, NC)].to_broadcast([P, NC])).then_inc(tab_in, 16)
                act.wait_ge(tab, 9 * c + 9)
                act.activation(ang[:, :], ang[:, :], ACT.Sin).then_inc(tab_sin, 1)
                act.activation(turns[:, :], turns[:, :], ACT.Sin, bias=half_pi[:, :], scale=-1.0).then_inc(tab_sin, 1)
                act.wait_ge(tab_sin, 2 * c + 2)
                act.dma_start(tab_d[0, :, bass.ds(c * NC, NC)], ang[:, :]).then_inc(tab_st, 16)
                act.dma_start(tab_d[1, :, bass.ds(c * NC, NC)], turns[:, :]).then_inc(tab_st, 16)
                for n in range(NS):
                    released(act, G + CUM[2] + n)
                    act.activation(st[:, n, :], st[:, n, :], ACT.Sigmoid).then_inc(sig_done, 1)
                high(1, 0)
                store_kv(0, 0)
                store_proj(4, 0)
                high(3, 1)
                store_kv(1, 1)
                high(5, 2)
                store_kv(2, 2)
                store_proj(6, 4)
                high(7, 3)
                store_kv(3, 3)
                store_proj(8, 8)
                store_proj(9, 12)
                act.wait_ge(conv_step, 1 + TAPS * c + TAPS)
                act.dma_start(conv_d[c], acc[:, :]).then_inc(acc_st, 16)
            leave_phase(act)

            act.wait_ge(iot, 5)
            for h in range(HEADS):
                for d, xi in ((0, xi_f), (1, xi_b)):
                    s = lg[:, 5, d, h:h + 1]
                    act.activation(xi[:, h, :], io_s[:, d, :], ACT.Exp, scale=s).then_inc(dec_act, 1)
                    act.activation(zeta[:, d, h:h + 1], io_c[:, d:d + 1], ACT.Exp, scale=s).then_inc(dec_act, 1)
            act.activation(gch[:, :, :], lg[:, 5], ACT.Exp, scale=float(P)).then_inc(dec_act, 1)

            def key_evac(h):
                act.wait_ge(kvb_mm, 4 * h)
                for i in range(4):
                    act.wait_ge(kt_mm, 4 * h + i + 1)
                    act.activation(k_tok[:, 4 * i:4 * i + 4, :].rearrange("p c d -> p (c d)"), ps[:, 4 + i, :], ACT.Copy).then_inc(kt_ev, 1)

            def value_evac(h):
                act.wait_ge(y_mm, 4 * h)
                for i in range(4):
                    act.wait_ge(vt_mm, 4 * h + i + 1)
                    act.activation(v_tok[:, 4 * i:4 * i + 4, :].rearrange("p c d -> p (c d)"), ps[:, 4 + i, :], ACT.Copy).then_inc(vt_ev, 1)

            def weighted_values(h):
                act.wait_ge(vt_ev, 4 * h + 4)
                if not first(h):
                    wait_alone(act, kvb_mm, 4 * h)
                act.activation(v_f[:, :, :], v_tok[:, :, :], ACT.Copy, scale=zeta[:, 0, bass.ds(h, 1)]).then_inc(v2, 1)
                act.activation(v_b[:, :, :], v_tok[:, :, :], ACT.Copy, scale=zeta[:, 1, bass.ds(h, 1)]).then_inc(v2, 1)

            def affine(h):
                for i in range(4):
                    wait_alone(act, y_mul, 1 + 4 * h + i + 1)
                    act.activation(y_b[:, i, :], y_b[:, i, :], ACT.Identity, bias=vec[:, bass.ds(V_GNB + h, 1)],
                                   scale=vec[:, bass.ds(V_GNW + h, 1)]).then_inc(y_aff, 1)

            def gates(h):
                act.wait_ge(l_g, 16 * h + 16)
                if not first(h):
                    act.wait_ge(y_out, 4 * h)
                for i in range(4):
                    act.activation(sg[:, i, :], gb[:, i * NC:(i + 1) * NC], ACT.Sigmoid).then_inc(sgd, 1)
                if not first(h):
                    act.wait_ge(y_st, 16 * h)
                for i in range(4):
                    act.wait_ge(y_mm, 4 * h + i + 1)
                    act.activation(y_b[:, i, :], ps[:, 4 + i, :], ACT.Copy).then_inc(y_ev, 1)

            def spreads(h):
                if not first(h):
                    act.wait_ge(c_out, CT * h)
                for i in range(4):
                    act.wait_ge(cen, 4 * h + i + 1)
                    if i >= 2:
                        act.wait_ge(va_mm, 4 * h + i - 1)
                    act.activation(w1[:, i % 2, :], y_b[:, i, :], ACT.Square).then_inc(sqd, 1)
                for c in range(CT):
                    act.wait_ge(c_cen, CT * h + c + 1)
                    if c >= 2:
                        act.wait_ge(c_va, CT * h + c - 1)
                    act.activation(cv_w[:, c % 2, :], cv[:, c, :], ACT.Square).then_inc(c_sq, 1)
                    if c == 1:
                        act.wait_ge(va_mm, 4 * h + 4)
                        act.activation(rec[:, :], ps[:, 0, :], ACT.Sqrt, bias=eps[:, :]).then_inc(std, 1)
                act.wait_ge(c_va, CT * h + CT)
                act.activation(cv_r[:, :], ps[:, 2, :], ACT.Sqrt, bias=eps[:, :], scale=P / CW).then_inc(c_std, 1)

            def conv_gates(h):
                for c in range(CT):
                    w, b = vec[:, V_LNW + c:V_LNW + c + 1], vec[:, V_LNB + c:V_LNB + c + 1]
                    act.wait_ge(c_mul, CT * h + c + 1)
                    act.activation((w1 if c < 2 else cv_w)[:, c % 2, :], cv[:, c, :], ACT.Sigmoid, bias=b, scale=w).then_inc(c_gat, 1)
                for c in range(CT):
                    w, b = vec[:, V_LNW + c:V_LNW + c + 1], vec[:, V_LNB + c:V_LNB + c + 1]
                    act.wait_ge(c_gat, CT * h + c + 1)
                    act.activation(cv[:, c, :], cv[:, c, :], ACT.Identity, bias=b, scale=w).then_inc(c_sig, 1)

            for i in range(4):
                act.wait_ge(kt_mm, i + 1)
                act.activation(k_tok[:, 4 * i:4 * i + 4, :].rearrange("p c d -> p (c d)"), ps[:, 4 + i, :], ACT.Copy).then_inc(kt_ev, 1)
            for i in range(4):
                act.wait_ge(vt_mm, i + 1)
                act.activation(v_tok[:, 4 * i:4 * i + 4, :].rearrange("p c d -> p (c d)"), ps[:, 4 + i, :], ACT.Copy).then_inc(vt_ev, 1)
            act.wait_ge(dec_dve, 11 + HEADS)
            weighted_values(0)
            act.activation(dmask[:, :, :], dmask[:, :, :], ACT.Exp).then_inc(dec_act, 1)
            act.wait_ge(phase, 5 * 1)
            gates(0)
            key_evac(1)
            value_evac(1)
            spreads(0)
            weighted_values(1)
            affine(0)
            with act.Fori(1, HEADS - 1) as h:
                conv_gates(h - 1)
                gates(h)
                key_evac(h + 1)
                value_evac(h + 1)
                spreads(h)
                weighted_values(h + 1)
                affine(h)
            conv_gates(HEADS - 2)
            gates(HEADS - 1)
            spreads(HEADS - 1)
            affine(HEADS - 1)

            def split_high(h, tiles):
                for k in tiles:
                    if k != HEADS - 1:
                        act.wait_ge(y_in[k], 16 * h + 16)
                    elif h == 0:
                        act.wait_ge(y_out, 4 * (HEADS - 1) + NH)
                    else:
                        act.wait_ge(y_in[k], 16)
                    act.activation(ahi[:, k, :, :], y_stage[:, k, :, :], ACT.Copy).then_inc(ysp_hi, 1)

            def load_residual(k, h):
                act.dma_start(res[:, k, :, :], xT_d[k, :, bass.ds(2 * h, 2), :]).then_inc(r_in[k], 16)

            split_high(0, Y_ORDER[:KT - 1])
            for k in range(KT):
                load_residual(k, 0)
            conv_gates(HEADS - 1)
            split_high(0, Y_ORDER[KT - 1:])
            leave_phase(act)
            act.wait_ge(phase, 5 * 2)

            for h in range(2):
                G = G_HALF0 + G_PER_HALF * h
                H = H_PER_HALF * h
                Q = Q_PER_HALF * h
                def residual(i, u, hb, qb):
                    for s in range(2):
                        for n in range(NH):
                            e = 4 * i + 2 * s + n
                            released(act, u + 4 * i + 2 * s + n)
                            act.activation(bhi[:, 2 * i + s, n, :], res[:, 2 * i + s, n, :], ACT.Copy).then_inc(hi_done, 1)
                            wait_alone(act, ss_done, qb + e + 1)
                            act.activation(sq[:, n, :], res[:, 2 * i + s, n, :], ACT.Square).then_inc(sq_done, 1)

                def norm_sqrt(count):
                    for n in range(NH):
                        act.wait_ge(n_mm, 6 * h + count + n + 1)
                        act.activation(rstd[:, n, :], ps[:, 4 + n, :], ACT.Sqrt, bias=eps[:, :], scale=P / D).then_inc(n_sq, 1)

                with act.Fori(h, KT // 2) as i:
                    residual(i, G, H, Q)
                norm_sqrt(0)
                with act.Fori(0, XH) as hh:
                    U = 16 * h + 4 * hh
                    act.wait_ge(mm_done, G + G_XQ + 8 * hh)
                    act.dma_start(kh[:, :, :, :].bitcast(F32), k_d[bass.ds(2 * hh, 2)].rearrange("r p a m -> p r a m")).then_inc(kv_in, 16)
                    act.dma_start(vh[:, :, :, :, :].rearrange("p d a m k -> p d a (m k)").bitcast(F32),
                                  v_d[bass.ds(2 * hh, 2)].rearrange("r p a m -> p r a m")).then_inc(kv_in, 16)
                    for r in range(2):
                        for n in range(NH):
                            e = 4 * hh + 2 * r + n
                            released(act, G + G_XQ + 8 * hh + 2 * r + n)
                            act.activation(ahi[:, 6 + r, n, :], z[:, n, :], ACT.Copy).then_inc(hi_done, 1)

                    def o_high(n):
                        for d in range(2):
                            act.wait_ge(mm_done, G + G_XQ + 8 * hh + 4 + 2 * n + d + 1)
                            act.activation(ahi[:, 2 * hh + d, n, :], ps[:, 2 * n + d, :], ACT.Copy).then_inc(o_hi, 1)

                    def exponents(u):
                        act.wait_ge(nb_done, U + u + 1)
                        for t in range(2):
                            c = 2 * u + t
                            act.activation(pr[:, u % 2, t, :], ps[:, 4 + u % 2, t * M:(t + 1) * M], ACT.Exp, bias=nb[:, c:c + 1],
                                           scale=XSCALE, accum_out=sm[:, c:c + 1]).then_inc(p_exp, 1)

                    def probs_high(u):
                        act.wait_ge(pt_mm, U + u + 1)
                        act.activation(pth[:, :, (u % 2) * M:(u % 2 + 1) * M],
                                       ps[:, 6 + u % 2, :].rearrange("p (m k) -> p m k", m=2), ACT.Copy).then_inc(pt_hi, 1)

                    exponents(0)
                    exponents(1)
                    if h:
                        for slot in range(2):
                            act.wait_ge(f_st[slot], 64)
                    probs_high(0)
                    probs_high(1)
                    exponents(2)
                    exponents(3)
                    o_high(0)
                    probs_high(2)
                    probs_high(3)
                    o_high(1)
                with act.Fori(0, KT // 2) as i:
                    residual(i, G + G_XO, H + H_XO, Q + 16)
                norm_sqrt(2)
                def hidden_high(g):
                    with act.Fori(0, KT // 2) as i:
                        for s in range(2):
                            for n in range(NH):
                                e = 4 * i + 2 * s + n
                                act.wait_ge(z_up, 64 * h + 16 * g + e + 1)
                                act.activation(ahi[:, 2 * i + s, n, :], z[:, n, :], ACT.Copy).then_inc(hi_done, 1)

                with act.Fori(0, FG - 1) as g:
                    hidden_high(g)
                hidden_high(FG - 1)
                if h == 0:
                    act.wait_ge(mm_done, G + G_FF + 32 * (FG - 1) + 16)
                    for k in Y_ORDER:
                        act.dma_start(y_stage[:, k, :, :].rearrange("p a b -> p (a b)"), y_d[k, :, HALF:S]).then_inc(y_in[k], 16)
                with act.Fori(0, KT // 2) as i:
                    for s in range(2):
                        for n in range(NH):
                            e = 4 * i + 2 * s + n
                            released(act, G + G_FF + 32 * (FG - 1) + 16 + e)
                            wait_alone(act, ss_done, Q + 32 + e + 1)
                            act.activation(sq[:, n, :], res[:, 2 * i + s, n, :], ACT.Square).then_inc(sq_done, 1)
                if h == 0:
                    act.wait_ge(mm_done, G + G_PER_HALF)
                    split_high(1, Y_ORDER)
                norm_sqrt(4)
                if h == 0:
                    for k in range(KT):
                        act.wait_ge(zf, 2 * k + 2)
                        load_residual(k, 1)
                for n in range(NH):
                    for t in range(4):
                        f = 8 * h + 4 * n + t
                        if f >= 2:
                            act.wait_ge(f_st[f % 2], 16 * (f // 2))
                        for b in range(2):
                            act.wait_ge(f_tr, 2 * f + b + 1)
                            act.activation(rows[:, t % 2, b * NC:(b + 1) * NC], ps[:, 4 + 2 * (t % 2) + b, :], ACT.Copy).then_inc(f_cp, 1)
                        act.wait_ge(f_cp, 2 * f + 2)
                        at = h * HALF + n * NC + t * P
                        act.dma_start(out[0, at:at + P, :], rows[:, t % 2, :]).then_inc(f_st[t % 2], 16)
                if h == 0:
                    residual(0, G_HALF0 + G_PER_HALF, H_PER_HALF, Q_PER_HALF)
            for s in range(2):
                act.wait_ge(f_st[s], 128)

        @block.vector
        def _(dve):
            start_at_one(dve, kv_lo, y_mul, conv_step)
            dve.memset(rs[:, :, :], 0.0).then_inc(ssq_done, 1)
            dve.memset(rsm[:, :], 0.0).then_inc(ssq_done, 1)
            dve.memset(junk[:, 3:4], 0.0).then_inc(bank_free, G0)
            def step(ins, n):
                ins.then_inc(dec_dve, 1)
                dve.wait_ge(dec_dve, n)
            dve.wait_ge(dec_in, 32)
            step(dve.scalar_tensor_tensor(out=lg[:, 0], in0=dec[:, :, :], scalar=-1.0, in1=dec[:, :, :],
                                          op0=ALU.mult, op1=ALU.max), 1)
            dve.wait_ge(dec_act, 1)
            step(dve.tensor_scalar(lg[:, 2], lg[:, 1], 1.0, None, ALU.add), 2)
            step(dve.tensor_scalar(lg[:, 4], lg[:, 2], -1.0, None, ALU.add), 3)
            step(dve.tensor_tensor(lg[:, 4], lg[:, 1], lg[:, 4], ALU.subtract), 4)
            step(dve.reciprocal(lg[:, 5], lg[:, 2]), 5)
            step(dve.tensor_tensor(lg[:, 4], lg[:, 4], lg[:, 5], ALU.mult), 6)
            dve.wait_ge(dec_act, 2)
            step(dve.tensor_tensor(lg[:, 4], lg[:, 4], lg[:, 3], ALU.add), 7)
            step(dve.tensor_scalar(lg[:, 5], dec[:, :, :], 0.0, None, ALU.min), 8)
            step(dve.tensor_tensor(lg[:, 5], lg[:, 5], lg[:, 4], ALU.subtract), 9)
            dve.wait_ge(vec_mm, 1)
            dve.tensor_copy(vec[:, :], ps[:, 4, 0:60]).then_inc(vec_ok, 1)
            dve.wait_ge(vec_mm, 2)
            dve.tensor_copy(taps[:, :], ps[:, 5, 0:TAPS * CT]).then_inc(vec_ok, 1)
            with dve.Fori(0, NS) as n:
                for k in range(KT):
                    g = KT * n + k
                    dve.wait_ge(sq0_done, g + 1)
                    dve.tensor_tensor(xlo[:, k, n, :], ps[:, k % 4, :], xhi[:, k, n, :], ALU.subtract).then_inc(bank_free, 1)
                    dve.wait_ge(ssq_done, g + 2)
                    dve.tensor_tensor(rs[:, n, :], rs[:, n, :], sq0[:, k % 2, :], ALU.add).then_inc(ssq_done, 1)
            for k in range(KT):
                g = G_MEM + k
                dve.wait_ge(sq0_done, g + 1)
                dve.tensor_tensor(mlo[:, k, :], ps[:, k % 4, 0:M], mhi[:, k, :], ALU.subtract).then_inc(bank_free, 1)
                dve.wait_ge(ssq_done, g + 2)
                dve.tensor_tensor(rsm[:, :], rsm[:, :], sq0[:, k % 2, 0:M], ALU.add).then_inc(ssq_done, 1)
            for n in range(NS):
                dve.wait_ge(stat_sq, n + 1)
                dve.reciprocal(rs[:, n, :], rs[:, n, :]).then_inc(stat_rc, 1)
            dve.wait_ge(stat_sq, NS + 1)
            dve.reciprocal(rsm[:, :], rsm[:, :]).then_inc(stat_rc, 1)
            dve.wait_ge(stat_rc, NS + 1)

            dve.memset(upad[:, :], 0.0).then_inc(pad_ok, 1)
            dve.wait_ge(pad_ok, 1)
            with dve.Fori(0, HEADS) as c:
                G = G_PROJ + GP * c

                def evac(b, n, dst):
                    g = CUM[b] + n
                    dve.wait_ge(mm_done, G + g + 1)
                    dve.tensor_tensor(dst, ps[:, g % 4, :], rs[:, n, :], ALU.mult).then_inc(bank_free, 1)

                def evac_kv(b, slot):
                    g = CUM[b]
                    dve.wait_ge(mm_done, G + g + 1)
                    dve.tensor_tensor(kz[:, slot, :], ps[:, g % 4, 0:M], rsm[:, :], ALU.mult).then_inc(bank_free, 1)

                def low(slot, order):
                    dve.wait_ge(kv_hi, 4 * c + order + 1)
                    src = ps[:, 6 + slot, 0:M] if slot < 2 else kz[:, slot, :]
                    dve.tensor_tensor(khl[:, slot, 1, :], src, khl[:, slot, 0, :], ALU.subtract).then_inc(kv_lo, 1)

                def tap(t):
                    src = upad[:, t:t + S]
                    dve.wait_ge(conv_step, 1 + TAPS * c + t)
                    if t == 0:
                        dve.wait_ge(acc_st, 1 + 16 * c)
                        for slot in range(4):
                            dve.wait_ge(xf_st[slot], 1 + 16 * NS * KT // 4)
                        ins = dve.tensor_scalar(acc[:, :], src, taps[:, bass.ds(c, 1)], vec[:, bass.ds(V_CB + c, 1)],
                                                ALU.mult, ALU.add)
                    else:
                        ins = dve.scalar_tensor_tensor(out=acc[:, :], in0=src, scalar=taps[:, bass.ds(CT * t + c, 1)],
                                                       in1=acc[:, :], op0=ALU.mult, op1=ALU.add)
                    ins.then_inc(conv_step, 1)

                dve.wait_ge(conv_step, 1 + TAPS * c)
                for n in range(NS):
                    evac(0, n, upad[:, PAD + n * NC:PAD + (n + 1) * NC])
                evac_kv(1, 0)

                def turn(m, ins):
                    ins.then_inc(tab, 1)
                    dve.wait_ge(tab, 9 * c + m + 1)
                dve.wait_ge(tab_in, 16 * c + 32)
                turn(0, dve.tensor_copy(ang[:, :], pos_i[:, :]))
                turn(1, dve.tensor_scalar(ang[:, :], ang[:, :], freq[:, 0:1], None, ALU.mult))
                turn(2, dve.tensor_scalar(turns[:, :], ang[:, :], float(1 / (2 * np.pi)), MAGIC, ALU.mult, ALU.add))
                turn(3, dve.tensor_scalar(turns[:, :], turns[:, :], -MAGIC, None, ALU.add))
                for m, part in enumerate(TWO_PI_PARTS):
                    turn(4 + m, dve.scalar_tensor_tensor(out=ang[:, :], in0=turns[:, :], scalar=-part, in1=ang[:, :],
                                                         op0=ALU.mult, op1=ALU.add))
                turn(7, dve.tensor_scalar(ang[:, :], ang[:, :], 3.1415925, -3.1415925, ALU.min, ALU.max))
                turn(8, dve.scalar_tensor_tensor(out=turns[:, :], in0=ang[:, :], scalar=-1.0, in1=ang[:, :],
                                                 op0=ALU.mult, op1=ALU.max))
                for n in range(NS):
                    dve.wait_ge(st_st[n], 1 + 64 * c)
                    evac(2, n, st[:, n, :])
                for n in range(NS):
                    dve.wait_ge(sig_done, 4 * c + n + 1)
                    u = upad[:, PAD + n * NC:PAD + (n + 1) * NC]
                    dve.tensor_tensor(u, u, st[:, n, :], ALU.mult).then_inc(u_done, 1)
                dve.wait_ge(u_done, 4 * c + 4)
                low(0, 0)
                evac_kv(3, 1)
                taps_after = [2] * 15 + [1]
                t = 0
                for stage, b in enumerate((4, 6, 8, 9)):
                    for n in range(NS):
                        if stage:
                            dve.wait_ge(st_st[n], 1 + 64 * c + 16 * stage)
                        evac(b, n, st[:, n, :])
                        for _ in range(taps_after[4 * stage + n]):
                            tap(t)
                            t += 1
                        if stage == 0 and n == 3:
                            low(1, 1)
                            evac_kv(5, 2)
                        if stage == 1 and n == 0:
                            low(2, 2)
                        if stage == 1 and n == 3:
                            evac_kv(7, 3)
                        if stage == 2 and n == 0:
                            low(3, 3)
            leave_phase(dve)

            def decay_masks():
                dve.wait_ge(iot, 5)
                dve.tensor_scalar(io_t[:, 1, :], io_t[:, 0, :], 0.0, None, ALU.max).then_inc(dpos, 1)
                dve.wait_ge(dpos, 1)
                step(dve.tensor_scalar(io_t[:, 2, :], io_t[:, 0, :], 0.0, -1.0, ALU.min, ALU.mult), 10)
                for h in range(HEADS):
                    dve.tensor_scalar(dmask[:, h, :], io_t[:, 1, :], lg[:, 5, 0, h:h + 1], None, ALU.mult).then_inc(dlin, 1)
                    dve.wait_ge(dlin, h + 1)
                    step(dve.scalar_tensor_tensor(out=dmask[:, h, :], in0=io_t[:, 2, :], scalar=lg[:, 5, 1, h:h + 1],
                                                  in1=dmask[:, h, :], op0=ALU.mult, op1=ALU.add), 11 + h)
                dve.wait_ge(dec_act, 2 + 4 * HEADS + 1)
                step(dve.tensor_scalar(zeta[:, :, :], zeta[:, :, :], KSCALE, None, ALU.mult), 11 + HEADS)

            def rotate_k(h):
                dve.wait_ge(l_k, 16 * h + 16)
                dve.tensor_tensor(kb_[:, :], kb_[:, :], cos_t[:, :], ALU.mult).then_inc(r_k, 1)
                dve.wait_ge(r_k, h + 1)
                dve.wait_ge(p_ks, h + 1)
                dve.tensor_tensor(k_rot_b[:, :], kb_[:, :], ksb[:, :], ALU.add).then_inc(k_rot, 1)

            def rotate_q(h):
                dve.wait_ge(l_q, 16 * h + 16)
                dve.tensor_tensor(qb_[:, :], qb_[:, :], cos_t[:, :], ALU.mult).then_inc(r_q, 1)
                dve.wait_ge(r_q, h + 1)
                dve.wait_ge(p_qs, h + 1)
                dve.tensor_tensor(q_rot_b[:, :], qb_[:, :], qsb[:, :], ALU.add).then_inc(q_rot, 1)

            def scans(h):
                if not first(h):
                    dve.wait_ge(y_mm, 4 * h)
                for c in range(CH - 1):
                    if c % 4 == 0:
                        dve.wait_ge(kvf_mm, 4 * h + c // 4 + 1)
                    if c or not first(h):
                        dve.wait_ge(f_scan, 15 * h + c)
                    dve.scalar_tensor_tensor(out=st_f[:, c + 1, :], in0=st_f[:, c, :], scalar=gch[:, 0, bass.ds(h, 1)],
                                             in1=ps[:, c // 4, (c % 4) * P:(c % 4 + 1) * P],
                                             op0=ALU.mult, op1=ALU.add).then_inc(f_scan, 1)
                for m in range(CH - 1):
                    c = CH - 1 - m
                    if m % 4 == 0:
                        dve.wait_ge(kvb_mm, 4 * h + m // 4 + 1)
                    if m or not first(h):
                        dve.wait_ge(b_scan, 15 * h + m)
                    dve.scalar_tensor_tensor(out=st_b[:, c - 1, :], in0=st_b[:, c, :], scalar=gch[:, 1, bass.ds(h, 1)],
                                             in1=ps[:, 4 + c // 4, (c % 4) * P:(c % 4 + 1) * P],
                                             op0=ALU.mult, op1=ALU.add).then_inc(b_scan, 1)

            def masked_scores(h):
                for i in range(4):
                    dve.wait_ge(s_mm, 4 * h + i + 1)
                    dve.tensor_tensor(sT[:, 4 * i:4 * i + 4, :], ps[:, i, :].rearrange("p (c q) -> p c q", c=4),
                                      dmask[:, h, :].unsqueeze(1).to_broadcast([P, 4, P]), ALU.mult).then_inc(s_ev, 1)

            def norm(h):
                for i in range(4):
                    dve.wait_ge(me_mm, 4 * h + i + 1)
                    dve.tensor_tensor(y_b[:, i, :], y_b[:, i, :], ps[:, i, :], ALU.subtract).then_inc(cen, 1)
                dve.wait_ge(c_me, h + 1)
                for c in range(CT):
                    dve.scalar_tensor_tensor(out=cv[:, c, :], in0=ps[:, 1, :], scalar=-float(P) / CW, in1=cv[:, c, :],
                                             op0=ALU.mult, op1=ALU.add).then_inc(c_cen, 1)
                dve.wait_ge(std, 1 + h + 1)
                dve.reciprocal(rec[:, :], rec[:, :]).then_inc(rc, 1)
                for i in range(4):
                    dve.wait_ge(bc_mm, 4 * h + i + 1)
                    dve.tensor_tensor(y_b[:, i, :], y_b[:, i, :], ps[:, 4 + i, :], ALU.mult).then_inc(y_mul, 1)

            def conv_norm(h):
                dve.wait_ge(c_std, 1 + h + 1)
                dve.reciprocal(cv_r[:, :], cv_r[:, :]).then_inc(c_rc, 1)
                dve.wait_ge(c_rc, h + 1)
                for c in range(CT):
                    dve.tensor_tensor(cv[:, c, :], cv[:, c, :], cv_r[:, :], ALU.mult).then_inc(c_mul, 1)

            def split_low(h, tiles):
                for k in tiles:
                    dve.wait_ge(ysp_hi, KT * h + Y_ORDER.index(k) + 1)
                    dve.tensor_tensor(alo[:, k, :, :], y_stage[:, k, :, :], ahi[:, k, :, :], ALU.subtract).then_inc(ysp_lo, 1)

            dve.wait_ge(l_tab, 32)
            rotate_k(0)
            decay_masks()
            dve.memset(st_f[:, 0, :], 0.0).then_inc(zero_st, 1)
            dve.memset(st_b[:, CH - 1, :], 0.0).then_inc(zero_st, 1)
            rotate_q(0)
            dve.wait_ge(dec_act, 2 + 4 * HEADS + 2)
            step(dve.tensor_scalar(dmask[:, :, :], dmask[:, :, :], KSCALE, None, ALU.mult), 12 + HEADS)
            dve.wait_ge(zero_st, 2)

            def next_rotation(h):
                dve.wait_ge(s_mm, 4 * h + 4)
                dve.wait_ge(p_qf, 2 * h + 2)
                rotate_k(h + 1)
                rotate_q(h + 1)

            scans(0)
            masked_scores(0)
            next_rotation(0)
            norm(0)
            with dve.Fori(1, HEADS - 1) as h:
                scans(h)
                conv_norm(h - 1)
                masked_scores(h)
                next_rotation(h)
                norm(h)
            scans(HEADS - 1)
            conv_norm(HEADS - 2)
            masked_scores(HEADS - 1)
            norm(HEADS - 1)
            split_low(0, Y_ORDER[:KT - 1])
            conv_norm(HEADS - 1)
            split_low(0, Y_ORDER[KT - 1:])
            leave_phase(dve)
            dve.wait_ge(phase, 5 * 2)

            dve.memset(junk[:, 4:5], 0.0).then_inc(ss_done, 2)
            dve.memset(junk[:, 5:6], 0.0).then_inc(pt_lo, 2)
            for h in range(2):
                G = G_HALF0 + G_PER_HALF * h
                H = H_PER_HALF * h
                Q = Q_PER_HALF * h
                def residual(i, g, hb, qb):
                    for s in range(2):
                        for n in range(NH):
                            e = 4 * i + 2 * s + n
                            m = 2 * i + s
                            dve.wait_ge(mm_done, g + e + 1)
                            dve.tensor_tensor(res[:, m, n, :], ps[:, 2 * s + n, :], res[:, m, n, :], ALU.add).then_inc(bank_free, 1)
                            dve.wait_ge(hi_done, hb + e + 1)
                            dve.tensor_tensor(blo[:, m, n, :], res[:, m, n, :], bhi[:, m, n, :], ALU.subtract).then_inc(lo_done, 1)
                            dve.wait_ge(sq_done, qb + e + 1)
                            dve.wait_ge(ss_done, qb + e + 1)
                            dve.tensor_tensor(ssq[:, n, :], ssq[:, n, :], sq[:, n, :], ALU.add).then_inc(ss_done, 1)

                def norm_recip(count):
                    for n in range(NH):
                        dve.wait_ge(n_sq, 6 * h + count + n + 1)
                        dve.reciprocal(rstd[:, n, :], rstd[:, n, :]).then_inc(n_rc, 1)
                    dve.wait_ge(n_rc, 6 * h + count + 2)

                def zero_sums(count, h=h):
                    dve.memset(ssq[:, :, :], 0.0).then_inc(ss_zero, 1)
                    wait_alone(dve, ss_zero, 3 * h + count + 1)

                def first_sums(h):
                    zero_sums(0, h)
                    for k in range(KT):
                        wait_alone(dve, r_in[k], 16 * h + 16)

                if h == 0:
                    first_sums(0)
                with dve.Fori(h, KT // 2) as i:
                    residual(i, G, H, Q)
                norm_recip(0)
                zero_sums(1)
                with dve.Fori(0, XH) as hh:
                    U = 16 * h + 4 * hh
                    for r in range(2):
                        for n in range(NH):
                            e = 2 * r + n
                            dve.wait_ge(mm_done, G + G_XQ + 8 * hh + e + 1)
                            dve.tensor_tensor(z[:, n, :], ps[:, e, :], rstd[:, n, :], ALU.mult).then_inc(bank_free, 1)
                            dve.wait_ge(hi_done, H + H_XQ + 4 * hh + e + 1)
                            dve.tensor_tensor(alo[:, 6 + r, n, :], z[:, n, :], ahi[:, 6 + r, n, :], ALU.subtract).then_inc(lo_done, 1)

                    def row_max(u):
                        c = slice(2 * u, 2 * u + 2)
                        dve.wait_ge(sc_mm, U + u + 1)
                        dve.tensor_reduce(mx[:, c], ps[:, 4 + u % 2, :].rearrange("p (t m) -> p t m", t=2), AX.X, ALU.max).then_inc(mx_done, 1)
                        dve.wait_ge(mx_done, U + u + 1)
                        dve.tensor_scalar(nb[:, c], mx[:, c], -XSCALE, None, ALU.mult).then_inc(nb_done, 1)

                    def normalise(u):
                        dve.wait_ge(p_exp, 2 * U + 2 * u + 6)
                        dve.reciprocal(ri[:, 2 * u:2 * u + 2], sm[:, 2 * u:2 * u + 2]).then_inc(ri_done, 1)
                        dve.wait_ge(ri_done, U + u + 1)
                        for t in range(2):
                            dve.tensor_scalar(pr[:, u % 2, t, :], pr[:, u % 2, t, :], ri[:, 2 * u + t:2 * u + t + 1], None,
                                              ALU.mult).then_inc(p_nrm, 1)

                    def probs_low(u):
                        cols = slice((u % 2) * M, (u % 2 + 1) * M)
                        dve.wait_ge(pt_hi, U + u + 1)
                        dve.tensor_tensor(ptl[:, :, cols], ps[:, 6 + u % 2, :].rearrange("p (m k) -> p m k", m=2),
                                          pth[:, :, cols], ALU.subtract).then_inc(pt_lo, 1)

                    def o_low(n):
                        for d in range(2):
                            dve.wait_ge(o_hi, 16 * h + 4 * hh + 2 * n + d + 1)
                            dve.tensor_tensor(alo[:, 2 * hh + d, n, :], ps[:, 2 * n + d, :], ahi[:, 2 * hh + d, n, :],
                                              ALU.subtract).then_inc(bank_free, 1)

                    row_max(0)
                    row_max(1)
                    normalise(0)
                    normalise(1)
                    probs_low(0)
                    row_max(2)
                    probs_low(1)
                    row_max(3)
                    normalise(2)
                    normalise(3)
                    o_low(0)
                    probs_low(2)
                    probs_low(3)
                    o_low(1)
                with dve.Fori(0, KT // 2) as i:
                    residual(i, G + G_XO, H + H_XO, Q + 16)
                norm_recip(2)
                zero_sums(2)
                def hidden(g):
                    with dve.Fori(0, KT // 2) as i:
                        for s in range(2):
                            for n in range(NH):
                                e = 4 * i + 2 * s + n
                                gg = G + G_FF + 32 * g + e
                                dve.wait_ge(mm_done, gg + 1)
                                dve.tensor_tensor(z[:, n, :], ps[:, 2 * s + n, :], rstd[:, n, :], ALU.mult).then_inc(bank_free, 1)
                                released(dve, gg)
                                dve.scalar_tensor_tensor(out=z[:, n, :], in0=z[:, n, :], scalar=0.0, in1=z[:, n, :],
                                                         op0=ALU.max, op1=ALU.mult).then_inc(z_up, 1)
                                dve.wait_ge(hi_done, H + H_FF + 16 * g + e + 1)
                                dve.tensor_tensor(alo[:, 2 * i + s, n, :], z[:, n, :], ahi[:, 2 * i + s, n, :],
                                                  ALU.subtract).then_inc(lo_done, 1)

                def add_hidden(g, squares):
                    with dve.Fori(0, KT // 2) as i:
                        for s in range(2):
                            for n in range(NH):
                                e = 4 * i + 2 * s + n
                                m = 2 * i + s
                                gg = G + G_FF + 32 * g + 16 + e
                                dve.wait_ge(mm_done, gg + 1)
                                dve.tensor_tensor(res[:, m, n, :], ps[:, 2 * s + n, :], res[:, m, n, :], ALU.add).then_inc(bank_free, 1)
                                if squares:
                                    dve.wait_ge(sq_done, Q + 32 + e + 1)
                                    dve.wait_ge(ss_done, Q + 32 + e + 1)
                                    dve.tensor_tensor(ssq[:, n, :], ssq[:, n, :], sq[:, n, :], ALU.add).then_inc(ss_done, 1)

                with dve.Fori(0, FG - 1) as g:
                    hidden(g)
                    add_hidden(g, False)
                hidden(FG - 1)
                add_hidden(FG - 1, True)
                if h == 0:
                    split_low(1, Y_ORDER)
                def final_norm(k, n):
                    dve.scalar_tensor_tensor(out=zfin[:, k, n, :], in0=res[:, k, n, :], scalar=vec[:, V_FIN + k:V_FIN + k + 1],
                                             in1=rstd[:, n, :], op0=ALU.mult, op1=ALU.mult).then_inc(zf, 1)

                if h == 0:
                    norm_recip(4)
                    for k in range(KT):
                        for n in range(NH):
                            final_norm(k, n)
                else:
                    for n in range(NH):
                        dve.wait_ge(n_sq, 6 * h + 4 + n + 1)
                        dve.reciprocal(rstd[:, n, :], rstd[:, n, :]).then_inc(n_rc, 1)
                        dve.wait_ge(n_rc, 6 * h + 4 + n + 1)
                        for k in range(KT):
                            final_norm(k, n)
                if h == 0:
                    first_sums(1)
                    dve.wait_ge(f_tr, 16)
                    residual(0, G_HALF0 + G_PER_HALF, H_PER_HALF, Q_PER_HALF)


_INS = ['x', 'mem', 'positions', 'mix_norm_w', 'w_in', 'ret_decay_f', 'ret_decay_b', 'ret_gn_w', 'ret_gn_b',
        'conv_w', 'conv_b', 'conv_ln_w', 'conv_ln_b', 'w_out', 'xattn_norm_w', 'mem_norm_w',
        'w_xq', 'w_xkv', 'w_xo', 'mlp_norm_w', 'w_ff1', 'w_ff2', 'final_norm_w']


def kernel(**inputs):
    import concourse.bacc as _bacc
    from concourse.bass_utils import run_bass_kernel_spmd as _run

    nc = _bacc.Bacc("TRN2", target_bir_lowering=False, num_devices=1, dynamic_dma_scratch_size=1024)
    arrays, args = {}, []
    for name in _INS:
        a = np.ascontiguousarray(inputs[name])
        arrays[f"in_{name}"] = a
        args.append(nc.dram_tensor(f"in_{name}", a.shape, mybir.dt.from_np(a.dtype), kind="ExternalInput").ap())
    half = 64
    f = (np.float32(ROPE_THETA) ** (-np.arange(half, dtype=np.float32) / np.float32(half))).astype(np.float32)
    arrays["rope_freq"] = np.concatenate([-f, f]).reshape(2 * half, 1)
    args.append(nc.dram_tensor("rope_freq", (2 * half, 1), F32, kind="ExternalInput").ap())
    out = nc.dram_tensor("out", (1, 2048, 1024), F32, kind="ExternalOutput").ap()
    build(nc, *args, out)
    r = _run(nc, [arrays], core_ids=[0])
    return r.results[0]["out"]
```
